# Optimizing a Trainium2 kernel written in Bass

```python
import jax, jax.numpy as jnp
from jax import lax
import numpy as np

D_MODEL = 1024
BATCH = 1
SEQ = 256
DEPTH = 2

GRID_W = 64
CTX_LEN = 256
N_MIXERS = 2
N_MOD = 9
D_FF = 2816
GMLP_D_FF = 6 * D_MODEL
GMLP_HALF = GMLP_D_FF // 2
CHUNK = 128
GMLP_GROUPS = 8
HEAD_DIM = 128
N_HEADS = D_MODEL // HEAD_DIM
N_KV_HEADS = 2
Q_DIM = N_HEADS * HEAD_DIM
KV_DIM = N_KV_HEADS * HEAD_DIM
ROPE_THETA = 10000.0
Q_BLOCK = 128
LN_EPS = 1e-5
RMS_EPS = 1e-6
ALPHA = (2.0 * DEPTH) ** 0.25
BETA = (8.0 * DEPTH) ** -0.25
N_A = (DEPTH + 1) // 2
N_B = DEPTH // 2


def layer_norm(x, g, b):
    xf = x.astype(jnp.float32)
    mu = jnp.mean(xf, axis=-1, keepdims=True)
    var = jnp.mean(jnp.square(xf - mu), axis=-1, keepdims=True)
    return ((xf - mu) * lax.rsqrt(var + LN_EPS) * g + b).astype(x.dtype)

def rms_norm(x, g):
    xf = x.astype(jnp.float32)
    return (xf * lax.rsqrt(jnp.mean(jnp.square(xf), axis=-1, keepdims=True) + RMS_EPS) * g).astype(x.dtype)

def modulation(cond, w_mod, b_mod):
    m = jax.nn.silu(cond) @ w_mod + b_mod
    return jnp.split(m[..., None, :], N_MOD, axis=-1)

def modulate(x, shift, scale):
    return x * (1.0 + scale) + shift

def swiglu(h, w_in, w_out):
    g, u = jnp.split(h @ w_in, 2, axis=-1)
    return (jax.nn.silu(g) * u) @ w_out

def ffn_sublayer(x, shift, scale, gate, w_in, w_out, ln_g, ln_b):
    y = swiglu(modulate(x, shift, scale), w_in, w_out)
    return layer_norm(ALPHA * x + 0.5 * gate * y, ln_g, ln_b)

def gmlp_mix(h, w_in, sgu_g, sgu_b, w_s, b_s, w_out):
    b_, t_, _ = h.shape
    u, v = jnp.split(jax.nn.gelu(h @ w_in, approximate=False), 2, axis=-1)
    v = layer_norm(v, sgu_g, sgu_b)
    v = v.reshape(b_, t_ // CHUNK, CHUNK, GMLP_GROUPS, GMLP_HALF // GMLP_GROUPS)
    v = jnp.einsum('gpq,bnqgc->bnpgc', w_s, v) + b_s.T[None, None, :, :, None]
    return (u * v.reshape(b_, t_, GMLP_HALF)) @ w_out

def rope_tables(rows, cols):
    quarter = HEAD_DIM // 4
    freqs = ROPE_THETA ** (-jnp.arange(quarter, dtype=jnp.float32) / quarter)
    ang = jnp.concatenate([rows.astype(jnp.float32)[:, None] * freqs,
                           cols.astype(jnp.float32)[:, None] * freqs], axis=-1)
    return jnp.cos(ang), jnp.sin(ang)

def apply_rope(x, cos, sin):
    x1, x2 = jnp.split(x, 2, axis=-1)
    out = jnp.concatenate([x1 * cos - x2 * sin, x2 * cos + x1 * sin], axis=-1)
    return out.astype(x.dtype)

def split_heads(x, n):
    b_, t_, _ = x.shape
    return x.reshape(b_, t_, n, HEAD_DIM).transpose(0, 2, 1, 3)

def merge_heads(x):
    b_, h_, t_, d_ = x.shape
    return x.transpose(0, 2, 1, 3).reshape(b_, t_, h_ * d_)

def attend(q, k, v):
    b_, h_, tq, hd = q.shape
    qg = q.reshape(b_, N_KV_HEADS, h_ // N_KV_HEADS, tq, hd)
    s = jnp.einsum('bkgqd,bktd->bkgqt', qg, k, preferred_element_type=jnp.float32) * (hd ** -0.5)
    p = jax.nn.softmax(s, axis=-1)
    o = jnp.einsum('bkgqt,bktd->bkgqd', p.astype(v.dtype), v)
    return o.reshape(b_, h_, tq, hd)

def block_attend(q, k, v):
    b_, h_, t_, hd = q.shape
    nb = t_ // Q_BLOCK
    qb = q.reshape(b_, h_, nb, Q_BLOCK, hd).transpose(2, 0, 1, 3, 4)
    ob = lax.map(lambda qblk: attend(qblk, k, v), qb)
    return ob.transpose(1, 2, 0, 3, 4).reshape(b_, h_, t_, hd)

def gqa_mix(h_lat, h_ctx, w_qkv, q_norm_g, k_norm_g, w_o, cos, sin, with_ctx_out):
    kv_c = h_ctx @ w_qkv[:, Q_DIM:]
    k_c = rms_norm(split_heads(kv_c[..., :KV_DIM], N_KV_HEADS), k_norm_g)
    v_c = split_heads(kv_c[..., KV_DIM:], N_KV_HEADS)
    qkv = h_lat @ w_qkv
    q_l = apply_rope(rms_norm(split_heads(qkv[..., :Q_DIM], N_HEADS), q_norm_g), cos, sin)
    k_l = apply_rope(rms_norm(split_heads(qkv[..., Q_DIM:Q_DIM + KV_DIM], N_KV_HEADS), k_norm_g), cos, sin)
    v_l = split_heads(qkv[..., Q_DIM + KV_DIM:], N_KV_HEADS)
    k_all = jnp.concatenate([k_c, k_l], axis=2)
    v_all = jnp.concatenate([v_c, v_l], axis=2)
    y_lat = merge_heads(block_attend(q_l, k_all, v_all)) @ w_o
    if not with_ctx_out:
        return y_lat, None
    q_c = rms_norm(split_heads(h_ctx @ w_qkv[:, :Q_DIM], N_HEADS), q_norm_g)
    y_ctx = merge_heads(attend(q_c, k_c, v_c)) @ w_o
    return y_lat, y_ctx

def first_inputs(seed: int = 0) -> dict:
    key = jax.random.key(seed)
    ks = jax.random.split(key, 20)
    f32 = jnp.float32
    nrm = lambda k, shape, s: jax.random.normal(k, shape, f32) * s
    return {
        "x": nrm(ks[0], (BATCH, SEQ, D_MODEL), 1.0),
        "c": nrm(ks[1], (BATCH, D_MODEL), 1.0),
        "ctx": nrm(ks[2], (BATCH, CTX_LEN, D_MODEL), 1.0),
        "c_ctx": nrm(ks[3], (D_MODEL,), 1.0),
        "w_mod": nrm(ks[4], (DEPTH, D_MODEL, N_MOD * D_MODEL), D_MODEL ** -0.5),
        "b_mod": nrm(ks[5], (DEPTH, N_MOD * D_MODEL), 0.02),
        "ln_g": 1.0 + nrm(ks[6], (DEPTH, 3, D_MODEL), 0.02),
        "ln_b": nrm(ks[7], (DEPTH, 3, D_MODEL), 0.02),
        "ffn_w_in": nrm(ks[8], (DEPTH, 2, D_MODEL, 2 * D_FF), D_MODEL ** -0.5),
        "ffn_w_out": nrm(ks[9], (DEPTH, 2, D_FF, D_MODEL), BETA * D_FF ** -0.5),
        "gmlp_w_in": nrm(ks[10], (N_A, D_MODEL, GMLP_D_FF), D_MODEL ** -0.5),
        "gmlp_ln_g": 1.0 + nrm(ks[11], (N_A, GMLP_HALF), 0.02),
        "gmlp_ln_b": nrm(ks[12], (N_A, GMLP_HALF), 0.02),
        "gmlp_w_s": nrm(ks[13], (N_A, GMLP_GROUPS, CHUNK, CHUNK), CHUNK ** -0.5),
        "gmlp_b_s": 1.0 + nrm(ks[14], (N_A, GMLP_GROUPS, CHUNK), 0.02),
        "gmlp_w_out": nrm(ks[15], (N_A, GMLP_HALF, D_MODEL), BETA * GMLP_HALF ** -0.5),
        "attn_w_qkv": nrm(ks[16], (N_B, D_MODEL, Q_DIM + 2 * KV_DIM), D_MODEL ** -0.5),
        "attn_q_norm": 1.0 + nrm(ks[17], (N_B, HEAD_DIM), 0.02),
        "attn_k_norm": 1.0 + nrm(ks[18], (N_B, HEAD_DIM), 0.02),
        "attn_w_o": nrm(ks[19], (N_B, Q_DIM, D_MODEL), BETA * Q_DIM ** -0.5),
    }

def first_block(x, c, ctx, c_ctx, w_mod, b_mod, ln_g, ln_b, ffn_w_in, ffn_w_out,
              gmlp_w_in, gmlp_ln_g, gmlp_ln_b, gmlp_w_s, gmlp_b_s, gmlp_w_out,
              attn_w_qkv, attn_q_norm, attn_k_norm, attn_w_o):
    n_tok = x.shape[1]
    ROWS = n_tok // GRID_W
    rows = jnp.repeat(jnp.arange(ROWS, dtype=jnp.int32), GRID_W)
    cols = jnp.tile(jnp.arange(GRID_W, dtype=jnp.int32), ROWS)
    cos, sin = rope_tables(rows, cols)

    x_lat, x_ctx = x, ctx
    for i in range(DEPTH):
        is_attn = (i % N_MIXERS) == 1
        j = i // N_MIXERS
        last = i == DEPTH - 1
        ctx_feeds_mixer = (not last) or is_attn
        m_lat = modulation(c, w_mod[i], b_mod[i])
        m_ctx = modulation(c_ctx, w_mod[i], b_mod[i])

        x_lat = ffn_sublayer(x_lat, m_lat[0], m_lat[1], m_lat[2],
                             ffn_w_in[i, 0], ffn_w_out[i, 0], ln_g[i, 0], ln_b[i, 0])
        if ctx_feeds_mixer:
            x_ctx = ffn_sublayer(x_ctx, m_ctx[0], m_ctx[1], m_ctx[2],
                                 ffn_w_in[i, 0], ffn_w_out[i, 0], ln_g[i, 0], ln_b[i, 0])

        h_lat = modulate(x_lat, m_lat[3], m_lat[4])
        if is_attn:
            h_ctx = modulate(x_ctx, m_ctx[3], m_ctx[4])
            y_lat, y_ctx = gqa_mix(h_lat, h_ctx, attn_w_qkv[j], attn_q_norm[j], attn_k_norm[j],
                                   attn_w_o[j], cos, sin, not last)
        else:
            y_lat = gmlp_mix(h_lat, gmlp_w_in[j], gmlp_ln_g[j], gmlp_ln_b[j],
                             gmlp_w_s[j], gmlp_b_s[j], gmlp_w_out[j])
            y_ctx = None
            if not last:
                h_ctx = modulate(x_ctx, m_ctx[3], m_ctx[4])
                y_ctx = gmlp_mix(h_ctx, gmlp_w_in[j], gmlp_ln_g[j], gmlp_ln_b[j],
                                 gmlp_w_s[j], gmlp_b_s[j], gmlp_w_out[j])
        x_lat = layer_norm(ALPHA * x_lat + m_lat[5] * y_lat, ln_g[i, 1], ln_b[i, 1])
        if not last:
            x_ctx = layer_norm(ALPHA * x_ctx + m_ctx[5] * y_ctx, ln_g[i, 1], ln_b[i, 1])

        x_lat = ffn_sublayer(x_lat, m_lat[6], m_lat[7], m_lat[8],
                             ffn_w_in[i, 1], ffn_w_out[i, 1], ln_g[i, 2], ln_b[i, 2])
        if not last:
            x_ctx = ffn_sublayer(x_ctx, m_ctx[6], m_ctx[7], m_ctx[8],
                                 ffn_w_in[i, 1], ffn_w_out[i, 1], ln_g[i, 2], ln_b[i, 2])
    return x_lat


HEAD_DIM_2 = 64
RET_HEADS = 8
DIL_HEADS = 8
SB_HEADS = D_MODEL // HEAD_DIM_2
RET_WIDTH = RET_HEADS * HEAD_DIM_2
DIL_WIDTH = DIL_HEADS * HEAD_DIM_2
SB_WIDTH = SB_HEADS * HEAD_DIM_2
HYB_IN = 4 * RET_WIDTH + 3 * DIL_WIDTH
BLOCK = 128
RET_CHUNK = 128
RET_ROPE_THETA = 10000.0
ROPE_THETA_2 = 500000.0
ROPE_DIM = HEAD_DIM_2 // 4
DILATED_PATTERNS = ((128, 1), (512, 4), (2048, 16))
NORM_EPS = 1e-6
GN_EPS = 1e-5
N_EVEN = (DEPTH + 1) // 2
N_ODD = DEPTH // 2


def rms_norm_2(x, g):
    xf = x.astype(jnp.float32)
    y = xf * lax.rsqrt(jnp.mean(xf * xf, axis=-1, keepdims=True) + NORM_EPS)
    return (y * g.astype(jnp.float32)).astype(x.dtype)

def swiglu_ffn(x, g, w_in, w_out):
    h = rms_norm_2(x, g)
    gate, up = jnp.split(h @ w_in, 2, axis=-1)
    return (jax.nn.silu(gate) * up) @ w_out

def split_heads_2(t, n_heads):
    b, s, _ = t.shape
    return t.reshape(b, s, n_heads, HEAD_DIM_2).transpose(0, 2, 1, 3)

def merge_heads_2(t):
    b, h, s, dh = t.shape
    return t.transpose(0, 2, 1, 3).reshape(b, s, h * dh)

def rotary(x, rot_dim, theta):
    s = x.shape[-2]
    half = rot_dim // 2
    inv_freq = 1.0 / (theta ** (jnp.arange(half, dtype=jnp.float32) / half))
    ang = jnp.arange(s, dtype=jnp.float32)[:, None] * inv_freq[None, :]
    cos, sin = jnp.cos(ang), jnp.sin(ang)
    xr = x[..., :rot_dim].astype(jnp.float32)
    x1, x2 = xr[..., :half], xr[..., half:]
    rot = jnp.concatenate([x1 * cos - x2 * sin, x2 * cos + x1 * sin], axis=-1).astype(x.dtype)
    return jnp.concatenate([rot, x[..., rot_dim:]], axis=-1)

def retention_chunkwise(q, k, v):
    b, h, s, dk = q.shape
    c = RET_CHUNK
    nc = s // c
    out_dtype = v.dtype
    q, k, v = (t.astype(jnp.float32) for t in (q, k, v))
    k = k * (dk ** -0.5)
    log_g = jnp.log(1.0 - 2.0 ** (-5.0 - jnp.arange(h, dtype=jnp.float32)))
    i = jnp.arange(c, dtype=jnp.float32)
    diff = i[:, None] - i[None, :]
    decay_in = jnp.where(diff >= 0, jnp.exp(jnp.maximum(diff, 0.0)[None] * log_g[:, None, None]), 0.0)
    qc = q.reshape(b, h, nc, c, dk)
    kc = k.reshape(b, h, nc, c, dk)
    vc = v.reshape(b, h, nc, c, -1)
    scores = jnp.einsum('bhnid,bhnjd->bhnij', qc, kc) * decay_in[None, :, None]
    inner = jnp.einsum('bhnij,bhnje->bhnie', scores, vc)
    k_decay = jnp.exp((c - 1 - i)[None, :] * log_g[:, None])
    kv = jnp.einsum('bhnjd,bhnje->nbhde', kc * k_decay[None, :, None, :, None], vc)
    chunk_decay = jnp.exp(c * log_g)[None, :, None, None]

    def step(state, kv_n):
        return state * chunk_decay + kv_n, state

    _, state_prev = lax.scan(step, jnp.zeros_like(kv[0]), kv)
    q_decay = jnp.exp((i + 1)[None, :] * log_g[:, None])
    cross = jnp.einsum('bhnid,nbhde->bhnie', qc * q_decay[None, :, None, :, None], state_prev)
    return (inner + cross).reshape(b, h, s, -1).astype(out_dtype)

def head_group_norm(o, g):
    of = o.astype(jnp.float32)
    mu = jnp.mean(of, axis=-1, keepdims=True)
    var = jnp.mean(jnp.square(of - mu), axis=-1, keepdims=True)
    y = (of - mu) * lax.rsqrt(var + GN_EPS)
    y = y * g.astype(jnp.float32).reshape(o.shape[1], 1, o.shape[3])
    return y.astype(o.dtype)

def band_attention(q, k, v, n_back):
    *lead, l_len, dh = q.shape
    nb = l_len // BLOCK
    qb = q.reshape(*lead, nb, BLOCK, dh)

    def with_prev(t):
        tb = t.reshape(*lead, nb, BLOCK, dh)
        prev = jnp.concatenate([jnp.zeros_like(tb[..., :1, :, :]), tb[..., :-1, :, :]], axis=-3)
        return jnp.concatenate([prev, tb], axis=-2)

    kb, vb = with_prev(k), with_prev(v)
    s = jnp.einsum('...nqd,...nkd->...nqk', qb, kb).astype(jnp.float32) * (dh ** -0.5)
    dist = (jnp.arange(BLOCK)[:, None] + BLOCK) - jnp.arange(2 * BLOCK)[None, :]
    in_band = (dist >= 0) & (dist <= n_back)
    key_pos = jnp.arange(nb)[:, None] * BLOCK - BLOCK + jnp.arange(2 * BLOCK)[None, :]
    mask = in_band[None] & (key_pos >= 0)[:, None, :]
    s = jnp.where(mask, s, -jnp.inf)
    m = jnp.max(s, axis=-1, keepdims=True)
    p = jnp.exp(s - m)
    den = jnp.sum(p, axis=-1, keepdims=True)
    o = jnp.einsum('...nqk,...nkd->...nqd', p, vb.astype(jnp.float32)) / den
    lse = (m + jnp.log(den))[..., 0]
    return o.reshape(*lead, l_len, dh), lse.reshape(*lead, l_len)

def dilated_attention(q, k, v):
    b, h, s, dh = q.shape
    outs, lses = [], []
    for window, dil in DILATED_PATTERNS:
        mult = dil * BLOCK
        s_pad = -(-s // mult) * mult
        pad = ((0, 0), (0, 0), (0, s_pad - s), (0, 0))

        def by_residue(t):
            return jnp.pad(t, pad).reshape(b, h, s_pad // dil, dil, dh).transpose(0, 1, 3, 2, 4)

        o, lse = band_attention(by_residue(q), by_residue(k), by_residue(v), window // dil)
        outs.append(o.transpose(0, 1, 3, 2, 4).reshape(b, h, s_pad, dh)[:, :, :s])
        lses.append(lse.transpose(0, 1, 3, 2).reshape(b, h, s_pad)[:, :, :s])
    w = jax.nn.softmax(jnp.stack(lses, axis=0), axis=0)
    o = jnp.sum(w[..., None] * jnp.stack(outs, axis=0), axis=0)
    return o.astype(q.dtype)

def stick_breaking_attention(q, k, v):
    b, h, s, dh = q.shape
    nb = s // BLOCK
    kf, vf = k.astype(jnp.float32), v.astype(jnp.float32)
    key_pos = jnp.arange(s)

    def one_block(args):
        q_blk, blk = args
        z = jnp.einsum('bhqd,bhkd->bhqk', q_blk.astype(jnp.float32), kf) * (dh ** -0.5)
        q_pos = blk * BLOCK + jnp.arange(BLOCK)
        causal = key_pos[None, :] < q_pos[:, None]
        log_stay = jnp.where(causal, jax.nn.log_sigmoid(-z), 0.0)
        later = lax.cumsum(log_stay, axis=3, reverse=True) - log_stay
        a = jnp.where(causal, jnp.exp(jax.nn.log_sigmoid(z) + later), 0.0)
        return jnp.einsum('bhqk,bhkd->bhqd', a, vf)

    q_blocks = q.reshape(b, h, nb, BLOCK, dh).transpose(2, 0, 1, 3, 4)
    o = lax.map(one_block, (q_blocks, jnp.arange(nb)))
    return o.transpose(1, 2, 0, 3, 4).reshape(b, h, s, dh).astype(q.dtype)

def retention_dilated_mixer(x, norm_g, w_in, ret_gn, w_out):
    h = rms_norm_2(x, norm_g)
    proj = h @ w_in
    cuts = [RET_WIDTH, 2 * RET_WIDTH, 3 * RET_WIDTH, 4 * RET_WIDTH,
            4 * RET_WIDTH + DIL_WIDTH, 4 * RET_WIDTH + 2 * DIL_WIDTH]
    rq, rk, rv, rg, dq, dk, dv = jnp.split(proj, cuts, axis=-1)
    rq = rotary(split_heads_2(rq, RET_HEADS), HEAD_DIM_2, RET_ROPE_THETA)
    rk = rotary(split_heads_2(rk, RET_HEADS), HEAD_DIM_2, RET_ROPE_THETA)
    ret = retention_chunkwise(rq, rk, split_heads_2(rv, RET_HEADS))
    ret = merge_heads_2(head_group_norm(ret, ret_gn)) * jax.nn.silu(rg)
    dq = rotary(split_heads_2(dq, DIL_HEADS), ROPE_DIM, ROPE_THETA_2)
    dk = rotary(split_heads_2(dk, DIL_HEADS), ROPE_DIM, ROPE_THETA_2)
    dil = merge_heads_2(dilated_attention(dq, dk, split_heads_2(dv, DIL_HEADS)))
    return jnp.concatenate([ret, dil], axis=-1) @ w_out

def stick_breaking_mixer(x, norm_g, w_in, w_out):
    h = rms_norm_2(x, norm_g)
    q, k, v = jnp.split(h @ w_in, 3, axis=-1)
    o = stick_breaking_attention(split_heads_2(q, SB_HEADS), split_heads_2(k, SB_HEADS), split_heads_2(v, SB_HEADS))
    return merge_heads_2(o) @ w_out

def second_inputs(seed: int = 0) -> dict:
    key = jax.random.key(seed)
    ks = jax.random.split(key, 16)
    f32 = jnp.float32

    def gain(k, shape):
        return 1.0 + 0.02 * jax.random.normal(k, shape, f32)

    def dense(k, shape, fan_in):
        return jax.random.normal(k, shape, f32) * (fan_in ** -0.5)

    return {
        'x': jax.random.normal(ks[0], (BATCH, SEQ, D_MODEL), f32),
        'ffn1_norm': gain(ks[1], (DEPTH, D_MODEL)),
        'ffn1_w_in': dense(ks[2], (DEPTH, D_MODEL, 2 * D_FF), D_MODEL),
        'ffn1_w_out': dense(ks[3], (DEPTH, D_FF, D_MODEL), D_FF),
        'mix_norm': gain(ks[4], (DEPTH, D_MODEL)),
        'ffn2_norm': gain(ks[5], (DEPTH, D_MODEL)),
        'ffn2_w_in': dense(ks[6], (DEPTH, D_MODEL, 2 * D_FF), D_MODEL),
        'ffn2_w_out': dense(ks[7], (DEPTH, D_FF, D_MODEL), D_FF),
        'hyb_w_in': dense(ks[8], (N_EVEN, D_MODEL, HYB_IN), D_MODEL),
        'ret_gn': gain(ks[9], (N_EVEN, RET_WIDTH)),
        'hyb_w_out': dense(ks[10], (N_EVEN, RET_WIDTH + DIL_WIDTH, D_MODEL), RET_WIDTH + DIL_WIDTH),
        'sb_w_in': dense(ks[11], (N_ODD, D_MODEL, 3 * SB_WIDTH), D_MODEL),
        'sb_w_out': dense(ks[12], (N_ODD, SB_WIDTH, D_MODEL), SB_WIDTH),
        'final_norm': gain(ks[13], (D_MODEL,)),
    }

def second_block(x, ffn1_norm, ffn1_w_in, ffn1_w_out, mix_norm, ffn2_norm, ffn2_w_in, ffn2_w_out,
              hyb_w_in, ret_gn, hyb_w_out, sb_w_in, sb_w_out, final_norm):
    for layer in range(DEPTH):
        x = x + 0.5 * swiglu_ffn(x, ffn1_norm[layer], ffn1_w_in[layer], ffn1_w_out[layer])
        if layer % 2 == 0:
            e = layer // 2
            x = x + retention_dilated_mixer(x, mix_norm[layer], hyb_w_in[e], ret_gn[e], hyb_w_out[e])
        else:
            o = layer // 2
            x = x + stick_breaking_mixer(x, mix_norm[layer], sb_w_in[o], sb_w_out[o])
        x = x + 0.5 * swiglu_ffn(x, ffn2_norm[layer], ffn2_w_in[layer], ffn2_w_out[layer])
    return rms_norm_2(x, final_norm)


def setup_inputs(seed=0):
    out = dict(first_inputs(seed))
    for name, value in second_inputs(seed + 1).items():
        if name != "x":
            out[name + "_2"] = value
    return out


def reference(
    x, c, ctx, c_ctx, w_mod, b_mod, ln_g, ln_b, ffn_w_in, ffn_w_out, gmlp_w_in, gmlp_ln_g,
    gmlp_ln_b, gmlp_w_s, gmlp_b_s, gmlp_w_out, attn_w_qkv, attn_q_norm, attn_k_norm, attn_w_o,
    ffn1_norm_2, ffn1_w_in_2, ffn1_w_out_2, mix_norm_2, ffn2_norm_2, ffn2_w_in_2, ffn2_w_out_2,
    hyb_w_in_2, ret_gn_2, hyb_w_out_2, sb_w_in_2, sb_w_out_2, final_norm_2,
):
    x = first_block(
        x, c, ctx, c_ctx, w_mod, b_mod, ln_g, ln_b, ffn_w_in, ffn_w_out, gmlp_w_in, gmlp_ln_g,
        gmlp_ln_b, gmlp_w_s, gmlp_b_s, gmlp_w_out, attn_w_qkv, attn_q_norm, attn_k_norm,
        attn_w_o,
    )
    return second_block(
        x, ffn1_norm_2, ffn1_w_in_2, ffn1_w_out_2, mix_norm_2, ffn2_norm_2, ffn2_w_in_2,
        ffn2_w_out_2, hyb_w_in_2, ret_gn_2, hyb_w_out_2, sb_w_in_2, sb_w_out_2, final_norm_2,
    )


_drawn_inputs = setup_inputs


def setup_inputs(seed=0):
    import zlib

    import numpy as np

    out = dict(_drawn_inputs(seed))
    spreads = {}
    factors = {'ctx': 2.771,
     'gmlp_ln_g': 8.0,
     'gmlp_ln_b': 8.0,
     'gmlp_b_s': 8.0,
     'attn_q_norm': 8.0,
     'attn_k_norm': 8.0,
     'ffn1_norm_2': 4.21,
     'ffn2_norm_2': 5.784,
     'ret_gn_2': 30.278,
     'final_norm_2': 7.738}
    for name, (base, spread) in spreads.items():
        noise = np.random.default_rng([zlib.crc32(name.encode()), seed]).standard_normal(out[name].shape)
        drawn = base * np.exp(spread * noise) if base else spread * noise
        out[name] = __import__('jax').numpy.asarray(drawn.astype(out[name].dtype))
    for name, factor in factors.items():
        out[name] = (out[name] * factor).astype(out[name].dtype)
    return out
```

```python
import concourse.bass as bass
from concourse import mybir
from contextlib import ExitStack

D = 1024
P = 128
DC = D // P
TOK = 512
FF = 2816
FT = FF // P
GT = 3 * D // P
GROUPS = 8
ALPHA = 4.0 ** 0.25
LN_EPS = 1e-5
RMS_EPS = 1e-6
RING = 4
AHEAD = 3
UNIT = 1024
LAT, CTX = 0, 1

FFN, GMLP, ATTN, HYB, SB = "ffn", "gmlp", "attn", "hyb", "sb"
STAGES = [FFN, GMLP, FFN, FFN, ATTN, FFN, FFN, HYB, FFN, FFN, SB, FFN]
N_MODULATED = 6
TILES = [4, 4, 4, 4] + [2] * 8
OUT_K = [{FFN: FT, GMLP: GT}.get(s, DC) for s in STAGES]
PROJ_GROUPS = {ATTN: 3, HYB: 7, SB: 6}


class Phase:

    def __init__(self, kind, stage, first, rounds, **more):
        self.kind, self.stage, self.first, self.rounds = kind, stage, first, rounds
        self.units = sum(trips * len(body) for trips, body in rounds)
        self.more = more


def tiles_ready(s):
    return 4 + sum(TILES[:s])


def plan():
    phases, at = [], 0

    def add(kind, stage, rounds, **more):
        nonlocal at
        phases.append(Phase(kind, stage, at, rounds, **more))
        at += phases[-1].units

    def chunk(a, b):
        return [("M", 4 * a + q, 4 * b) for q in range(4)]

    def shifted(body, by):
        return [(k, a + by * b, b) for k, a, b in body]

    def proj(groups, first_peeled):
        body = [("B", u, 8) for u in range(8)]
        rounds = [(1, body), (groups // 2 - 1, shifted(body, 1))] if first_peeled else [(groups // 2, body)]
        if groups % 2:
            rounds.append((1, [("B", 4 * (groups - 1) + q, 0) for q in range(4)]))
        return rounds

    def out(k):
        rounds = [(1, [("O", j, 0) for j in range(4)])]
        turns = max(0, (k - 8) // 4)
        if turns:
            rounds.append((turns, [("O", 4 + j, 4) for j in range(4)]))
        middle = [("O", j, 0) for j in range(4 + 4 * turns, k - RING)]
        return rounds + ([(1, middle)] if middle else [])

    add("mod", -1, [(1, chunk(0, 0)), (3, chunk(1, 1))])
    chunks = 4
    for s, kind in enumerate(STAGES):
        if kind == FFN:
            mods = {0: 10, 2: 10, 3: 6}.get(s, 0)
            m = chunk(chunks, 1)
            mixed = m[:2] + [("G", 0, 2), ("U", 0, 2)] + m[2:] + [("G", 1, 2), ("U", 1, 2)]
            rounds = []
            if mods and s == 0:
                rounds = [(1, mixed), (mods - 1, shifted(mixed, 1))]
            elif mods:
                rounds = [(mods, mixed)]
            rest = FT // 2 - mods
            rounds.append((rest, [("G", 2 * mods, 2), ("U", 2 * mods, 2), ("G", 2 * mods + 1, 2), ("U", 2 * mods + 1, 2)]))
            add("ffn_in", s, rounds)
            chunks += mods
        elif kind == GMLP:
            add("v", s, proj(GT // 4, True), vec=LAT)
            m = chunk(chunks, 1)
            body = m[:2] + [("F", 0, 4), ("F", 1, 4)] + m[2:] + [("F", 2, 4), ("F", 3, 4)]
            add("u", s, [(GT // 4, body)])
            chunks += GT // 4
            add("v", s, proj(GT // 4, False), vec=CTX)
        else:
            groups = PROJ_GROUPS[kind]
            if kind == ATTN:
                add("proj", s, [(1, [("B", u, 0) for u in range(4 * groups)])])
            else:
                add("proj", s, proj(groups, False))
        add("out", s, out(OUT_K[s]))
        add("tail", s, [(1, [("O", j, 0) for j in range(OUT_K[s] - RING, OUT_K[s])])])
    return phases, at


def fused_blocks(nc, a):
    f32, f32r = mybir.dt.float32, mybir.dt.float32r
    ALU, ACT, AX = mybir.AluOpType, mybir.ActivationFunctionType, mybir.AxisListType
    MUL, ADD, SUB = ALU.mult, ALU.add, ALU.subtract
    phases, n_units = plan()

    with ExitStack() as ctx:
        def sb(name, shape, dt=f32):
            return ctx.enter_context(nc.sbuf_tensor(name, shape, dt))

        def sem(name):
            return ctx.enter_context(nc.semaphore(name))

        w32 = sb("w32", [P, RING, UNIT])
        whi = sb("whi", [P, RING, UNIT], f32r)
        wlo = sb("wlo", [P, RING, UNIT], f32r)
        xhi = sb("xhi", [P, DC, TOK], f32r)
        xlo = sb("xlo", [P, DC, TOK], f32r)
        hid = sb("hid", [P, GT, TOK])
        hs = sb("hs", [P, RING, 2, TOK], f32r)
        X = sb("X", [P, 4, D])
        arena = sb("arena", [P, 6144])
        side = sb("side", [P, 2048])
        cvec = sb("cvec", [P, DC, P], f32r)
        modrow = sb("modrow", [P, 512])
        modcol = sb("modcol", [P, 2 * 9 * DC * 2])
        cols = sb("cols", [P, a["cols"].shape[1]])
        consts = sb("consts", [P, a["consts"].shape[1]])
        coef = sb("coef", [P, 4, DC, 2])
        csil = sb("csil", [P, DC, 2])
        bnst = sb("bnst", [P, 4, 6, 6])
        mv = sb("mv", [P, 4, 2])
        std = sb("std", [P, 64])
        rstd = sb("rstd", [P, 64])
        stat = sb("stat", [P, 64])
        mx = sb("mx", [P, 16])
        den = sb("den", [P, 16])
        rden = sb("rden", [P, 16])
        ps = ctx.enter_context(nc.psum_tensor("ps", [P, 8, 512], f32))

        hidf = hid[:, :, :].rearrange("p c n -> p (c n)")
        Xf = X[:, :, :].rearrange("p t n -> p (t n)")
        ident, ones, sel = consts[:, 0:P], consts[:, P:2 * P], consts[:, 2 * P:2 * P + 2]

        def col(name, per):
            at = {"c": 0, "b_mod": 16, "ln_g": 160, "ln_b": 208, "gmlp_g": 256}[name]
            return cols[:, at:at + per]

        c_col = col("c", 16).rearrange("p (c v) -> p c v", v=2)
        bmod = col("b_mod", 144)
        lng = col("ln_g", 48).rearrange("p (s c) -> p s c", c=DC)
        lnb = col("ln_b", 48).rearrange("p (s c) -> p s c", c=DC)
        gmg = col("gmlp_g", GT)
        gate_row = arena[:, 0:2 * D].rearrange("p (v n) -> p v n", v=2)
        g_row, b_row = arena[:, 2 * D:3 * D], arena[:, 3 * D:4 * D]
        diag = arena[:, 4 * D:5 * D]
        full = arena[:, 4 * D:6 * D].rearrange("p (b n) -> p b n", b=2)
        next_gain = arena[:, 4 * D:5 * D]
        normed = [arena[:, D:2 * D], arena[:, 0:D]]
        v_tok = arena[:, :].rearrange("p (t n) -> p t n", t=2)
        wsT = side[:, 0:GROUPS * P]
        lnb_row, sum_row = side[:, 1024:1792], side[:, 1792:2048]

        mixbuf = modrow[:, :].rearrange("p (b n) -> p b n", b=2)

        def modv(layer, v):
            at = (layer * 9 + v) * DC * 2
            return modcol[:, at:at + DC * 2].rearrange("p (c v) -> p c v", v=2)

        landed = [sem(f"unit_landed{i}") for i in range(RING)]
        hi_ready, lo_ready, unit_used = sem("hi_ready"), sem("lo_ready"), sem("unit_used")
        names = """gate_ready hid_ready proj_ready vstat_ready modrow_ready modcol_ps modcol_ready
            hs_hi hs_lo y_ready diag_ready gate_ps gate_row_ready dve_step act_step pool_step
            var_ready std_ready norm_ready xT_ps full_ready x_ready xres_ready coef_ready
            mix_ps mix_scaled mix_step mix_done v_normed rs_ps rs_ready qk_ready qkT_ps qkT_ready
            s_ps max_ready exp_ready p_ready pT_ps pT_ready o_ps o_ready
            ret_s_ps ret_s_ready ret_o_ps ret_ready silu_rg retT_ps
            z_ps negabs_ready log_ready stay_ready later_ps arg_ready a_exp a_ready ss_ready
            csil_ready cvec_ready out_ready""".split()
        S = {n: sem(n) for n in names}
        loads = {n: sem("loaded_" + n) for n in ("x", "consts", "cols", "gmlp", "rows", "attn", "hyb", "decay", "gain")}
        stored = sem("stored")

        class Tally:

            def __init__(self):
                self.n = {}

            def __call__(self, name, k=1):
                self.n[name] = self.n.get(name, 0) + k
                return self.n[name]

        class Chain:

            def __init__(self, eng, ended):
                self.eng, self.ended, self.n = eng, ended, 0

            def give(self, ins):
                self.n += 1
                ins.then_inc(self.ended, 1)

            def wait(self):
                self.eng.wait_ge(self.ended, self.n)

            def __call__(self, ins):
                self.give(ins)
                self.wait()

        def walk(eng, phase, visit):
            n0 = phase.first
            for trips, body in phase.rounds:
                def once(i):
                    for off, (kind, x, b) in enumerate(body):
                        visit(kind, x, x + b * i, n0 + off, i * (len(body) // RING), i)
                if trips == 1:
                    once(0)
                else:
                    assert len(body) % RING == 0
                    with eng.Fori(0, trips) as i:
                        once(i)
                n0 += trips * len(body)

        tiles_before, hs_before, groups_before = {}, {}, {}
        n_tiles = n_hs = n_groups = 0
        for p_ in phases:
            if p_.kind in ("ffn_in", "u"):
                tiles_before[p_.stage] = n_tiles
                n_tiles += FT if p_.kind == "ffn_in" else GT
            if p_.kind == "out":
                hs_before[p_.stage] = n_hs
                n_hs += OUT_K[p_.stage]
            if p_.kind in ("v", "proj"):
                groups_before[p_.first] = n_groups
                n_groups += GT // 4 if p_.kind == "v" else PROJ_GROUPS[STAGES[p_.stage]]
        mods_by, n_mods = {}, 0
        for p_ in phases:
            here = sum(trips * sum(k == "M" for k, _, _ in body) for trips, body in p_.rounds) // 4
            n_mods += here
            if here:
                mods_by[p_.stage] = n_mods
        hid_before, n_hid = {}, 0
        for s, kind in enumerate(STAGES):
            hid_before[s] = n_hid
            if kind == FFN:
                n_hid += FT

        def tokens(s):
            return TILES[s] * P

        def proj_dst(s):
            w = {HYB: 3584, SB: 3072}[STAGES[s]]
            return hidf[:, 0:2 * w].rearrange("p (t n) -> p t n", t=2)

        att = dict(
            q=Xf[:, 2048:4096].rearrange("p (t n) -> p t n", t=2),
            kv=hidf[:, 0:2048].rearrange("p (t n) -> p t n", t=4),
            qT=hidf[:, 2048:4096].rearrange("p (h n) -> p h n", h=8),
            kT=hidf[:, 4096:5120].rearrange("p (h n) -> p h n", h=2),
            P=hidf[:, 5120:6144].rearrange("p (b n) -> p b n", b=2),
            PT=hidf[:, 6144:8192].rearrange("p (b k n) -> p b k n", b=2, k=4),
            oT=hidf[:, 8192:10240].rearrange("p (c n) -> p c n", c=8),
            tmp=hidf[:, 10240:12288],
        )
        HW_ = 3584
        hyb = dict(
            qkT=hidf[:, 7168:11264].rearrange("p (c n) -> p c n", c=16),
            PT=hidf[:, 11264:12288].rearrange("p (b k n) -> p b k n", b=2, k=2),
            oT=arena[:, 0:2048].rearrange("p (c n) -> p c n", c=8),
            tmp=arena[:, 2048:4096],
            St=arena[:, 4096:4864].rearrange("p (b n) -> p b n", b=2),
            P=arena[:, 4864:5376].rearrange("p (b n) -> p b n", b=2),
            gn=arena[:, 5376:5888],
            decay=Xf[:, 2048:4096].rearrange("p (h n) -> p h n", h=8),
            ret=hidf[:, 0:HW_ * 2].rearrange("p (t n) -> p t n", t=2)[:, :, 0:512],
            sq=hidf[:, 0:HW_ * 2].rearrange("p (t n) -> p t n", t=2)[:, :, 512:1024],
        )
        sbk = dict(
            qkT=hidf[:, 6144:10240].rearrange("p (c n) -> p c n", c=16),
            oT=hidf[:, 10240:12288].rearrange("p (c n) -> p c n", c=8),
            E=arena[:, 0:1536].rearrange("p (b h n) -> p b h n", b=2, h=2),
            LS=arena[:, 1536:3072].rearrange("p (b h n) -> p b h n", b=2, h=2),
            ST=arena[:, 3072:4608].rearrange("p (b h n) -> p b h n", b=2, h=2),
            A=arena[:, 4608:6144].rearrange("p (b h n) -> p b h n", b=2, h=2),
        )
        T = dict(att_rope=side[:, 0:256].rearrange("p (k t n) -> p k t n", k=2, t=2),
                 qk_gain=side[:, 256:512].rearrange("p (k n) -> p k n", k=2),
                 ret_rope=side[:, 512:640].rearrange("p (k t n) -> p k t n", k=2, t=2),
                 dil_rope=side[:, 640:672].rearrange("p (k t n) -> p k t n", k=2, t=2),
                 mask=side[:, 672:928], count=side[:, 928:1184],
                 causal=side[:, 1184:1312], tri=side[:, 1312:1440])

        def out_source(s):
            return {ATTN: att["oT"], HYB: hyb["oT"], SB: sbk["oT"]}.get(STAGES[s])

        block = ctx.enter_context(nc.Block())

        @block.sync
        def _(sp):
            def load(kind, x, idx, n0, q, i):
                src = sources[kind]
                if n0 >= RING or not isinstance(q, int):
                    sp.wait_ge(S_lo, n0 - RING + 1 + RING * q)
                sp.dma_start(w32[:, n0 % RING, :],
                             src[bass.ds(idx, 1), :, :].rearrange("o p n -> p (o n)")
                             ).then_inc(landed[n0 % RING], 16)

            S_lo = lo_ready
            ffn = 0
            for ph in phases:
                s = ph.stage
                sources = {"M": a["w_mod"]}
                if ph.kind == "ffn_in":
                    sources["G"], sources["U"] = a["ffn_gate"][ffn], a["ffn_up"][ffn]
                elif ph.kind == "u":
                    sources["F"] = a["gmlp_u"]
                elif ph.kind == "v":
                    sources["B"] = a["gmlp_v"]
                elif ph.kind == "proj":
                    sources["B"] = a[STAGES[s] + "_in"]
                elif ph.kind in ("out", "tail"):
                    sources["O"] = a["ffn_out"][ffn] if STAGES[s] == FFN else a[STAGES[s] + "_out"]
                    ffn += ph.kind == "tail" and STAGES[s] == FFN
                walk(sp, ph, load)

        @block.gpsimd
        def _(pool):
            chain = Chain(pool, S["pool_step"])
            pool.dma_start(consts[:, :], a["consts"]).then_inc(loads["consts"], 16)
            pool.dma_start(cols[:, :], a["cols"]).then_inc(loads["cols"], 16)
            pool.dma_start(X[:, 0:2, :], a["x"]).then_inc(loads["x"], 16)
            pool.dma_start(X[:, 2:4, :], a["ctx"]).then_inc(loads["x"], 16)
            pool.dma_start(wsT, a["wsT"]).then_inc(loads["gmlp"], 16)
            chain(nc.gpsimd.memset(side[:, 1024:2048], 1.0))
            for i in range(4):
                pool.dma_start(lnb_row[32 * i:32 * i + 1, :], a["gmlp_ln_b"][i:i + 1, :]).then_inc(loads["gmlp"], 16)
                pool.dma_start(sum_row[32 * i + 1:32 * i + 2, :], a["gmlp_b_s"][i:i + 1, :]).then_inc(loads["gmlp"], 16)
            done = Tally()
            for s in range(N_MODULATED):
                pool.wait_ge(S["gate_row_ready"], done("gate_row", 2 if TILES[s] == 4 else 1))
                if s == 1:
                    pool.wait_ge(S["mix_done"], 2 * GT)
                    pool.dma_start(side[:, 0:256], a["att_rope"]).then_inc(loads["attn"], 16)
                    for k, g in enumerate(("q_norm", "k_norm")):
                        pool.dma_start(T["qk_gain"][:, k, :], a[g].to_broadcast((P, P))).then_inc(loads["attn"], 16)
                    pool.dma_start(side[:, 512:1440], a["tables"]).then_inc(loads["hyb"], 16)
                pool.dma_start(g_row, a["ln_g"][s:s + 1, :].to_broadcast((P, D))).then_inc(loads["rows"], 16)
                pool.dma_start(b_row, a["ln_b"][s:s + 1, :].to_broadcast((P, D))).then_inc(loads["rows"], 16)
                if s == 5:
                    continue
                pool.wait_ge(loads["rows"], 32 * (s + 1))
                for t in range(4 if s < 3 else 2):
                    pool.wait_ge(S["xT_ps"], tiles_ready(s) + t + 1)
                    chain(nc.gpsimd.tensor_tensor(X[:, t, :], X[:, t, :], g_row, MUL))
                    nc.gpsimd.tensor_tensor(X[:, t, :], X[:, t, :], b_row, ADD).then_inc(S["xres_ready"], 1)
                pool.wait_ge(S["xres_ready"], 4 * min(s + 1, 3) + 2 * max(0, s - 2))
            outputs = {ATTN: 8, HYB: 17, SB: 25}
            for s in range(5, len(STAGES)):
                if s > 5:
                    pool.wait_ge(S["norm_ready"], tiles_ready(s) - 4)
                if STAGES[s] in outputs:
                    pool.wait_ge(S["o_ready"], outputs[STAGES[s]])
                gain = a["norm_rows"][s - 5:s - 4, :]
                pool.dma_start(next_gain, gain.to_broadcast((P, D))).then_inc(loads["gain"], 16)
                if s == 5:
                    pool.wait_ge(S["norm_ready"], tiles_ready(6) - 4)
                    pool.dma_start(hyb["decay"], a["decay"]).then_inc(loads["decay"], 16)
                if s == 6:
                    pool.wait_ge(S["x_ready"], tiles_ready(7))
                    pool.dma_start(hyb["gn"], a["ret_gn"].to_broadcast((P, 512))).then_inc(loads["decay"], 16)
            for t in range(2):
                pool.wait_ge(S["out_ready"], t + 1)
                pool.dma_start(a["out"][:, t, :], X[:, t, :]).then_inc(stored, 16)
            pool.wait_ge(stored, 32)

        @block.scalar
        def _(act):
            seen = Tally()
            ident_f = ACT.Identity

            def split_hi(n0, q):
                if isinstance(q, int) and n0 >= n_units:
                    return
                act.wait_ge(landed[n0 % RING], 16 * (n0 // RING + 1) + 16 * q)
                if n0 >= RING or not isinstance(q, int):
                    act.wait_ge(unit_used, n0 - RING + 1 + RING * q)
                nc.scalar.copy(whi[:, n0 % RING, :], w32[:, n0 % RING, :]).then_inc(hi_ready, 1)

            def hs_hi(s, src, k, x):
                n = tokens(s)
                nc.scalar.copy(hs[:, x % RING, 0, 0:n], src(k)).then_inc(S["hs_hi"], 1)

            def transposed(t, modulated):
                n = seen("tile")
                act.wait_ge(S["xT_ps"], n)
                bank = ps[:, 2 * t:2 * t + 2, :].rearrange("p b (c n) -> p (b c) n", n=P)
                high = xhi[:, :, t * P:(t + 1) * P]
                if modulated:
                    if n > 2:
                        act.wait_ge(S["x_ready"], n - 2)
                    f = full[:, n % 2, :].rearrange("p (c n) -> p c n", n=P)
                    for c in range(DC):
                        ins = nc.scalar.activation(f[:, c, :], bank[:, c, :], ident_f,
                                                   scale=coef[:, 0, c, t // 2:t // 2 + 1], bias=coef[:, 1, c, t // 2:t // 2 + 1])
                    ins.then_inc(S["act_step"], 1)
                    act.wait_ge(S["act_step"], seen("act_step"))
                    nc.scalar.copy(high, f).then_inc(S["full_ready"], 1)
                else:
                    nc.scalar.copy(high, bank).then_inc(S["full_ready"], 1)

            def sqrt(dst, src, scale, eps):
                act.wait_ge(S["var_ready"], seen("var_ready"))
                nc.scalar.activation(dst, src, ACT.Sqrt, bias=eps, scale=scale).then_inc(S["std_ready"], 1)

            def gates(s):
                for v in range(2 if TILES[s] == 4 else 1):
                    act.wait_ge(S["gate_ps"], seen("gate_ps"))
                    nc.scalar.activation(gate_row[:, v, :].rearrange("p (h n) -> p h n", h=2), ps[:, 6:8, :],
                                         ACT.Copy, scale=0.5 if STAGES[s] == FFN else 1.0
                                         ).then_inc(S["gate_row_ready"], 1)

            def sum_squares(t):
                act.wait_ge(S["ss_ready"], seen("ss_ready"))
                nc.scalar.activation(normed[t], X[:, t, :], ACT.Square,
                                     accum_out=stat[:, t:t + 1]).then_inc(S["act_step"], 1)
                act.wait_ge(S["act_step"], seen("act_step"))
                nc.scalar.activation(std[:, 8 + t:9 + t], stat[:, t:t + 1], ACT.Sqrt, bias=consts[:, 260:261],
                                     scale=1.0 / D).then_inc(S["std_ready"], 1)

            def epilogue(s, first):
                n = TILES[s]
                for t in range(n):
                    if t == n - 1:
                        split_hi(first, 0)
                    if 0 < t and s < 11:
                        transposed(t - 1, s < 5)
                    if s < N_MODULATED:
                        sqrt(std[:, t:t + 1], mv[:, t, 1:2], 1.0, consts[:, 261:262])
                    if s >= 5:
                        sum_squares(t)
                if s < 11:
                    transposed(n - 1, s < 5)
                for k in range(1, AHEAD):
                    split_hi(first + k, 0)
                table = {GMLP: ACT.Gelu}.get(STAGES[min(s + 1, 11)], ACT.Silu)
                nc.scalar.activation(std[:, 63:64], consts[:, 260:261], table).then_inc(S["act_step"], 1)
                seen("act_step")

            def mix(vec):
                for c in range(GT):
                    i = GT * vec + c
                    act.wait_ge(S["mix_ps"], i + 1)
                    if i >= 2:
                        act.wait_ge(S["mix_done"], i - 1)
                    nc.scalar.activation(mixbuf[:, c % 2, :], ps[:, 4 + c % 4, 0:256], ACT.Copy,
                                         scale=gmg[:, c:c + 1]).then_inc(S["mix_scaled"], 1)

            def attention():
                act.wait_ge(S["qkT_ps"], seen("qkT_ps"))
                nc.scalar.copy(att["qT"].rearrange("p (b h) n -> p b (h n)", b=4), ps[:, 0:4, :]).then_inc(S["qkT_ready"], 1)
                nc.scalar.copy(att["kT"], ps[:, 4:6, :]).then_inc(S["qkT_ready"], 1)

                def exp(i):
                    act.wait_ge(S["max_ready"], i + 1)
                    if i >= 2:
                        act.wait_ge(S["pT_ps"], i - 1)
                    nc.scalar.activation(att["P"][:, i % 2, :], ps[:, i % 2, :], ACT.Exp, bias=mx[:, i:i + 1],
                                         scale=P ** -0.5, accum_out=den[:, i:i + 1]).then_inc(S["exp_ready"], 1)

                exp(0)
                for i in range(16):
                    h, t = divmod(i, 2)
                    if i < 15:
                        exp(i + 1)
                    act.wait_ge(S["pT_ps"], i + 1)
                    if t == 0 and h >= 2:
                        act.wait_ge(S["o_ps"], h - 1)
                    nc.scalar.copy(att["PT"][:, h % 2, :, t * P:(t + 1) * P],
                                   ps[:, 2 + i % 2, :].rearrange("p (k n) -> p k n", k=4)).then_inc(S["pT_ready"], 1)
                    if t == 1:
                        act.wait_ge(S["o_ps"], h + 1)
                        nc.scalar.copy(att["oT"][:, h, :], ps[:, 4 + h % 2, 0:256]).then_inc(S["o_ready"], 1)

            def qk_transposed(dst):
                for half in range(2):
                    act.wait_ge(S["qkT_ps"], seen("qkT_ps"))
                    nc.scalar.copy(dst[:, 8 * half:8 * half + 8, :].rearrange("p (b h) n -> p b (h n)", b=4),
                                   ps[:, 4 * half:4 * half + 4, :]).then_inc(S["qkT_ready"], 1)

            def hybrid():
                pr = proj_dst(7)
                qk_transposed(hyb["qkT"])
                sqrt(std[:, 0:16], stat[:, 16:32], 1.0 / 64, consts[:, 261:262])
                nc.scalar.activation(pr[:, :, 1536:2048], pr[:, :, 1536:2048], ACT.Silu).then_inc(S["silu_rg"], 1)
                act.wait_ge(S["retT_ps"], 1)
                nc.scalar.copy(hyb["oT"][:, 0:4, :].rearrange("p (b h) n -> p b (h n)", b=2), ps[:, 4:6, :]
                               ).then_inc(S["o_ready"], 1)

                def exp(i):
                    n = P * (i % 2 + 1)
                    act.wait_ge(S["max_ready"], 16 + i + 1)
                    nc.scalar.activation(hyb["P"][:, i % 2, 0:n], hyb["P"][:, i % 2, 0:n], ACT.Exp, bias=mx[:, i:i + 1],
                                         scale=0.125).then_inc(S["exp_ready"], 1)

                exp(0)
                for i in range(16):
                    h, t = divmod(i, 2)
                    if i < 15:
                        exp(i + 1)
                    act.wait_ge(S["pT_ps"], 16 + i + 1)
                    if t == 0 and h >= 2:
                        act.wait_ge(S["o_ps"], 8 + h - 1)
                    nc.scalar.copy(hyb["PT"][:, h % 2, 0:t + 1, t * P:(t + 1) * P],
                                   ps[:, 2 + i % 2, 0:P * (t + 1)].rearrange("p (k n) -> p k n", k=t + 1)
                                   ).then_inc(S["pT_ready"], 1)
                    if t == 1:
                        act.wait_ge(S["o_ps"], 8 + h + 1)
                        r = slice(64 * (h % 2), 64 * (h % 2) + 64)
                        nc.scalar.copy(hyb["oT"][r, 4 + h // 2, :], ps[r, 4 + h % 2, 0:256]).then_inc(S["o_ready"], 1)

            def stick_breaking():
                qk_transposed(sbk["qkT"])

                def logs(g):
                    act.wait_ge(S["negabs_ready"], g + 1)
                    E_ = sbk["E"][:, g % 2]
                    nc.scalar.activation(E_, E_, ACT.Exp, scale=0.125).then_inc(S["act_step"], 1)
                    act.wait_ge(S["act_step"], seen("act_step"))
                    nc.scalar.activation(E_, E_, ACT.Ln, bias=1.0).then_inc(S["log_ready"], 1)

                logs(0)
                for g in range(8):
                    if g < 7:
                        logs(g + 1)
                    act.wait_ge(S["arg_ready"], g + 1)
                    A_ = sbk["A"][:, g % 2]
                    nc.scalar.activation(A_, A_, ACT.Exp).then_inc(S["a_exp"], 1)
                    act.wait_ge(S["o_ps"], 16 + g + 1)
                    nc.scalar.copy(sbk["oT"][:, g, :], ps[:, 4 + g % 2, 0:256]).then_inc(S["o_ready"], 1)

            act.wait_ge(loads["cols"], 16)
            nc.scalar.activation(csil[:, :, :], c_col, ACT.Silu).then_inc(S["csil_ready"], 1)
            act.wait_ge(loads["consts"], 16)
            for n in range(AHEAD):
                split_hi(n, 0)
            n_proj = n_o = 0
            for ph in phases:
                s = ph.stage
                N = tokens(s)

                def mod_row(ch, n0, q):
                    act.wait_ge(unit_used, n0 + 1 + RING * q)
                    if not isinstance(ch, int) or ch > 0:
                        act.wait_ge(S["modcol_ps"], ch)
                    nc.scalar.copy(modrow[:, :], ps[:, 4, :]).then_inc(S["modrow_ready"], 1)

                if ph.kind == "mod":
                    def visit(kind, x, idx, n0, q, i):
                        split_hi(n0 + AHEAD, q)
                        if x % 4 == 3:
                            mod_row(x // 4 + i, n0, q)
                    walk(act, ph, visit)
                    for t in range(4):
                        transposed(t, True)
                elif ph.kind in ("ffn_in", "u"):
                    func = ACT.Silu if ph.kind == "ffn_in" else ACT.Gelu

                    def visit(kind, x, idx, n0, q, i):
                        split_hi(n0 + AHEAD, q)
                        if kind in "GF":
                            act.wait_ge(unit_used, n0 + 1 + RING * q)
                            nc.scalar.activation(hidf[:, bass.ds(idx * TOK, N)], ps[:, x % 2, 0:N],
                                                 func).then_inc(S["gate_ready"], 1)
                        elif kind == "M" and x % 4 == 3:
                            mod_row(x // 4 + i, n0, q)
                    walk(act, ph, visit)
                    if ph.kind == "u":
                        mix(LAT)
                elif ph.kind in ("v", "proj"):
                    kind_ = STAGES[s]
                    if ph.kind == "v" and ph.more["vec"] == LAT:
                        act.wait_ge(S["xres_ready"], 4 * s)

                    def visit(kind, x, idx, n0, q, i):
                        split_hi(n0 + AHEAD, q)
                        if x % 4 != 3:
                            return
                        g = x // 4
                        act.wait_ge(unit_used, n0 + 1 + RING * q)
                        if kind_ == ATTN:
                            if g < 2:
                                dst, src = att["q"][:, :, 512 * g:512 * g + 512], ps[:, 2 * g:2 * g + 2, :]
                            else:
                                dst, src = att["kv"], ps[:, 4:8, :]
                        else:
                            b = 2 * (g % 2)
                            to = v_tok if kind_ == GMLP else proj_dst(s)
                            dst, src = to[:, :, bass.ds((idx - 3) * 128, 512)], ps[:, b:b + 2, :]
                        nc.scalar.activation(dst, src, ACT.Gelu if kind_ == GMLP else ACT.Copy
                                             ).then_inc(S["proj_ready"], 1)
                    walk(act, ph, visit)
                    if ph.kind == "v" and ph.more["vec"] == LAT:
                        act.wait_ge(S["rs_ps"], 1)
                        for i in range(4):
                            nc.scalar.copy(sum_row[32 * i:32 * i + 1, :], ps[32 * i:32 * i + 1, 7, 0:256]
                                           ).then_inc(S["rs_ready"], 1)
                    if ph.kind == "v":
                        sqrt(std[:, 0:2], mv[:, 0:2, 1], 1.0, consts[:, 261:262])
                        if ph.more["vec"] == CTX:
                            mix(CTX)
                    if kind_ == ATTN:
                        sqrt(std[:, 0:24], stat[:, 0:24], 1.0 / P, consts[:, 260:261])
                        attention()
                    if kind_ == HYB:
                        hybrid()
                    if kind_ == SB:
                        stick_breaking()
                elif ph.kind == "out":
                    if s < N_MODULATED:
                        gates(s)
                    K = OUT_K[s]
                    src_ap = out_source(s)
                    if STAGES[s] == FFN:
                        act.wait_ge(S["hid_ready"], hid_before[s] + FT)
                        src = lambda k: hidf[:, bass.ds(k * TOK, N)]
                    elif STAGES[s] == GMLP:
                        act.wait_ge(S["mix_done"], 2 * GT)
                        src = lambda k: hidf[:, bass.ds(k * TOK, N)]
                    else:
                        n_o += {ATTN: 8, HYB: 9, SB: 8}[STAGES[s]]
                        act.wait_ge(S["o_ready"], n_o)
                        src = lambda k: src_ap[:, k, :]
                    for k in range(AHEAD):
                        hs_hi(s, src, k, k)

                    def visit(kind, x, idx, n0, q, i):
                        split_hi(n0 + AHEAD, q)
                        hs_hi(s, src, idx + AHEAD, x + AHEAD)
                    walk(act, ph, visit)
                elif ph.kind == "tail":
                    k = OUT_K[s] - 1
                    split_hi(ph.first + RING - 1, 0)
                    hs_hi(s, src, k, k)
                    epilogue(s, ph.first + ph.units)

        @block.vector
        def _(dve):
            seen = Tally()
            chain = Chain(dve, S["dve_step"])
            V = nc.vector

            def split_lo(n0, q):
                if isinstance(q, int) and n0 >= n_units:
                    return
                dve.wait_ge(hi_ready, n0 + 1 + RING * q)
                V.tensor_tensor(wlo[:, n0 % RING, :], w32[:, n0 % RING, :], whi[:, n0 % RING, :], SUB
                                ).then_inc(lo_ready, 1)

            def hs_lo(s, src, k, x, count):
                n = tokens(s)
                dve.wait_ge(S["hs_hi"], count)
                V.tensor_tensor(hs[:, x % RING, 1, 0:n], src(k), hs[:, x % RING, 0, 0:n], SUB).then_inc(S["hs_lo"], 1)

            def split_x(t, modulated):
                n = seen("tile")
                dve.wait_ge(S["full_ready"], n)
                if modulated:
                    f = full[:, n % 2, :]
                else:
                    f = ps[:, 2 * t:2 * t + 2, :].rearrange("p b n -> p (b n)")
                r = slice(t * P, (t + 1) * P)
                V.tensor_tensor(xlo[:, :, r], f.rearrange("p (c n) -> p c n", n=P), xhi[:, :, r], SUB
                                ).then_inc(S["x_ready"], 1)

            def invert_std(n, at=0):
                dve.wait_ge(S["std_ready"], seen("std_ready"))
                chain(V.reciprocal(rstd[:, at:at + n], std[:, at:at + n]))

            def coefficients(s):
                layer, i = divmod(s + 1, 3)
                shift, scale = modv(layer, 3 * i), modv(layer, 3 * i + 1)
                dve.wait_ge(S["modcol_ready"], layer * 18 + 2 * (3 * i + 1) + 2)
                A_, B_ = coef[:, 0, :, :], coef[:, 1, :, :]
                if s < 0:
                    V.tensor_scalar(A_, scale, 1.0, None, ADD)
                    chain(V.tensor_copy(B_, shift))
                    return
                one = coef[:, 2, :, :]
                g = lng[:, s, :].unsqueeze(2).to_broadcast((P, DC, 2))
                b = lnb[:, s, :].unsqueeze(2).to_broadcast((P, DC, 2))
                chain(V.tensor_scalar(one, scale, 1.0, None, ADD))
                chain(V.tensor_tensor(A_, one, g, MUL))
                chain(V.tensor_tensor(B_, one, b, MUL))
                chain(V.tensor_tensor(B_, B_, shift, ADD))

            def gates(s):
                layer, i = divmod(s, 3)
                dve.wait_ge(S["modcol_ready"], layer * 18 + 2 * (3 * i + 2) + 2)
                gate = modv(layer, 3 * i + 2)
                for v in range(2 if TILES[s] == 4 else 1):
                    if v:
                        dve.wait_ge(S["gate_ps"], seen("gate_ps"))
                    V.tensor_tensor(diag.rearrange("p (c n) -> p c n", c=DC),
                                    ident.unsqueeze(1).to_broadcast((P, DC, P)),
                                    gate[:, :, v:v + 1].to_broadcast((P, DC, P)), MUL).then_inc(S["diag_ready"], 1)
                seen("gate_ps", 1)

            last_unit = {ph.stage: ph.first + ph.units for ph in phases if ph.kind == "tail"}

            def y_wait(s, t):
                if t < TILES[s] - 1:
                    dve.wait_ge(S["y_ready"], seen("y_ready"))
                else:
                    dve.wait_ge(unit_used, last_unit[s])

            def residual_norm(s, t):
                y = ps[:, 2 * t:2 * t + 2, :]
                Xt = X[:, t, :].rearrange("p (h n) -> p h n", h=2)
                y_wait(s, t)
                chain(V.tensor_tensor(y, y, gate_row[:, t // 2, :].rearrange("p (h n) -> p h n", h=2), MUL))
                chain(V.scalar_tensor_tensor(Xt, Xt, ALPHA, y, MUL, ADD))
                for h in range(2):
                    chain.give(V.bn_stats(bnst[:, t, h, :], X[:, t, 512 * h:512 * h + 512]))
                chain.wait()
                V.bn_aggr(mv[:, t, :], bnst[:, t, 0:2, :]).then_inc(S["var_ready"], 1)
                invert_std(1, t)
                ins = V.tensor_scalar(X[:, t, :], X[:, t, :], mv[:, t, 0:1], rstd[:, t:t + 1], SUB, MUL)
                if s < 5:
                    ins.then_inc(S["norm_ready"], 1)
                    return
                chain(ins)
                dve.wait_ge(loads["rows"], 32 * 6)
                chain(V.tensor_tensor(X[:, t, :], X[:, t, :], g_row, MUL))
                V.tensor_tensor(X[:, t, :], X[:, t, :], b_row, ADD).then_inc(S["ss_ready"], 1)

            def epilogue(s, first):
                n = TILES[s]
                if s < N_MODULATED:
                    if s < 5:
                        coefficients(s)
                    dve.wait_ge(S["gate_row_ready"], seen("gate_row", 2 if n == 4 else 1))
                    if s > 0:
                        dve.wait_ge(S["xres_ready"], 4 * min(s, 3) + 2 * max(0, s - 3))
                for t in range(n):
                    if t == n - 1:
                        split_lo(first, 0)
                    if s < N_MODULATED:
                        residual_norm(s, t)
                    else:
                        y_wait(s, t)
                        Xt = X[:, t, :].rearrange("p (h n) -> p h n", h=2)
                        V.scalar_tensor_tensor(Xt, ps[:, 2 * t:2 * t + 2, :], 0.5 if STAGES[s] == FFN else 1.0, Xt,
                                               MUL, ADD).then_inc(S["ss_ready"], 1)
                    if t and 5 <= s < 11:
                        split_x(t - 1, False)
                    if s >= 5:
                        dve.wait_ge(S["ss_ready"], seen("ss"))
                        invert_std(1, 8 + t)
                        if t == 0:
                            dve.wait_ge(loads["gain"], 16 * (s - 4))
                        dst = normed[t] if s < 11 else X[:, t, :]
                        V.scalar_tensor_tensor(dst, X[:, t, :], rstd[:, 8 + t:9 + t], next_gain, MUL, MUL
                                               ).then_inc(S["norm_ready" if s < 11 else "out_ready"], 1)
                    if t and s < 5:
                        split_x(t - 1, True)
                if s < 11:
                    split_x(n - 1, s < 5)
                for k in range(1, AHEAD):
                    split_lo(first + k, 0)

            def rope(x1, x2, cos, sin, tmp, heads, half):
                c = cos.unsqueeze(1).to_broadcast((P, heads, half))
                s_ = sin.unsqueeze(1).to_broadcast((P, heads, half))
                w = heads * half
                t4 = [tmp[:, k * w:(k + 1) * w].rearrange("p (h n) -> p h n", h=heads) for k in range(4)]
                for dst, x, table in zip(t4, (x1, x2, x2, x1), (c, s_, c, s_)):
                    chain.give(V.tensor_tensor(dst, x, table, MUL))
                chain.wait()
                chain.give(V.tensor_tensor(x1, t4[0], t4[1], SUB))
                ins = V.tensor_tensor(x2, t4[2], t4[3], ADD)
                chain(ins)

            def attention():
                q, kv, tmp = att["q"], att["kv"], att["tmp"]
                dve.wait_ge(loads["attn"], 48)
                views = [q[:, t, :].rearrange("p (h n) -> p h n", n=P) for t in range(2)]
                views.append(kv[:, :, 0:256].rearrange("p t (h n) -> p t h n", n=P))
                for k, v in enumerate(views):
                    sq = tmp[:, 0:1024]
                    sqv = sq.rearrange("p (h n) -> p h n", n=P) if k < 2 else sq.rearrange("p (t h n) -> p t h n", t=4, n=P)
                    chain(V.tensor_tensor(sqv, v, v, MUL))
                    ins = V.tensor_reduce(stat[:, 8 * k:8 * k + 8], sq.rearrange("p (h n) -> p h n", n=P), AX.X, ADD)
                    if k < 2:
                        chain(ins)
                    else:
                        ins.then_inc(S["var_ready"], 1)
                invert_std(24)
                gain = T["qk_gain"]
                for t in range(2):
                    v = views[t]
                    chain(V.tensor_tensor(v, v, rstd[:, 8 * t:8 * t + 8].unsqueeze(2).to_broadcast((P, 8, P)), MUL))
                    chain(V.tensor_tensor(v, v, gain[:, 0, :].unsqueeze(1).to_broadcast((P, 8, P)), MUL))
                for t in range(4):
                    v = kv[:, t, 0:256].rearrange("p (h n) -> p h n", n=P)
                    r = rstd[:, 16 + 2 * t:18 + 2 * t].unsqueeze(2).to_broadcast((P, 2, P))
                    chain(V.tensor_tensor(v, v, r, MUL))
                    chain(V.tensor_tensor(v, v, gain[:, 1, :].unsqueeze(1).to_broadcast((P, 2, P)), MUL))
                for t in range(2):
                    cos, sin = T["att_rope"][:, 0, t, :], T["att_rope"][:, 1, t, :]
                    for v, heads in ((views[t], 8), (kv[:, t, 0:256].rearrange("p (h n) -> p h n", n=P), 2)):
                        rope(v[:, :, 0:64], v[:, :, 64:128], cos, sin, tmp, heads, 64)
                V.tensor_copy(mx[:, 0:1], rstd[:, 0:1]).then_inc(S["qk_ready"], 1)
                dve.wait_ge(S["qk_ready"], 1)

                def top(i):
                    dve.wait_ge(S["s_ps"], i + 1)
                    chain(V.reduce_max(mx[:, i:i + 1], ps[:, i % 2, :], AX.X))
                    V.tensor_scalar(mx[:, i:i + 1], mx[:, i:i + 1], -(P ** -0.5), None, MUL).then_inc(S["max_ready"], 1)

                top(0)
                for i in range(16):
                    if i < 15:
                        top(i + 1)
                    dve.wait_ge(S["exp_ready"], i + 1)
                    chain(V.reciprocal(rden[:, i:i + 1], den[:, i:i + 1]))
                    Pi = att["P"][:, i % 2, :]
                    V.tensor_scalar(Pi, Pi, rden[:, i:i + 1], None, MUL).then_inc(S["p_ready"], 1)

            def hybrid():
                pr = proj_dst(7)
                tmp = hyb["tmp"]
                dve.wait_ge(loads["hyb"], 16)
                for t in range(2):
                    for at, table, half in ((0, T["ret_rope"], 32), (2048, T["dil_rope"], 8)):
                        v = pr[:, t, at:at + 1024].rearrange("p (h n) -> p h n", n=64)
                        rope(v[:, :, 0:half], v[:, :, half:2 * half], table[:, 0, t, :], table[:, 1, t, :], tmp, 16, half)
                V.tensor_copy(mx[:, 0:1], rstd[:, 0:1]).then_inc(S["qk_ready"], 1)
                dve.wait_ge(S["qk_ready"], 2)
                dve.wait_ge(loads["decay"], 32)
                for h in range(8):
                    dve.wait_ge(S["ret_s_ps"], h + 1)
                    if h >= 2:
                        dve.wait_ge(S["ret_o_ps"], h - 1)
                    St, dec = hyb["St"][:, h % 2, :], hyb["decay"][:, h, :]
                    chain.give(V.tensor_tensor(St[:, 0:256], ps[:, h % 2, 0:256], dec, MUL))
                    V.tensor_tensor(St[:, 256:384], ps[:, h % 2, 256:384], dec[:, 0:P], MUL).then_inc(S["ret_s_ready"], 1)
                dve.wait_ge(S["ret_o_ps"], 8)
                o = ps[:, 6:8, :].rearrange("p t (h n) -> p t h n", n=64)
                ret = hyb["ret"].rearrange("p t (h n) -> p t h n", n=64)
                sq = hyb["sq"].rearrange("p t (h n) -> p t h n", n=64)
                mean = stat[:, 0:16].rearrange("p (t h) -> p t h", t=2)
                var = stat[:, 16:32].rearrange("p (t h) -> p t h", t=2)

                def over(x):
                    return x.unsqueeze(3).to_broadcast((P, 2, 8, 64))

                def each(f):
                    for t in range(2):
                        chain.give(f(t))
                    chain.wait()

                chain(V.tensor_reduce(mean, o, AX.X, ADD))
                chain(V.tensor_scalar(mean, mean, 1.0 / 64, None, MUL))
                each(lambda t: V.tensor_tensor(ret[:, t], o[:, t], mean[:, t].unsqueeze(2).to_broadcast((P, 8, 64)), SUB))
                each(lambda t: V.tensor_tensor(sq[:, t], ret[:, t], ret[:, t], MUL))
                V.tensor_reduce(var, sq, AX.X, ADD).then_inc(S["var_ready"], 1)
                invert_std(16)
                r = rstd[:, 0:16].rearrange("p (t h) -> p t h", t=2)
                each(lambda t: V.tensor_tensor(ret[:, t], ret[:, t], r[:, t].unsqueeze(2).to_broadcast((P, 8, 64)), MUL))
                rt = hyb["ret"]
                each(lambda t: V.tensor_tensor(rt[:, t], rt[:, t], hyb["gn"], MUL))
                dve.wait_ge(S["silu_rg"], 1)
                for t in range(2):
                    V.tensor_tensor(rt[:, t], rt[:, t], pr[:, t, 1536:2048], MUL).then_inc(S["ret_ready"], 1)

                def top(i):
                    n = P * (i % 2 + 1)
                    dve.wait_ge(S["s_ps"], 16 + i + 1)
                    if i >= 2:
                        dve.wait_ge(S["pT_ps"], 16 + i - 1)
                    Pi = hyb["P"][:, i % 2, 0:n]
                    m = T["mask"][:, 256 - n:256]
                    chain(V.tensor_tensor(Pi, ps[:, i % 2, 0:n], m, ADD))
                    chain(V.reduce_max(mx[:, i:i + 1], Pi, AX.X))
                    V.tensor_scalar(mx[:, i:i + 1], mx[:, i:i + 1], -0.125, None, MUL).then_inc(S["max_ready"], 1)

                top(0)
                for i in range(16):
                    if i < 15:
                        top(i + 1)
                    n = P * (i % 2 + 1)
                    Pi = hyb["P"][:, i % 2, 0:n]
                    dve.wait_ge(S["exp_ready"], 16 + i + 1)
                    chain(V.scalar_tensor_tensor(Pi, Pi, 1.0, T["count"][:, 256 - n:256], MUL, MUL,
                                                 accum_out=den[:, i:i + 1]))
                    chain(V.reciprocal(rden[:, i:i + 1], den[:, i:i + 1]))
                    V.tensor_scalar(Pi, Pi, rden[:, i:i + 1], None, MUL).then_inc(S["p_ready"], 1)

            def stick_breaking():
                causal = T["causal"].unsqueeze(1).to_broadcast((P, 2, P))

                def masked(buf, last):
                    for h in range(2):
                        v = buf[:, h, :].rearrange("p (b n) -> p b n", b=3)[:, 0:3:2, :]
                        ins = V.tensor_tensor(v, v, causal, MUL)
                        if h:
                            last(ins)
                        else:
                            chain.give(ins)

                def z_of(g):
                    return ps[:, 2 * (g % 2):2 * (g % 2) + 2, 0:384]

                def negabs(g):
                    dve.wait_ge(S["z_ps"], g + 1)
                    chain(V.tensor_scalar(sbk["E"][:, g % 2], z_of(g), -1.0, None, MUL))
                    V.tensor_tensor(sbk["E"][:, g % 2], sbk["E"][:, g % 2], z_of(g), ALU.min).then_inc(S["negabs_ready"], 1)

                negabs(0)
                for g in range(8):
                    if g < 7:
                        negabs(g + 1)
                    b = g % 2
                    z, E_, LS, ST, A_ = z_of(g), sbk["E"][:, b], sbk["LS"][:, b], sbk["ST"][:, b], sbk["A"][:, b]
                    chain(V.tensor_scalar(LS, z, 0.0, 0.125, ALU.min, MUL))
                    dve.wait_ge(S["log_ready"], g + 1)
                    chain(V.tensor_tensor(LS, LS, E_, SUB))
                    chain(V.scalar_tensor_tensor(ST, z, -0.125, LS, MUL, ADD))
                    masked(ST, lambda ins: ins.then_inc(S["stay_ready"], 1))
                    dve.wait_ge(S["later_ps"], g + 1)
                    V.tensor_tensor(A_, LS, ps[:, 6:8, 0:384], ADD).then_inc(S["arg_ready"], 1)
                    dve.wait_ge(S["a_exp"], g + 1)
                    masked(A_, lambda ins: ins.then_inc(S["a_ready"], 1))

            dve.wait_ge(S["csil_ready"], 1)
            dve.wait_ge(loads["consts"], 16)
            for v in range(2):
                src = csil[:, :, v:v + 1].to_broadcast((P, DC, 32))
                h = cvec[:, :, 64 * v:64 * v + 32]
                chain(V.tensor_copy(h, src))
                V.tensor_tensor(cvec[:, :, 64 * v + 32:64 * v + 64], src, h, SUB).then_inc(S["cvec_ready"], 1)
            for n in range(AHEAD):
                split_lo(n, 0)
            for ph in phases:
                s = ph.stage
                N = tokens(s)

                def mod_column(ch):
                    dve.wait_ge(S["modcol_ps"], ch + 1)
                    V.tensor_tensor(modcol[:, bass.ds(ch * 8, 8)].rearrange("p (c v) -> p c v", v=2),
                                    ps[:, 5, 0:8].rearrange("p (c v) -> p c v", v=2),
                                    bmod[:, bass.ds(ch * 4, 4)].rearrange("p (c o) -> p c o", o=1).to_broadcast((P, 4, 2)),
                                    ADD).then_inc(S["modcol_ready"], 1)

                if ph.kind == "mod":
                    def visit(kind, x, idx, n0, q, i):
                        split_lo(n0 + AHEAD, q)
                        if x % 4 == 3:
                            mod_column(x // 4 + i)
                    walk(dve, ph, visit)
                    coefficients(-1)
                    V.tensor_copy(mx[:, 0:1], csil[:, 0, 0:1]).then_inc(S["coef_ready"], 1)
                    for t in range(4):
                        split_x(t, True)
                elif ph.kind in ("ffn_in", "u"):
                    pending = []

                    def visit(kind, x, idx, n0, q, i):
                        split_lo(n0 + AHEAD, q)
                        if kind == "M":
                            if x % 4 == 3:
                                pending.append(x // 4 + i)
                            return
                        if kind == "U":
                            dve.wait_ge(S["gate_ready"], tiles_before[s] + idx + 1)
                            dve.wait_ge(unit_used, n0 + 1 + RING * q)
                            h = hidf[:, bass.ds(idx * TOK, N)]
                            V.tensor_tensor(h, h, ps[:, 2 + x % 2, 0:N], MUL).then_inc(S["hid_ready"], 1)
                        if pending:
                            mod_column(pending.pop())
                    walk(dve, ph, visit)
                elif ph.kind in ("v", "proj"):
                    base = groups_before[ph.first]

                    def visit(kind, x, idx, n0, q, i):
                        split_lo(n0 + AHEAD, q)
                        if ph.kind == "v" and x % 4 == 3:
                            g = x // 4
                            dve.wait_ge(S["proj_ready"], base + g + 1 + q)
                            for t in range(2):
                                V.bn_stats(bnst[:, 2 * t:2 * t + 2, :, :].rearrange("p a b c -> p (a b c)")[:, bass.ds((g + q) * 6, 6)],
                                           v_tok[:, t, bass.ds((idx - 3) * 128, 512)]).then_inc(S["vstat_ready"], 1)
                    walk(dve, ph, visit)
                    if ph.kind == "v":
                        vec = ph.more["vec"]
                        dve.wait_ge(S["vstat_ready"], 12 * (vec + 1))
                        for t in range(2):
                            st_ = bnst[:, 2 * t:2 * t + 2, :, :].rearrange("p a b c -> p (a b c)")[:, 0:36]
                            ins = V.bn_aggr(mv[:, t, :], st_.rearrange("p (a b) -> p a b", b=6))
                            if t:
                                ins.then_inc(S["var_ready"], 1)
                            else:
                                chain.give(ins)
                        invert_std(2)
                        for t in range(2):
                            V.tensor_scalar(v_tok[:, t, :], v_tok[:, t, :], mv[:, t, 0:1], rstd[:, t:t + 1], SUB, MUL
                                            ).then_inc(S["v_normed"], 1)
                    if STAGES[s] == ATTN:
                        dve.wait_ge(S["proj_ready"], base + 3)
                        attention()
                    elif STAGES[s] == HYB:
                        dve.wait_ge(S["proj_ready"], base + 7)
                        hybrid()
                    elif STAGES[s] == SB:
                        dve.wait_ge(S["proj_ready"], base + 6)
                        stick_breaking()
                elif ph.kind == "out":
                    if s < N_MODULATED:
                        gates(s)
                    K = OUT_K[s]
                    src_ap = out_source(s)
                    src = (lambda k: hidf[:, bass.ds(k * TOK, N)]) if src_ap is None else (lambda k: src_ap[:, k, :])
                    for k in range(AHEAD):
                        hs_lo(s, src, k, k, hs_before[s] + k + 1)

                    def visit(kind, x, idx, n0, q, i):
                        split_lo(n0 + AHEAD, q)
                        hs_lo(s, src, idx + AHEAD, x + AHEAD, hs_before[s] + idx + AHEAD + 1)
                    walk(dve, ph, visit)
                elif ph.kind == "tail":
                    k = OUT_K[s] - 1
                    split_lo(ph.first + RING - 1, 0)
                    hs_lo(s, src, k, k, hs_before[s] + k + 1)
                    epilogue(s, ph.first + ph.units)
                if ph.kind in ("u", "v") and not (ph.kind == "v" and ph.more["vec"] == LAT):
                    vec = LAT if ph.kind == "u" else CTX
                    def affine(c):
                        dve.wait_ge(S["mix_scaled"], GT * vec + c + 1)
                        m = mixbuf[:, c % 2, :].rearrange("p (n q) -> p n q", n=2)
                        b = ps[:, 4 + c % 4, 256:384].unsqueeze(1).to_broadcast((P, 2, P))
                        V.tensor_tensor(m, m, b, ADD).then_inc(S["mix_step"], 1)

                    affine(0)
                    for c in range(GT):
                        if c < GT - 1:
                            affine(c + 1)
                        h = hid[:, c, 256 * vec:256 * vec + 256]
                        dve.wait_ge(S["mix_step"], GT * vec + c + 1)
                        if c == 0:
                            dve.wait_ge(S["gate_ready"], tiles_before[s] + GT)
                        V.tensor_tensor(h, h, mixbuf[:, c % 2, :], MUL).then_inc(S["mix_done"], 1)

        @block.tensor
        def _(pe):
            seen = Tally()
            mm = nc.tensor.matmul

            def passes(out, hi, lo, w_hi, w_lo, first, last, stationary_w):
                todo = [(hi, w_hi), (lo, w_hi), (hi, w_lo)] if stationary_w else [(hi, w_hi), (hi, w_lo), (lo, w_hi)]
                for k, (x, w) in enumerate(todo):
                    ins = mm(out, w if stationary_w else x, x if stationary_w else w,
                             start=first and k == 0, stop=last and k == 2)
                return ins

            def feature_unit(n0, bank, N):
                slot = n0 % RING
                for kt in range(DC):
                    w = slice(kt * P, kt * P + P)
                    ins = passes(ps[:, bank, 0:N], xhi[:, kt, 0:N], xlo[:, kt, 0:N], whi[:, slot, w], wlo[:, slot, w],
                                 kt == 0, kt == DC - 1, True)
                ins.then_inc(unit_used, 1)

            def token_unit(n0, quarter, tiles, banks):
                slot = n0 % RING
                for kk in range(2):
                    kt = 2 * quarter + kk
                    for t, bank in zip(tiles, banks):
                        r, w = slice(t * P, t * P + P), slice(512 * kk, 512 * kk + 512)
                        ins = passes(ps[:, bank, :], xhi[:, kt, r], xlo[:, kt, r], whi[:, slot, w], wlo[:, slot, w],
                                     kt == 0, kt == DC - 1, False)
                ins.then_inc(unit_used, 1)

            def mod_unit(n0, quarter):
                slot = n0 % RING
                for kk in range(2):
                    kt = 2 * quarter + kk
                    for w, part in ((whi, 0), (wlo, 1)):
                        ins = mm(ps[:, 4, :], cvec[:, kt, :], w[:, slot, 512 * kk:512 * kk + 512],
                                 start=kt == 0 and part == 0, stop=kt == DC - 1 and part == 1)
                ins.then_inc(unit_used, 1)

            def mod_column(ch):
                pe.wait_ge(S["modrow_ready"], ch + 1)
                if not isinstance(ch, int) or ch > 0:
                    pe.wait_ge(S["modcol_ready"], ch)
                for c in range(4):
                    ins = mm(ps[:, 5, 2 * c:2 * c + 2], modrow[:, c * P:c * P + P], sel, start=True, stop=True)
                ins.then_inc(S["modcol_ps"], 1)

            def out_products(s, n0, x, t, last):
                slot, h = n0 % RING, x % RING
                first = x == 0
                r = slice(t * P, t * P + P)
                hi, lo = hs[:, h, 0, r], hs[:, h, 1, r]
                for half in range(2):
                    w = slice(512 * half, 512 * half + 512)
                    mm(ps[:, 2 * t + half, :], hi, whi[:, slot, w], start=first, stop=False)
                    mm(ps[:, 2 * t + half, :], hi, wlo[:, slot, w], start=False, stop=False)
                for half in range(2):
                    w = slice(512 * half, 512 * half + 512)
                    ins = mm(ps[:, 2 * t + half, :], lo, whi[:, slot, w], start=False, stop=last)
                return ins

            def transposes(src, t):
                for c in range(DC):
                    ins = nc.tensor.transpose(ps[:, 2 * t + c // 4, (c % 4) * P:(c % 4 + 1) * P],
                                              src[:, c * P:(c + 1) * P], ident)
                ins.then_inc(S["xT_ps"], 1)

            def out_tail(s, first):
                k0, n = OUT_K[s] - RING, TILES[s]
                src = [X[:, t, :] for t in range(n)] if s < 5 else normed
                for t in range(n):
                    for j in range(RING):
                        if t == 0:
                            unit_wait(first + j, 0)
                            pe.wait_ge(S["hs_lo"], hs_before[s] + k0 + j + 1)
                        ins = out_products(s, first + j, k0 + j, t, j == RING - 1)
                        if t == n - 1:
                            ins.then_inc(unit_used, 1)
                    if t < n - 1:
                        ins.then_inc(S["y_ready"], 1)
                    if t and s < 11:
                        pe.wait_ge(S["norm_ready"], seen("norm"))
                        transposes(src[t - 1], t - 1)
                if s < 11:
                    pe.wait_ge(S["norm_ready"], seen("norm"))
                    transposes(src[n - 1], n - 1)

            def gates(s):
                for v in range(2 if TILES[s] == 4 else 1):
                    pe.wait_ge(S["diag_ready"], seen("diag"))
                    if v:
                        pe.wait_ge(S["gate_row_ready"], seen.n.get("gate_row", 0) + 1)
                    for h in range(2):
                        ins = mm(ps[:, 6 + h, :], ones, diag[:, 512 * h:512 * h + 512], start=True, stop=True)
                    ins.then_inc(S["gate_ps"], 1)
                seen("gate_row", 2 if TILES[s] == 4 else 1)
                pe.wait_ge(S["gate_row_ready"], seen.n["gate_row"])

            def mix(vec):
                pe.wait_ge(S["v_normed"], 2 * (vec + 1))
                if vec == LAT:
                    pe.wait_ge(S["rs_ready"], 4)
                for c in range(GT):
                    g, bank = c // 3, 4 + c % 4
                    i = GT * vec + c
                    if c >= 4:
                        pe.wait_ge(S["mix_done"], i - 3)
                    for n in range(2):
                        mm(ps[:, bank, n * P:(n + 1) * P], v_tok[:, n, c * P:(c + 1) * P], wsT[:, g * P:(g + 1) * P],
                           start=True, stop=True)
                    r = 32 * (c // 6)
                    mm(ps[:, bank, 256:384], lnb_row[r:r + 2, (c % 6) * P:(c % 6 + 1) * P],
                       sum_row[r:r + 2, (g % 2) * P:(g % 2 + 1) * P], start=True, stop=True).then_inc(S["mix_ps"], 1)

            def attention():
                pe.wait_ge(S["qk_ready"], 1)
                for h in range(8):
                    for t in range(2):
                        nc.tensor.transpose(ps[:, h // 2, (h % 2) * 256 + t * P:(h % 2) * 256 + (t + 1) * P],
                                            att["q"][:, t, h * P:(h + 1) * P], ident)
                for g in range(2):
                    for t in range(4):
                        ins = nc.tensor.transpose(ps[:, 4 + g, t * P:(t + 1) * P], att["kv"][:, t, g * P:(g + 1) * P], ident)
                ins.then_inc(S["qkT_ps"], 1)
                pe.wait_ge(S["qkT_ready"], 2)

                def scores(i):
                    h, t = divmod(i, 2)
                    if i >= 2:
                        pe.wait_ge(S["exp_ready"], i - 1)
                    mm(ps[:, i % 2, :], att["qT"][:, h, t * P:(t + 1) * P], att["kT"][:, h // 4, :],
                       start=True, stop=True).then_inc(S["s_ps"], 1)

                scores(0)
                for i in range(16):
                    h, t = divmod(i, 2)
                    if i < 15:
                        scores(i + 1)
                    pe.wait_ge(S["p_ready"], i + 1)
                    if i >= 2:
                        pe.wait_ge(S["pT_ready"], i - 1)
                    for k in range(4):
                        ins = nc.tensor.transpose(ps[:, 2 + i % 2, k * P:(k + 1) * P], att["P"][:, i % 2, k * P:(k + 1) * P], ident)
                    ins.then_inc(S["pT_ps"], 1)
                    if t == 1:
                        pe.wait_ge(S["pT_ready"], i + 1)
                        if h >= 2:
                            pe.wait_ge(S["o_ready"], h - 1)
                        v0 = 256 + (h // 4) * P
                        for k in range(4):
                            ins = mm(ps[:, 4 + h % 2, 0:256], att["kv"][:, k, v0:v0 + P], att["PT"][:, h % 2, k, :],
                                     start=k == 0, stop=k == 3)
                        ins.then_inc(S["o_ps"], 1)
                pe.wait_ge(S["o_ready"], 8)

            def qk_transposes(pr, columns):
                for k, at in enumerate(columns):
                    for t in range(2):
                        ins = nc.tensor.transpose(ps[:, k // 2, (k % 2) * 256 + t * P:(k % 2) * 256 + (t + 1) * P],
                                                  pr[:, t, at:at + P], ident)
                    if k % 8 == 7:
                        ins.then_inc(S["qkT_ps"], 1)

            def key_major(bank, qT, kT, head):
                r = slice(64 * (head % 2), 64 * (head % 2) + 64)
                c = head // 2
                mm(ps[:, bank, 0:256], kT[r, c, 0:P], qT[r, c, 0:256], start=True, stop=True)
                return mm(ps[:, bank, 256:384], kT[r, c, P:256], qT[r, c, P:256], start=True, stop=True)

            def hybrid():
                pr = proj_dst(7)
                pe.wait_ge(S["qk_ready"], 2)
                qk_transposes(pr, [P * k for k in range(8)] + [2048 + P * k for k in range(8)])
                pe.wait_ge(S["qkT_ready"], 4)
                rq, rk, dq, dk = (hyb["qkT"][:, 4 * k:4 * k + 4, :] for k in range(4))

                def ret_scores(h):
                    if h >= 2:
                        pe.wait_ge(S["ret_s_ready"], h - 1)
                    key_major(h % 2, rq, rk, h).then_inc(S["ret_s_ps"], 1)

                ret_scores(0)
                for h in range(8):
                    if h < 7:
                        ret_scores(h + 1)
                    pe.wait_ge(S["ret_s_ready"], h + 1)
                    St = hyb["St"][:, h % 2, :]
                    c = slice(64 * h, 64 * h + 64)
                    v = slice(1024 + 64 * h, 1024 + 64 * h + 64)
                    mm(ps[:, 6, c], St[:, 0:P], pr[:, 0, v], start=True, stop=True)
                    mm(ps[:, 7, c], St[:, P:256], pr[:, 0, v], start=True, stop=False)
                    mm(ps[:, 7, c], St[:, 256:384], pr[:, 1, v], start=False, stop=True).then_inc(S["ret_o_ps"], 1)
                pe.wait_ge(S["ret_ready"], 2)
                for k in range(4):
                    for t in range(2):
                        ins = nc.tensor.transpose(ps[:, 4 + k // 2, (k % 2) * 256 + t * P:(k % 2) * 256 + (t + 1) * P],
                                                  hyb["ret"][:, t, k * P:(k + 1) * P], ident)
                ins.then_inc(S["retT_ps"], 1)
                pe.wait_ge(S["o_ready"], 9)

                def scores(i):
                    h, t = divmod(i, 2)
                    r = slice(64 * (h % 2), 64 * (h % 2) + 64)
                    if i >= 2:
                        pe.wait_ge(S["max_ready"], 16 + i - 1)
                    mm(ps[:, i % 2, 0:P * (t + 1)], dq[r, h // 2, t * P:(t + 1) * P], dk[r, h // 2, 0:P * (t + 1)],
                       start=True, stop=True).then_inc(S["s_ps"], 1)

                scores(0)
                for i in range(16):
                    h, t = divmod(i, 2)
                    if i < 15:
                        scores(i + 1)
                    pe.wait_ge(S["p_ready"], 16 + i + 1)
                    if i >= 2:
                        pe.wait_ge(S["pT_ready"], 16 + i - 1)
                    for k in range(t + 1):
                        ins = nc.tensor.transpose(ps[:, 2 + i % 2, k * P:(k + 1) * P], hyb["P"][:, i % 2, k * P:(k + 1) * P], ident)
                    ins.then_inc(S["pT_ps"], 1)
                    if t == 1:
                        pe.wait_ge(S["pT_ready"], 16 + i + 1)
                        if h >= 2:
                            pe.wait_ge(S["o_ready"], 9 + h - 1)
                        r = slice(64 * (h % 2), 64 * (h % 2) + 64)
                        v = slice(3072 + 64 * h, 3072 + 64 * h + 64)
                        mm(ps[r, 4 + h % 2, 0:256], pr[:, 0, v], hyb["PT"][:, h % 2, 0, :], start=True, stop=False)
                        mm(ps[r, 4 + h % 2, P:256], pr[:, 1, v], hyb["PT"][:, h % 2, 1, P:256], start=False, stop=True
                           ).then_inc(S["o_ps"], 1)
                pe.wait_ge(S["o_ready"], 17)

            def stick_breaking():
                pr = proj_dst(10)
                qk_transposes(pr, [P * k for k in range(16)])
                pe.wait_ge(S["qkT_ready"], 6)
                qT, kT = sbk["qkT"][:, 0:8, :], sbk["qkT"][:, 8:16, :]
                tri = T["tri"]

                def scores(g):
                    if g >= 2:
                        pe.wait_ge(S["stay_ready"], g - 1)
                    for h in range(2):
                        ins = key_major(2 * (g % 2) + h, qT, kT, 2 * g + h)
                    ins.then_inc(S["z_ps"], 1)

                scores(0)
                for g in range(8):
                    if g < 7:
                        scores(g + 1)
                    pe.wait_ge(S["stay_ready"], g + 1)
                    ST, A_ = sbk["ST"][:, g % 2], sbk["A"][:, g % 2]
                    if g:
                        pe.wait_ge(S["arg_ready"], g)
                    for h in range(2):
                        mm(ps[:, 6 + h, 0:256], tri, ST[:, h, 0:256], start=True, stop=False)
                        mm(ps[:, 6 + h, P:256], ones, ST[:, h, 256:384], start=False, stop=True)
                        ins = mm(ps[:, 6 + h, 256:384], tri, ST[:, h, 256:384], start=True, stop=True)
                    ins.then_inc(S["later_ps"], 1)
                    pe.wait_ge(S["a_ready"], g + 1)
                    if g >= 2:
                        pe.wait_ge(S["o_ready"], 17 + g - 1)
                    for h in range(2):
                        r = slice(64 * h, 64 * h + 64)
                        v = slice(2048 + 64 * (2 * g + h), 2048 + 64 * (2 * g + h) + 64)
                        mm(ps[r, 4 + g % 2, 0:256], pr[:, 0, v], A_[:, h, 0:256], start=True, stop=False)
                        ins = mm(ps[r, 4 + g % 2, P:256], pr[:, 1, v], A_[:, h, 256:384], start=False, stop=True)
                    ins.then_inc(S["o_ps"], 1)
                pe.wait_ge(S["o_ready"], 25)

            def unit_wait(n0, q):
                pe.wait_ge(lo_ready, n0 + 1 + RING * q)

            pe.wait_ge(S["cvec_ready"], 2)
            pe.wait_ge(loads["consts"], 16)
            for ph in phases:
                s = ph.stage
                N = tokens(s)

                def before_chunk(ch, x):
                    if not isinstance(ch, int) or ch > 0:
                        pe.wait_ge(S["modrow_ready"], ch)

                if ph.kind == "mod":
                    def visit(kind, x, idx, n0, q, i):
                        ch = x // 4 + i
                        unit_wait(n0, q)
                        if x % 4 == 0:
                            before_chunk(ch, x)
                        mod_unit(n0, x % 4)
                        if x % 4 == 3:
                            mod_column(ch)
                    walk(pe, ph, visit)
                    pe.wait_ge(loads["x"], 32)
                    pe.wait_ge(S["coef_ready"], 1)
                    for t in range(4):
                        transposes(X[:, t, :], t)
                elif ph.kind in ("ffn_in", "u"):
                    pending = []
                    base = tiles_before[s]
                    pe.wait_ge(S["x_ready"], tiles_ready(s))

                    def visit(kind, x, idx, n0, q, i):
                        unit_wait(n0, q)
                        if kind == "M":
                            ch = x // 4 + i
                            if x % 4 == 0:
                                before_chunk(ch, x)
                            mod_unit(n0, x % 4)
                            if x % 4 == 3:
                                pending.append(ch)
                            return
                        if kind in "GF":
                            if not isinstance(q, int) or base + idx > 1:
                                pe.wait_ge(S["gate_ready"], base + idx - 1)
                            feature_unit(n0, x % 2, N)
                        else:
                            hb = hid_before[s]
                            if not isinstance(q, int) or hb + idx > 1:
                                pe.wait_ge(S["hid_ready"], hb + idx - 1)
                            feature_unit(n0, 2 + x % 2, N)
                        if pending:
                            mod_column(pending.pop())
                    walk(pe, ph, visit)
                    if s in mods_by:
                        pe.wait_ge(S["modcol_ready"], mods_by[s])
                    if ph.kind == "u":
                        mix(LAT)
                elif ph.kind in ("v", "proj"):
                    base = groups_before[ph.first]
                    pe.wait_ge(S["x_ready"], tiles_ready(s))
                    if ph.kind == "v" and ph.more["vec"] == LAT:
                        pe.wait_ge(loads["gmlp"], 16 * 9)
                        for i in range(4):
                            ins = mm(ps[32 * i:32 * i + 1, 7, 0:256], ones[:, 0:1], wsT[:, 256 * i:256 * i + 256],
                                     start=True, stop=True)
                        ins.then_inc(S["rs_ps"], 1)

                    def visit(kind, x, idx, n0, q, i):
                        g = x // 4
                        unit_wait(n0, q)
                        if STAGES[s] == ATTN:
                            tiles, banks = [([0, 1], [0, 1]), ([0, 1], [2, 3]), (range(4), range(4, 8))][g]
                        else:
                            t0 = 2 * ph.more.get("vec", 0)
                            tiles, banks = [t0, t0 + 1], [2 * (g % 2), 2 * (g % 2) + 1]
                            if x % 4 == 0 and (not isinstance(q, int) or base + g > 1):
                                pe.wait_ge(S["proj_ready"], base + g - 1 + q)
                        token_unit(n0, x % 4, tiles, banks)
                    walk(pe, ph, visit)
                    if ph.kind == "v" and ph.more["vec"] == CTX:
                        mix(CTX)
                    if STAGES[s] == ATTN:
                        attention()
                    elif STAGES[s] == HYB:
                        hybrid()
                    elif STAGES[s] == SB:
                        pe.wait_ge(S["proj_ready"], base + 6)
                        stick_breaking()
                elif ph.kind == "out":
                    if STAGES[s] == FFN:
                        pe.wait_ge(S["hid_ready"], hid_before[s] + FT)
                    elif STAGES[s] == GMLP:
                        pe.wait_ge(S["mix_done"], 2 * GT)
                    if s < N_MODULATED:
                        gates(s)

                    def visit(kind, x, idx, n0, q, i):
                        unit_wait(n0, q)
                        pe.wait_ge(S["hs_lo"], hs_before[s] + idx + 1)
                        for t in range(TILES[s]):
                            ins = out_products(s, n0, x, t, False)
                        ins.then_inc(unit_used, 1)
                    walk(pe, ph, visit)
                elif ph.kind == "tail":
                    out_tail(s, ph.first)


def constants():
    import numpy as np

    f4 = np.float32
    consts = np.zeros((P, 264), f4)
    consts[:, 0:P] = np.eye(P)
    consts[:, P:2 * P] = 1.0
    consts[[0, 32], 2 * P] = 1.0
    consts[[64, 96], 2 * P + 1] = 1.0
    consts[:, 260], consts[:, 261] = RMS_EPS, LN_EPS
    pos = np.arange(256)

    def rope(angle):
        both = np.stack([np.cos(angle), np.sin(angle)]).astype(f4)
        return both.reshape(2, 2, P, -1).transpose(2, 0, 1, 3).reshape(P, -1)

    quarter = 32
    freqs = (f4(10000.0) ** (-np.arange(quarter, dtype=f4) / f4(quarter))).astype(f4)
    grid = np.concatenate([(pos // 64).astype(f4)[:, None] * freqs, (pos % 64).astype(f4)[:, None] * freqs], 1)

    def plain(half, theta):
        inv = (f4(1.0) / (f4(theta) ** (np.arange(half, dtype=f4) / f4(half)))).astype(f4)
        return pos.astype(f4)[:, None] * inv[None, :]

    i, j = np.arange(P)[:, None], np.arange(256)[None, :]
    dist = i + P - j
    count = ((dist >= 0) & (dist <= 128)).astype(f4)
    count += (dist >= 0) & (dist % 4 == 0)
    count += (dist >= 0) & (dist % 16 == 0)
    mask = np.where(count > 0, 0.0, -1e30).astype(f4)
    key, query = np.arange(P)[:, None], np.arange(P)[None, :]
    causal = (key < query).astype(f4)
    tri = (key > query).astype(f4)
    tables = np.concatenate([rope(plain(32, 10000.0)), rope(plain(8, 500000.0)), mask, count, causal, tri], 1)
    lag = np.arange(256)[None, :] - np.arange(P)[:, None]
    log_g = np.log(1.0 - 2.0 ** (-5.0 - np.arange(8)))
    decay = np.where(lag >= 0, np.exp(np.maximum(lag, 0)[None] * log_g[:, None, None]), 0.0) * 0.125
    return dict(consts=consts, att_rope=rope(grid), tables=tables.astype(f4),
                decay=np.ascontiguousarray(decay.transpose(1, 0, 2)).astype(f4))


def kernel(**inputs):
    import numpy as np
    import concourse.bacc as bacc
    from concourse.bass_utils import run_bass_kernel_spmd

    g = {k: np.asarray(v) for k, v in inputs.items()}

    def feature_units(w, n):
        return w.reshape(DC, P, n, P).transpose(2, 1, 0, 3).reshape(n, P, UNIT)

    def token_units(w):
        n = w.shape[1] // 512
        return w.reshape(4, 2, P, n, 512).transpose(3, 0, 2, 1, 4).reshape(4 * n, P, UNIT)

    def out_units(w):
        return w.reshape(-1, P, UNIT)

    def column(v):
        return v.reshape(-1, P).T

    ffns = [(g["ffn_w_in"][l, i], g["ffn_w_out"][l, i]) for l in range(2) for i in range(2)]
    ffns += [(g[f"ffn{i}_w_in_2"][l], g[f"ffn{i}_w_out_2"][l]) for l in range(2) for i in (1, 2)]
    arrays = constants()
    for i, (w_in, w_out) in enumerate(ffns):
        arrays[f"ffn_gate{i}"] = feature_units(w_in[:, :FF], FT)
        arrays[f"ffn_up{i}"] = feature_units(w_in[:, FF:], FT)
        arrays[f"ffn_out{i}"] = out_units(w_out)
    arrays.update(
        w_mod=np.concatenate([token_units(w) for w in g["w_mod"]]),
        gmlp_u=feature_units(g["gmlp_w_in"][0][:, :3 * D], GT),
        gmlp_v=token_units(g["gmlp_w_in"][0][:, 3 * D:]),
        gmlp_out=out_units(g["gmlp_w_out"][0]),
        attn_in=token_units(g["attn_w_qkv"][0]), attn_out=out_units(g["attn_w_o"][0]),
        hyb_in=token_units(g["hyb_w_in_2"][0]), hyb_out=out_units(g["hyb_w_out_2"][0]),
        sb_in=token_units(g["sb_w_in_2"][0]), sb_out=out_units(g["sb_w_out_2"][0]),
        x=g["x"][0].reshape(2, P, D).transpose(1, 0, 2), ctx=g["ctx"][0].reshape(2, P, D).transpose(1, 0, 2),
        wsT=g["gmlp_w_s"][0].transpose(2, 0, 1).reshape(P, GROUPS * P),
        gmlp_ln_b=g["gmlp_ln_b"].reshape(4, 768), gmlp_b_s=g["gmlp_b_s"].reshape(4, 256),
        q_norm=g["attn_q_norm"].reshape(1, P), k_norm=g["attn_k_norm"].reshape(1, P),
        ln_g=g["ln_g"].reshape(6, D), ln_b=g["ln_b"].reshape(6, D),
        ret_gn=g["ret_gn_2"].reshape(1, 512),
        norm_rows=np.stack([g[n][l] for l in range(2) for n in ("ffn1_norm_2", "mix_norm_2", "ffn2_norm_2")]
                           + [g["final_norm_2"]]),
        cols=np.concatenate([
            np.stack([column(g["c"]), column(g["c_ctx"])], -1).reshape(P, 2 * DC),
            column(g["b_mod"]), column(g["ln_g"]), column(g["ln_b"]), column(g["gmlp_ln_g"])], 1),
    )
    nc = bacc.Bacc("TRN2", target_bir_lowering=False, num_devices=1)
    feed, aps = {}, {}
    for name, v in arrays.items():
        feed["in_" + name] = np.ascontiguousarray(v)
        aps[name] = nc.dram_tensor("in_" + name, v.shape, mybir.dt.from_np(v.dtype), kind="ExternalInput").ap()
    for part in ("gate", "up", "out"):
        aps["ffn_" + part] = [aps[f"ffn_{part}{i}"] for i in range(len(ffns))]
    result = nc.dram_tensor("out_dram", (2, P, D), mybir.dt.float32, kind="ExternalOutput").ap()
    aps["out"] = result.rearrange("t p n -> p t n")
    fused_blocks(nc, aps)
    r = run_bass_kernel_spmd(nc, [feed], core_ids=[0])
    return r.results[0]["out_dram"].reshape(1, 256, D)
```

```python
import concourse.bass as bass
from concourse import mybir
from contextlib import ExitStack

D = 1024
P = 128
DC = D // P
TOK = 512
FF = 2816
FT = FF // P
GT = 3 * D // P
GROUPS = 8
ALPHA = 4.0 ** 0.25
LN_EPS = 1e-5
RMS_EPS = 1e-6
RING = 4
AHEAD = 3
UNIT = 1024
LAT, CTX = 0, 1

FFN, GMLP, ATTN, HYB, SB = "ffn", "gmlp", "attn", "hyb", "sb"
STAGES = [FFN, GMLP, FFN, FFN, ATTN, FFN, FFN, HYB, FFN, FFN, SB, FFN]
N_MODULATED = 6
TILES = [4, 4, 4, 4] + [2] * 8
OUT_K = [{FFN: FT, GMLP: GT}.get(s, DC) for s in STAGES]
DIL_PAIRS = 4
SCORE_BANKS = (0, 1, 6, 7)
PROJ_GROUPS = {ATTN: 3, HYB: 7, SB: 6}


class Phase:

    def __init__(self, kind, stage, first, rounds, **more):
        self.kind, self.stage, self.first, self.rounds = kind, stage, first, rounds
        self.units = sum(trips * len(body) for trips, body in rounds)
        self.more = more


def tiles_ready(s):
    return 4 + sum(TILES[:s])


def plan():
    phases, at = [], 0

    def add(kind, stage, rounds, **more):
        nonlocal at
        phases.append(Phase(kind, stage, at, rounds, **more))
        at += phases[-1].units

    def chunk(a, b):
        return [("M", 4 * a + q, 4 * b) for q in range(4)]

    def shifted(body, by):
        return [(k, a + by * b, b) for k, a, b in body]

    def proj(groups, first_peeled):
        body = [("B", u, 8) for u in range(8)]
        rounds = [(1, body), (groups // 2 - 1, shifted(body, 1))] if first_peeled else [(groups // 2, body)]
        if groups % 2:
            rounds.append((1, [("B", 4 * (groups - 1) + q, 0) for q in range(4)]))
        return rounds

    def out(k):
        rounds = [(1, [("O", j, 0) for j in range(4)])]
        turns = max(0, (k - 8) // 4)
        if turns:
            rounds.append((turns, [("O", 4 + j, 4) for j in range(4)]))
        middle = [("O", j, 0) for j in range(4 + 4 * turns, k - RING)]
        return rounds + ([(1, middle)] if middle else [])

    add("mod", -1, [(1, chunk(0, 0)), (3, chunk(1, 1))])
    chunks = 4
    for s, kind in enumerate(STAGES):
        if kind == FFN:
            mods = {0: 10, 2: 10, 3: 6}.get(s, 0)
            m = chunk(chunks, 1)
            mixed = m[:2] + [("G", 0, 2), ("U", 0, 2)] + m[2:] + [("G", 1, 2), ("U", 1, 2)]
            rounds = []
            if mods and s == 0:
                rounds = [(1, mixed), (mods - 1, shifted(mixed, 1))]
            elif mods:
                rounds = [(mods, mixed)]
            rest = FT // 2 - mods
            rounds.append((rest, [("G", 2 * mods, 2), ("U", 2 * mods, 2), ("G", 2 * mods + 1, 2), ("U", 2 * mods + 1, 2)]))
            add("ffn_in", s, rounds)
            chunks += mods
        elif kind == GMLP:
            add("v", s, proj(GT // 4, True), vec=LAT)
            m = chunk(chunks, 1)
            body = m[:2] + [("F", 0, 4), ("F", 1, 4)] + m[2:] + [("F", 2, 4), ("F", 3, 4)]
            add("u", s, [(GT // 4, body)])
            chunks += GT // 4
            add("v", s, proj(GT // 4, False), vec=CTX)
        else:
            groups = PROJ_GROUPS[kind]
            if kind == ATTN:
                add("proj", s, [(1, [("B", u, 0) for u in range(4 * groups)])])
            elif kind == HYB:
                body = [("B", u, 8) for u in range(8)]
                last = [("B", u, 0) for u in range(16, 4 * groups)]
                add("proj", s, [(2, body), (1, last)])
            else:
                add("proj", s, proj(groups, False))
        add("out", s, out(OUT_K[s]))
        add("tail", s, [(1, [("O", j, 0) for j in range(OUT_K[s] - RING, OUT_K[s])])])
    return phases, at


def fused_blocks(nc, a):
    f32, f32r = mybir.dt.float32, mybir.dt.float32r
    ALU, ACT, AX = mybir.AluOpType, mybir.ActivationFunctionType, mybir.AxisListType
    MUL, ADD, SUB = ALU.mult, ALU.add, ALU.subtract
    phases, n_units = plan()

    with ExitStack() as ctx:
        def sb(name, shape, dt=f32):
            return ctx.enter_context(nc.sbuf_tensor(name, shape, dt))

        def sem(name):
            return ctx.enter_context(nc.semaphore(name))

        w32 = sb("w32", [P, RING, UNIT])
        whi = sb("whi", [P, RING, UNIT], f32r)
        wlo = sb("wlo", [P, RING, UNIT], f32r)
        xhi = sb("xhi", [P, DC, TOK], f32r)
        xlo = sb("xlo", [P, DC, TOK], f32r)
        hid = sb("hid", [P, GT, TOK])
        hs = sb("hs", [P, RING, 2, TOK], f32r)
        X = sb("X", [P, 4, D])
        arena = sb("arena", [P, 6144])
        side = sb("side", [P, 2048])
        cvec = sb("cvec", [P, DC, P], f32r)
        modrow = sb("modrow", [P, 512])
        modcol = sb("modcol", [P, 2 * 9 * DC * 2])
        cols = sb("cols", [P, a["cols"].shape[1]])
        consts = sb("consts", [P, a["consts"].shape[1]])
        coef = sb("coef", [P, 4, DC, 2])
        csil = sb("csil", [P, DC, 2])
        bnst = sb("bnst", [P, 4, 6, 6])
        mv = sb("mv", [P, 4, 2])
        std = sb("std", [P, 64])
        rstd = sb("rstd", [P, 64])
        stat = sb("stat", [P, 64])
        mx = sb("mx", [P, 16])
        den = sb("den", [P, 16])
        rden = sb("rden", [P, 16])
        ps = ctx.enter_context(nc.psum_tensor("ps", [P, 8, 512], f32))

        hidf = hid[:, :, :].rearrange("p c n -> p (c n)")
        Xf = X[:, :, :].rearrange("p t n -> p (t n)")
        ident, ones, sel = consts[:, 0:P], consts[:, P:2 * P], consts[:, 2 * P:2 * P + 2]

        def col(name, per):
            at = {"c": 0, "b_mod": 16, "ln_g": 160, "ln_b": 208, "gmlp_g": 256}[name]
            return cols[:, at:at + per]

        c_col = col("c", 16).rearrange("p (c v) -> p c v", v=2)
        bmod = col("b_mod", 144)
        lng = col("ln_g", 48).rearrange("p (s c) -> p s c", c=DC)
        lnb = col("ln_b", 48).rearrange("p (s c) -> p s c", c=DC)
        gmg = col("gmlp_g", GT)
        gate_row = arena[:, 0:2 * D].rearrange("p (v n) -> p v n", v=2)
        g_row, b_row = arena[:, 2 * D:3 * D], arena[:, 3 * D:4 * D]
        diag = arena[:, 4 * D:5 * D]
        full = arena[:, 4 * D:6 * D].rearrange("p (b n) -> p b n", b=2)
        next_gain = arena[:, 4 * D:5 * D]
        normed = [arena[:, D:2 * D], arena[:, 0:D]]
        v_tok = arena[:, :].rearrange("p (t n) -> p t n", t=2)
        wsT = side[:, 0:GROUPS * P]
        lnb_row, sum_row = side[:, 1024:1792], side[:, 1792:2048]

        mixbuf = modrow[:, :].rearrange("p (b n) -> p b n", b=2)

        def modv(layer, v):
            at = (layer * 9 + v) * DC * 2
            return modcol[:, at:at + DC * 2].rearrange("p (c v) -> p c v", v=2)

        landed = [sem(f"unit_landed{i}") for i in range(RING)]
        hi_ready, lo_ready, unit_used = sem("hi_ready"), sem("lo_ready"), sem("unit_used")
        names = """gate_ready hid_ready proj_ready vstat_ready modrow_ready modcol_ps modcol_ready
            hs_hi hs_lo y_ready diag_ready gate_ps gate_row_ready dve_step act_step pool_step
            var_ready std_ready norm_ready xT_ps full_ready x_ready xres_ready coef_ready
            mix_ps mix_scaled mix_step mix_done v_normed rs_ps rs_ready value_ready qk_ready qkT_ps qkT_ready
            s_ps max_ready exp_ready p_ready pT_ps pT_ready o_ps o_ready
            ret_s_ps ret_s_ready ret_o_ps ret_ready silu_rg retT_ps
            z_ps negabs_ready log_ready stay_ready later_ps arg_ready a_exp a_ready ss_ready
            csil_ready cvec_ready out_ready""".split()
        S = {n: sem(n) for n in names}
        loads = {n: sem("loaded_" + n) for n in ("x", "consts", "cols", "gmlp", "rows", "attn", "hyb", "decay", "gain")}
        stored = sem("stored")

        class Tally:

            def __init__(self):
                self.n = {}

            def __call__(self, name, k=1):
                self.n[name] = self.n.get(name, 0) + k
                return self.n[name]

        class Chain:

            def __init__(self, eng, ended):
                self.eng, self.ended, self.n = eng, ended, 0

            def give(self, ins):
                self.n += 1
                ins.then_inc(self.ended, 1)

            def wait(self):
                self.eng.wait_ge(self.ended, self.n)

            def __call__(self, ins):
                self.give(ins)
                self.wait()

        def walk(eng, phase, visit):
            n0 = phase.first
            for trips, body in phase.rounds:
                def once(i):
                    for off, (kind, x, b) in enumerate(body):
                        visit(kind, x, x + b * i, n0 + off, i * (len(body) // RING), i)
                if trips == 1:
                    once(0)
                else:
                    assert len(body) % RING == 0
                    with eng.Fori(0, trips) as i:
                        once(i)
                n0 += trips * len(body)

        tiles_before, hs_before, groups_before = {}, {}, {}
        n_tiles = n_hs = n_groups = 0
        for p_ in phases:
            if p_.kind in ("ffn_in", "u"):
                tiles_before[p_.stage] = n_tiles
                n_tiles += FT if p_.kind == "ffn_in" else GT
            if p_.kind == "out":
                hs_before[p_.stage] = n_hs
                n_hs += OUT_K[p_.stage]
            if p_.kind in ("v", "proj"):
                groups_before[p_.first] = n_groups
                n_groups += GT // 4 if p_.kind == "v" else PROJ_GROUPS[STAGES[p_.stage]]
        mods_by, n_mods = {}, 0
        for p_ in phases:
            here = sum(trips * sum(k == "M" for k, _, _ in body) for trips, body in p_.rounds) // 4
            n_mods += here
            if here:
                mods_by[p_.stage] = n_mods
        hid_before, n_hid = {}, 0
        for s, kind in enumerate(STAGES):
            hid_before[s] = n_hid
            if kind == FFN:
                n_hid += FT

        o_before = {ATTN: 0, HYB: 8, SB: 8 + DIL_PAIRS}
        o_made = {ATTN: 8, HYB: 9 + DIL_PAIRS, SB: 17 + DIL_PAIRS}

        def tokens(s):
            return TILES[s] * P

        def proj_dst(s):
            w = {HYB: 3584, SB: 3072}[STAGES[s]]
            return hidf[:, 0:2 * w].rearrange("p (t n) -> p t n", t=2)

        att = dict(
            q=Xf[:, 2048:4096].rearrange("p (t n) -> p t n", t=2),
            k=hidf[:, 0:1024].rearrange("p (t n) -> p t n", t=4),
            v=hidf[:, 1024:2048].rearrange("p (t n) -> p t n", t=4),
            qT=hidf[:, 2048:4096].rearrange("p (h n) -> p h n", h=8),
            kT=hidf[:, 4096:5120].rearrange("p (h n) -> p h n", h=2),
            P=hidf[:, 10240:12288].rearrange("p (b n) -> p b n", b=4),
            PT=hidf[:, 6144:8192].rearrange("p (b k n) -> p b k n", b=2, k=4),
            oT=hidf[:, 8192:10240].rearrange("p (c n) -> p c n", c=8),
            tmp=hidf[:, 10240:12288],
        )
        HW_ = 3584
        hyb = dict(
            qkT=hidf[:, 7168:11264].rearrange("p (c n) -> p c n", c=16),
            P=[hidf[:, 11264:11776], hidf[:, 11776:12288], arena[:, 4864:5376]],
            oT=arena[:, 0:2048].rearrange("p (c n) -> p c n", c=8),
            tmp=arena[:, 2048:4096],
            PT=arena[:, 2048:4096].rearrange("p (b k n) -> p b k n", b=2, k=4),
            St=arena[:, 4096:4864].rearrange("p (b n) -> p b n", b=2),
            gn=arena[:, 5376:5888],
            decay=Xf[:, 2048:4096].rearrange("p (h n) -> p h n", h=8),
            ret=hidf[:, 0:HW_ * 2].rearrange("p (t n) -> p t n", t=2)[:, :, 0:512],
            sq=hidf[:, 0:HW_ * 2].rearrange("p (t n) -> p t n", t=2)[:, :, 512:1024],
        )
        sbk = dict(
            qkT=hidf[:, 6144:10240].rearrange("p (c n) -> p c n", c=16),
            oT=hidf[:, 10240:12288].rearrange("p (c n) -> p c n", c=8),
            E=arena[:, 0:1536].rearrange("p (b h n) -> p b h n", b=2, h=2),
            LS=arena[:, 1536:3072].rearrange("p (b h n) -> p b h n", b=2, h=2),
            ST=arena[:, 3072:4608].rearrange("p (b h n) -> p b h n", b=2, h=2),
            A=arena[:, 4608:6144].rearrange("p (b h n) -> p b h n", b=2, h=2),
        )
        T = dict(att_rope=side[:, 0:256].rearrange("p (k t n) -> p k t n", k=2, t=2),
                 qk_gain=side[:, 256:512].rearrange("p (k n) -> p k n", k=2),
                 ret_rope=side[:, 512:640].rearrange("p (k t n) -> p k t n", k=2, t=2),
                 dil_rope=side[:, 640:672].rearrange("p (k t n) -> p k t n", k=2, t=2),
                 bias=side[:, 672:928], causal=side[:, 928:1056], tri=side[:, 1056:1184])

        def out_source(s):
            return {ATTN: att["oT"], HYB: hyb["oT"], SB: sbk["oT"]}.get(STAGES[s])

        block = ctx.enter_context(nc.Block())

        @block.sync
        def _(sp):
            def load(kind, x, idx, n0, q, i):
                src = sources[kind]
                if n0 >= RING or not isinstance(q, int):
                    sp.wait_ge(S_lo, n0 - RING + 1 + RING * q)
                sp.dma_start(w32[:, n0 % RING, :],
                             src[bass.ds(idx, 1), :, :].rearrange("o p n -> p (o n)")
                             ).then_inc(landed[n0 % RING], 16)

            S_lo = lo_ready
            ffn = 0
            for ph in phases:
                s = ph.stage
                sources = {"M": a["w_mod"]}
                if ph.kind == "ffn_in":
                    sources["G"], sources["U"] = a["ffn_gate"][ffn], a["ffn_up"][ffn]
                elif ph.kind == "u":
                    sources["F"] = a["gmlp_u"]
                elif ph.kind == "v":
                    sources["B"] = a["gmlp_v"]
                elif ph.kind == "proj":
                    sources["B"] = a[STAGES[s] + "_in"]
                elif ph.kind in ("out", "tail"):
                    sources["O"] = a["ffn_out"][ffn] if STAGES[s] == FFN else a[STAGES[s] + "_out"]
                    ffn += ph.kind == "tail" and STAGES[s] == FFN
                walk(sp, ph, load)

        @block.gpsimd
        def _(pool):
            chain = Chain(pool, S["pool_step"])
            pool.dma_start(consts[:, :], a["consts"]).then_inc(loads["consts"], 16)
            pool.dma_start(cols[:, :], a["cols"]).then_inc(loads["cols"], 16)
            pool.dma_start(X[:, 0:2, :], a["x"]).then_inc(loads["x"], 16)
            pool.dma_start(X[:, 2:4, :], a["ctx"]).then_inc(loads["x"], 16)
            pool.dma_start(wsT, a["wsT"]).then_inc(loads["gmlp"], 16)
            chain(nc.gpsimd.memset(side[:, 1024:2048], 1.0))
            for i in range(4):
                pool.dma_start(lnb_row[32 * i:32 * i + 1, :], a["gmlp_ln_b"][i:i + 1, :]).then_inc(loads["gmlp"], 16)
                pool.dma_start(sum_row[32 * i + 1:32 * i + 2, :], a["gmlp_b_s"][i:i + 1, :]).then_inc(loads["gmlp"], 16)
            done = Tally()
            for s in range(N_MODULATED):
                pool.wait_ge(S["gate_row_ready"], done("gate_row", 2 if TILES[s] == 4 else 1))
                if s == 1:
                    pool.wait_ge(S["mix_done"], 2 * GT)
                    pool.dma_start(side[:, 0:256], a["att_rope"]).then_inc(loads["attn"], 16)
                    for k, g in enumerate(("q_norm", "k_norm")):
                        pool.dma_start(T["qk_gain"][:, k, :], a[g].to_broadcast((P, P))).then_inc(loads["attn"], 16)
                    pool.dma_start(side[:, 512:1184], a["tables"]).then_inc(loads["hyb"], 16)
                pool.dma_start(g_row, a["ln_g"][s:s + 1, :].to_broadcast((P, D))).then_inc(loads["rows"], 16)
                pool.dma_start(b_row, a["ln_b"][s:s + 1, :].to_broadcast((P, D))).then_inc(loads["rows"], 16)
                if s == 5:
                    continue
                pool.wait_ge(loads["rows"], 32 * (s + 1))
                for t in range(4 if s < 3 else 2):
                    pool.wait_ge(S["xT_ps"], tiles_ready(s) + t + 1)
                    chain(nc.gpsimd.tensor_tensor(X[:, t, :], X[:, t, :], g_row, MUL))
                    nc.gpsimd.tensor_tensor(X[:, t, :], X[:, t, :], b_row, ADD).then_inc(S["xres_ready"], 1)
                pool.wait_ge(S["xres_ready"], 4 * min(s + 1, 3) + 2 * max(0, s - 2))
            for s in range(5, len(STAGES)):
                if s > 5:
                    pool.wait_ge(S["norm_ready"], tiles_ready(s) - 4)
                if STAGES[s] in o_made:
                    pool.wait_ge(S["o_ready"], o_made[STAGES[s]])
                gain = a["norm_rows"][s - 5:s - 4, :]
                pool.dma_start(next_gain, gain.to_broadcast((P, D))).then_inc(loads["gain"], 16)
                if s == 5:
                    pool.wait_ge(S["norm_ready"], tiles_ready(6) - 4)
                    pool.dma_start(hyb["decay"], a["decay"]).then_inc(loads["decay"], 16)
                if s == 6:
                    pool.wait_ge(S["x_ready"], tiles_ready(7))
                    pool.dma_start(hyb["gn"], a["ret_gn"].to_broadcast((P, 512))).then_inc(loads["decay"], 16)
            for t in range(2):
                pool.wait_ge(S["out_ready"], t + 1)
                pool.dma_start(a["out"][:, t, :], X[:, t, :]).then_inc(stored, 16)
            pool.wait_ge(stored, 32)

        @block.scalar
        def _(act):
            seen = Tally()
            ident_f = ACT.Identity

            def split_hi(n0, q):
                if isinstance(q, int) and n0 >= n_units:
                    return
                act.wait_ge(landed[n0 % RING], 16 * (n0 // RING + 1) + 16 * q)
                if n0 >= RING or not isinstance(q, int):
                    act.wait_ge(unit_used, n0 - RING + 1 + RING * q)
                nc.scalar.copy(whi[:, n0 % RING, :], w32[:, n0 % RING, :]).then_inc(hi_ready, 1)

            def hs_hi(s, src, k, x):
                n = tokens(s)
                nc.scalar.copy(hs[:, x % RING, 0, 0:n], src(k)).then_inc(S["hs_hi"], 1)

            def transposed(t, modulated):
                n = seen("tile")
                act.wait_ge(S["xT_ps"], n)
                bank = ps[:, 2 * t:2 * t + 2, :].rearrange("p b (c n) -> p (b c) n", n=P)
                high = xhi[:, :, t * P:(t + 1) * P]
                if modulated:
                    if n > 2:
                        act.wait_ge(S["x_ready"], n - 2)
                    f = full[:, n % 2, :].rearrange("p (c n) -> p c n", n=P)
                    for c in range(DC):
                        ins = nc.scalar.activation(f[:, c, :], bank[:, c, :], ident_f,
                                                   scale=coef[:, 0, c, t // 2:t // 2 + 1], bias=coef[:, 1, c, t // 2:t // 2 + 1])
                    ins.then_inc(S["act_step"], 1)
                    act.wait_ge(S["act_step"], seen("act_step"))
                    nc.scalar.copy(high, f).then_inc(S["full_ready"], 1)
                else:
                    nc.scalar.copy(high, bank).then_inc(S["full_ready"], 1)

            def sqrt(dst, src, scale, eps):
                act.wait_ge(S["var_ready"], seen("var_ready"))
                nc.scalar.activation(dst, src, ACT.Sqrt, bias=eps, scale=scale).then_inc(S["std_ready"], 1)

            def gates(s):
                for v in range(2 if TILES[s] == 4 else 1):
                    act.wait_ge(S["gate_ps"], seen("gate_ps"))
                    nc.scalar.activation(gate_row[:, v, :].rearrange("p (h n) -> p h n", h=2), ps[:, 6:8, :],
                                         ACT.Copy, scale=0.5 if STAGES[s] == FFN else 1.0
                                         ).then_inc(S["gate_row_ready"], 1)

            def sum_squares(t):
                act.wait_ge(S["ss_ready"], seen("ss_ready"))
                nc.scalar.activation(normed[t], X[:, t, :], ACT.Square,
                                     accum_out=stat[:, t:t + 1]).then_inc(S["act_step"], 1)
                act.wait_ge(S["act_step"], seen("act_step"))
                nc.scalar.activation(std[:, 8 + t:9 + t], stat[:, t:t + 1], ACT.Sqrt, bias=consts[:, 260:261],
                                     scale=1.0 / D).then_inc(S["std_ready"], 1)

            def epilogue(s, first):
                n = TILES[s]
                for t in range(n):
                    if t == n - 1:
                        split_hi(first, 0)
                    if 0 < t and s < 11:
                        transposed(t - 1, s < 5)
                    if s < N_MODULATED:
                        sqrt(std[:, t:t + 1], mv[:, t, 1:2], 1.0, consts[:, 261:262])
                    if s >= 5:
                        sum_squares(t)
                if s < 11:
                    transposed(n - 1, s < 5)
                for k in range(1, AHEAD):
                    split_hi(first + k, 0)
                table = {GMLP: ACT.Gelu}.get(STAGES[min(s + 1, 11)], ACT.Silu)
                nc.scalar.activation(std[:, 63:64], consts[:, 260:261], table).then_inc(S["act_step"], 1)
                seen("act_step")

            def mix(vec):
                for c in range(GT):
                    i = GT * vec + c
                    act.wait_ge(S["mix_ps"], i + 1)
                    if i >= 2:
                        act.wait_ge(S["mix_done"], i - 1)
                    nc.scalar.activation(mixbuf[:, c % 2, :], ps[:, 4 + c % 4, 0:256], ACT.Copy,
                                         scale=gmg[:, c:c + 1]).then_inc(S["mix_scaled"], 1)

            def attention():
                for part, src in ((att["qT"].rearrange("p (b h) n -> p b (h n)", b=4), ps[:, 0:4, :]),
                                  (att["kT"], ps[:, 4:6, :])):
                    act.wait_ge(S["qkT_ps"], seen("qkT_ps"))
                    nc.scalar.copy(part, src).then_inc(S["qkT_ready"], 1)

                def exp(i):
                    act.wait_ge(S["max_ready"], i + 1)
                    if i >= 4:
                        act.wait_ge(S["pT_ps"], i - 3)
                    nc.scalar.activation(att["P"][:, i % 4, :], ps[:, SCORE_BANKS[i % 4], :], ACT.Exp, bias=mx[:, i:i + 1],
                                         scale=P ** -0.5, accum_out=den[:, i:i + 1]).then_inc(S["exp_ready"], 1)

                exp(0)
                exp(1)
                for i in range(16):
                    h, t = divmod(i, 2)
                    if i < 14:
                        exp(i + 2)
                    act.wait_ge(S["pT_ps"], i + 1)
                    if t == 0 and h >= 2:
                        act.wait_ge(S["o_ps"], h - 1)
                    nc.scalar.copy(att["PT"][:, h % 2, :, t * P:(t + 1) * P],
                                   ps[:, 2 + i % 2, :].rearrange("p (k n) -> p k n", k=4)).then_inc(S["pT_ready"], 1)
                    if t == 1:
                        act.wait_ge(S["o_ps"], h + 1)
                        nc.scalar.copy(att["oT"][:, h, :], ps[:, 4 + h % 2, 0:256]).then_inc(S["o_ready"], 1)

            def qk_transposed(dst):
                for half, bank in enumerate((4, 0)):
                    act.wait_ge(S["qkT_ps"], seen("qkT_ps"))
                    nc.scalar.copy(dst[:, 8 * half:8 * half + 8, :].rearrange("p (b h) n -> p b (h n)", b=4),
                                   ps[:, bank:bank + 4, :]).then_inc(S["qkT_ready"], 1)

            def hybrid():
                qk_transposed(hyb["qkT"])

                def exp(j):
                    g, t = divmod(j, 2)
                    act.wait_ge(S["max_ready"], 16 + j + 1)
                    n = P * (t + 1)
                    for h in range(2):
                        part, at = hyb["P"][j % 3][:, n * h:n * h + n], 2 * j + h
                        ins = nc.scalar.activation(part, part, ACT.Exp, bias=mx[:, at:at + 1], scale=0.125,
                                                   accum_out=den[:, at:at + 1])
                    ins.then_inc(S["exp_ready"], 1)

                exp(0)
                exp(1)
                for j in range(2 * DIL_PAIRS):
                    g, t = divmod(j, 2)
                    if j == 1:
                        sqrt(std[:, 0:16], stat[:, 16:32], 1.0 / 64, consts[:, 261:262])
                    if j < 2 * DIL_PAIRS - 2:
                        exp(j + 2)
                    act.wait_ge(S["pT_ps"], 16 + j + 1)
                    if t == 0 and g >= 2:
                        act.wait_ge(S["o_ps"], o_before[HYB] + g - 1)
                    dst = hyb["PT"][:, g % 2, :, P:256] if t else hyb["PT"][:, g % 2, 0:4:2, 0:P]
                    nc.scalar.copy(dst, ps[:, 4 + j % 2, 0:256 * (t + 1)].rearrange("p (k n) -> p k n", n=P)
                                   ).then_inc(S["pT_ready"], 1)
                    if t == 1:
                        if g == DIL_PAIRS - 1:
                            act.wait_ge(S["retT_ps"], 1)
                            nc.scalar.copy(hyb["oT"][:, 0:4, :].rearrange("p (b h) n -> p b (h n)", b=2), ps[:, 0:2, :]
                                           ).then_inc(S["o_ready"], 1)
                        act.wait_ge(S["o_ps"], o_before[HYB] + g + 1)
                        nc.scalar.copy(hyb["oT"][:, 4 + g, :], ps[:, 6 + g % 2, 0:256]
                                       ).then_inc(S["o_ready"], 1)

            def stick_breaking():
                qk_transposed(sbk["qkT"])

                def logs(g):
                    act.wait_ge(S["negabs_ready"], g + 1)
                    E_ = sbk["E"][:, g % 2]
                    nc.scalar.activation(E_, E_, ACT.Exp).then_inc(S["act_step"], 1)
                    act.wait_ge(S["act_step"], seen("act_step"))
                    nc.scalar.activation(E_, E_, ACT.Ln, bias=1.0).then_inc(S["log_ready"], 1)

                def output(g):
                    act.wait_ge(S["o_ps"], o_before[SB] + g + 1)
                    nc.scalar.copy(sbk["oT"][:, g, :], ps[:, 4 + g % 2, 0:256]).then_inc(S["o_ready"], 1)

                logs(0)
                for g in range(8):
                    if g < 7:
                        logs(g + 1)
                    act.wait_ge(S["arg_ready"], g + 1)
                    A_ = sbk["A"][:, g % 2]
                    nc.scalar.activation(A_, A_, ACT.Exp).then_inc(S["a_exp"], 1)
                    if g:
                        output(g - 1)
                output(7)

            act.wait_ge(loads["cols"], 16)
            nc.scalar.activation(csil[:, :, :], c_col, ACT.Silu).then_inc(S["csil_ready"], 1)
            act.wait_ge(loads["consts"], 16)
            for n in range(AHEAD):
                split_hi(n, 0)
            for ph in phases:
                s = ph.stage
                N = tokens(s)

                def mod_row(ch, n0, q):
                    act.wait_ge(unit_used, n0 + 1 + RING * q)
                    if not isinstance(ch, int) or ch > 0:
                        act.wait_ge(S["modcol_ps"], ch)
                    nc.scalar.copy(modrow[:, :], ps[:, 4, :]).then_inc(S["modrow_ready"], 1)

                if ph.kind == "mod":
                    def visit(kind, x, idx, n0, q, i):
                        split_hi(n0 + AHEAD, q)
                        if x % 4 == 3:
                            mod_row(x // 4 + i, n0, q)
                    walk(act, ph, visit)
                    for t in range(4):
                        transposed(t, True)
                elif ph.kind in ("ffn_in", "u"):
                    func = ACT.Silu if ph.kind == "ffn_in" else ACT.Gelu

                    def visit(kind, x, idx, n0, q, i):
                        split_hi(n0 + AHEAD, q)
                        if kind in "GF":
                            act.wait_ge(unit_used, n0 + 1 + RING * q)
                            nc.scalar.activation(hidf[:, bass.ds(idx * TOK, N)], ps[:, x % 2, 0:N],
                                                 func).then_inc(S["gate_ready"], 1)
                        elif kind == "M" and x % 4 == 3:
                            mod_row(x // 4 + i, n0, q)
                    walk(act, ph, visit)
                    if ph.kind == "u":
                        mix(LAT)
                elif ph.kind in ("v", "proj"):
                    kind_ = STAGES[s]
                    base = groups_before[ph.first]
                    if ph.kind == "v" and ph.more["vec"] == LAT:
                        act.wait_ge(S["xres_ready"], 4 * s)

                    def visit(kind, x, idx, n0, q, i):
                        split_hi(n0 + AHEAD, q)
                        if kind_ == ATTN and idx == 9:
                            sqrt(std[:, 0:16], stat[:, 0:16], 1.0 / P, consts[:, 260:261])
                        if kind_ == HYB and isinstance(idx, int) and idx == 22:
                            act.wait_ge(S["proj_ready"], base + 4)
                            rg = proj_dst(s)[:, :, 1536:2048]
                            nc.scalar.activation(rg, rg, ACT.Silu).then_inc(S["silu_rg"], 1)
                        if x % 4 != 3:
                            return
                        g = x // 4
                        act.wait_ge(unit_used, n0 + 1 + RING * q)
                        if kind_ == ATTN:
                            if g < 2:
                                dst, src = att["q"][:, :, 512 * g:512 * g + 512], ps[:, 2 * g:2 * g + 2, :]
                            else:
                                dst, src = att["k"], ps[:, 4:8, 0:256]
                        else:
                            b = 2 * (g % 2)
                            to = v_tok if kind_ == GMLP else proj_dst(s)
                            dst, src = to[:, :, bass.ds((idx - 3) * 128, 512)], ps[:, b:b + 2, :]
                        nc.scalar.activation(dst, src, ACT.Gelu if kind_ == GMLP else ACT.Copy
                                             ).then_inc(S["proj_ready"], 1)
                    walk(act, ph, visit)
                    if ph.kind == "v" and ph.more["vec"] == LAT:
                        act.wait_ge(S["rs_ps"], 1)
                        for i in range(4):
                            nc.scalar.copy(sum_row[32 * i:32 * i + 1, :], ps[32 * i:32 * i + 1, 7, 0:256]
                                           ).then_inc(S["rs_ready"], 1)
                    if ph.kind == "v":
                        sqrt(std[:, 0:2], mv[:, 0:2, 1], 1.0, consts[:, 261:262])
                        if ph.more["vec"] == CTX:
                            mix(CTX)
                    if kind_ == ATTN:
                        nc.scalar.copy(att["v"], ps[:, 4:8, 256:512]).then_inc(S["value_ready"], 1)
                        sqrt(std[:, 16:24], stat[:, 16:24], 1.0 / P, consts[:, 260:261])
                        attention()
                    if kind_ == HYB:
                        hybrid()
                    if kind_ == SB:
                        stick_breaking()
                elif ph.kind == "out":
                    if s < N_MODULATED:
                        gates(s)
                    K = OUT_K[s]
                    src_ap = out_source(s)
                    if STAGES[s] == FFN:
                        act.wait_ge(S["hid_ready"], hid_before[s] + FT)
                        src = lambda k: hidf[:, bass.ds(k * TOK, N)]
                    elif STAGES[s] == GMLP:
                        act.wait_ge(S["mix_done"], 2 * GT)
                        src = lambda k: hidf[:, bass.ds(k * TOK, N)]
                    else:
                        act.wait_ge(S["o_ready"], o_made[STAGES[s]])
                        src = lambda k: src_ap[:, k, :]
                    for k in range(AHEAD):
                        hs_hi(s, src, k, k)

                    def visit(kind, x, idx, n0, q, i):
                        split_hi(n0 + AHEAD, q)
                        hs_hi(s, src, idx + AHEAD, x + AHEAD)
                    walk(act, ph, visit)
                elif ph.kind == "tail":
                    k = OUT_K[s] - 1
                    split_hi(ph.first + RING - 1, 0)
                    hs_hi(s, src, k, k)
                    epilogue(s, ph.first + ph.units)

        @block.vector
        def _(dve):
            seen = Tally()
            chain = Chain(dve, S["dve_step"])
            V = nc.vector

            def split_lo(n0, q):
                if isinstance(q, int) and n0 >= n_units:
                    return
                dve.wait_ge(hi_ready, n0 + 1 + RING * q)
                V.tensor_tensor(wlo[:, n0 % RING, :], w32[:, n0 % RING, :], whi[:, n0 % RING, :], SUB
                                ).then_inc(lo_ready, 1)

            def hs_lo(s, src, k, x, count):
                n = tokens(s)
                dve.wait_ge(S["hs_hi"], count)
                V.tensor_tensor(hs[:, x % RING, 1, 0:n], src(k), hs[:, x % RING, 0, 0:n], SUB).then_inc(S["hs_lo"], 1)

            def split_x(t, modulated):
                n = seen("tile")
                dve.wait_ge(S["full_ready"], n)
                if modulated:
                    f = full[:, n % 2, :]
                else:
                    f = ps[:, 2 * t:2 * t + 2, :].rearrange("p b n -> p (b n)")
                r = slice(t * P, (t + 1) * P)
                V.tensor_tensor(xlo[:, :, r], f.rearrange("p (c n) -> p c n", n=P), xhi[:, :, r], SUB
                                ).then_inc(S["x_ready"], 1)

            def invert_std(n, at=0):
                dve.wait_ge(S["std_ready"], seen("std_ready"))
                chain(V.reciprocal(rstd[:, at:at + n], std[:, at:at + n]))

            def coefficients(s):
                layer, i = divmod(s + 1, 3)
                shift, scale = modv(layer, 3 * i), modv(layer, 3 * i + 1)
                dve.wait_ge(S["modcol_ready"], layer * 18 + 2 * (3 * i + 1) + 2)
                A_, B_ = coef[:, 0, :, :], coef[:, 1, :, :]
                if s < 0:
                    V.tensor_scalar(A_, scale, 1.0, None, ADD)
                    chain(V.tensor_copy(B_, shift))
                    return
                one = coef[:, 2, :, :]
                g = lng[:, s, :].unsqueeze(2).to_broadcast((P, DC, 2))
                b = lnb[:, s, :].unsqueeze(2).to_broadcast((P, DC, 2))
                chain(V.tensor_scalar(one, scale, 1.0, None, ADD))
                chain(V.tensor_tensor(A_, one, g, MUL))
                chain(V.tensor_tensor(B_, one, b, MUL))
                chain(V.tensor_tensor(B_, B_, shift, ADD))

            def gates(s):
                layer, i = divmod(s, 3)
                dve.wait_ge(S["modcol_ready"], layer * 18 + 2 * (3 * i + 2) + 2)
                gate = modv(layer, 3 * i + 2)
                for v in range(2 if TILES[s] == 4 else 1):
                    if v:
                        dve.wait_ge(S["gate_ps"], seen("gate_ps"))
                    V.tensor_tensor(diag.rearrange("p (c n) -> p c n", c=DC),
                                    ident.unsqueeze(1).to_broadcast((P, DC, P)),
                                    gate[:, :, v:v + 1].to_broadcast((P, DC, P)), MUL).then_inc(S["diag_ready"], 1)
                seen("gate_ps", 1)

            last_unit = {ph.stage: ph.first + ph.units for ph in phases if ph.kind == "tail"}

            def y_wait(s, t):
                if t < TILES[s] - 1:
                    dve.wait_ge(S["y_ready"], seen("y_ready"))
                else:
                    dve.wait_ge(unit_used, last_unit[s])

            def residual_norm(s, t):
                y = ps[:, 2 * t:2 * t + 2, :]
                Xt = X[:, t, :].rearrange("p (h n) -> p h n", h=2)
                y_wait(s, t)
                chain(V.tensor_tensor(y, y, gate_row[:, t // 2, :].rearrange("p (h n) -> p h n", h=2), MUL))
                chain(V.scalar_tensor_tensor(Xt, Xt, ALPHA, y, MUL, ADD))
                for h in range(2):
                    chain.give(V.bn_stats(bnst[:, t, h, :], X[:, t, 512 * h:512 * h + 512]))
                chain.wait()
                V.bn_aggr(mv[:, t, :], bnst[:, t, 0:2, :]).then_inc(S["var_ready"], 1)
                invert_std(1, t)
                ins = V.tensor_scalar(X[:, t, :], X[:, t, :], mv[:, t, 0:1], rstd[:, t:t + 1], SUB, MUL)
                if s < 5:
                    ins.then_inc(S["norm_ready"], 1)
                    return
                chain(ins)
                dve.wait_ge(loads["rows"], 32 * 6)
                chain(V.tensor_tensor(X[:, t, :], X[:, t, :], g_row, MUL))
                V.tensor_tensor(X[:, t, :], X[:, t, :], b_row, ADD).then_inc(S["ss_ready"], 1)

            def epilogue(s, first):
                n = TILES[s]
                if s < N_MODULATED:
                    if s < 5:
                        coefficients(s)
                    dve.wait_ge(S["gate_row_ready"], seen("gate_row", 2 if n == 4 else 1))
                    if s > 0:
                        dve.wait_ge(S["xres_ready"], 4 * min(s, 3) + 2 * max(0, s - 3))
                for t in range(n):
                    if t == n - 1:
                        split_lo(first, 0)
                    if s < N_MODULATED:
                        residual_norm(s, t)
                    else:
                        y_wait(s, t)
                        Xt = X[:, t, :].rearrange("p (h n) -> p h n", h=2)
                        V.scalar_tensor_tensor(Xt, ps[:, 2 * t:2 * t + 2, :], 0.5 if STAGES[s] == FFN else 1.0, Xt,
                                               MUL, ADD).then_inc(S["ss_ready"], 1)
                    if t and 5 <= s < 11:
                        split_x(t - 1, False)
                    if s >= 5:
                        dve.wait_ge(S["ss_ready"], seen("ss"))
                        invert_std(1, 8 + t)
                        if t == 0:
                            dve.wait_ge(loads["gain"], 16 * (s - 4))
                        dst = normed[t] if s < 11 else X[:, t, :]
                        V.scalar_tensor_tensor(dst, X[:, t, :], rstd[:, 8 + t:9 + t], next_gain, MUL, MUL
                                               ).then_inc(S["norm_ready" if s < 11 else "out_ready"], 1)
                    if t and s < 5:
                        split_x(t - 1, True)
                if s < 11:
                    split_x(n - 1, s < 5)
                for k in range(1, AHEAD):
                    split_lo(first + k, 0)

            def rope(x1, x2, cos, sin, tmp, heads, half):
                c = cos.unsqueeze(1).to_broadcast((P, heads, half))
                s_ = sin.unsqueeze(1).to_broadcast((P, heads, half))
                w = heads * half
                t4 = [tmp[:, k * w:(k + 1) * w].rearrange("p (h n) -> p h n", h=heads) for k in range(4)]
                for dst, x, table in zip(t4, (x1, x2, x2, x1), (c, s_, c, s_)):
                    chain.give(V.tensor_tensor(dst, x, table, MUL))
                chain.wait()
                chain.give(V.tensor_tensor(x1, t4[0], t4[1], SUB))
                ins = V.tensor_tensor(x2, t4[2], t4[3], ADD)
                chain(ins)

            def head_squares(v, at):
                sq = att["tmp"][:, 0:1024].rearrange("p (h n) -> p h n", n=P)
                chain(V.tensor_tensor(sq, v, v, MUL))
                return V.tensor_reduce(stat[:, at:at + 8], sq, AX.X, ADD)

            def head_norm(v, at, gain):
                chain(V.tensor_tensor(v, v, rstd[:, at:at + 8].unsqueeze(2).to_broadcast((P, 8, P)), MUL))
                chain(V.tensor_tensor(v, v, gain.unsqueeze(1).to_broadcast((P, 8, P)), MUL))

            def attention_rope(v, heads, t):
                rope(v[:, :, 0:64], v[:, :, 64:128], T["att_rope"][:, 0, t, :], T["att_rope"][:, 1, t, :],
                     att["tmp"], heads, 64)

            def qk_given():
                V.tensor_copy(mx[:, 0:1], rstd[:, 0:1]).then_inc(S["qk_ready"], 1)
                dve.wait_ge(S["qk_ready"], seen("qk"))

            def attention_queries(unit, base):
                q = [att["q"][:, t, :].rearrange("p (h n) -> p h n", n=P) for t in range(2)]
                if unit == 8:
                    dve.wait_ge(loads["attn"], 48)
                    dve.wait_ge(S["proj_ready"], base + 2)
                    chain(head_squares(q[0], 0))
                    head_squares(q[1], 8).then_inc(S["var_ready"], 1)
                elif unit == 9:
                    invert_std(16)
                    for t in range(2):
                        head_norm(q[t], 8 * t, T["qk_gain"][:, 0, :])
                elif unit >= 10:
                    attention_rope(q[unit - 10], 8, unit - 10)
                if unit == 11:
                    qk_given()

            def attention():
                k = att["k"].rearrange("p t (h n) -> p (t h) n", n=P)
                head_squares(k, 16).then_inc(S["var_ready"], 1)
                invert_std(8, 16)
                head_norm(k, 16, T["qk_gain"][:, 1, :])
                for t in range(2):
                    attention_rope(k[:, 2 * t:2 * t + 2, :], 2, t)
                qk_given()

                def top(i):
                    dve.wait_ge(S["s_ps"], i + 1)
                    chain(V.reduce_max(mx[:, i:i + 1], ps[:, SCORE_BANKS[i % 4], :], AX.X))
                    V.tensor_scalar(mx[:, i:i + 1], mx[:, i:i + 1], -(P ** -0.5), None, MUL).then_inc(S["max_ready"], 1)

                top(0)
                top(1)
                for i in range(16):
                    if i < 14:
                        top(i + 2)
                    dve.wait_ge(S["exp_ready"], i + 1)
                    chain(V.reciprocal(rden[:, i:i + 1], den[:, i:i + 1]))
                    Pi = att["P"][:, i % 4, :]
                    V.tensor_scalar(Pi, Pi, rden[:, i:i + 1], None, MUL).then_inc(S["p_ready"], 1)

            def hybrid_positions(unit, base):
                pr = proj_dst(7)
                for units, groups, at, table, half in (((17, 20), 2, 0, T["ret_rope"], 32), ((25, 26), 6, 2048, T["dil_rope"], 8)):
                    if unit in units:
                        t = units.index(unit)
                        dve.wait_ge(loads["hyb"], 16)
                        dve.wait_ge(S["proj_ready"], base + groups)
                        v = pr[:, t, at:at + 1024].rearrange("p (h n) -> p h n", n=64)
                        rope(v[:, :, 0:half], v[:, :, half:2 * half], table[:, 0, t, :], table[:, 1, t, :], hyb["tmp"], 16, half)
                        if t:
                            qk_given()

            def hybrid():
                pr = proj_dst(7)
                dve.wait_ge(loads["decay"], 32)
                for h in range(8):
                    dve.wait_ge(S["ret_s_ps"], h + 1)
                    if h >= 2:
                        dve.wait_ge(S["ret_o_ps"], h - 1)
                    St, dec = hyb["St"][:, h % 2, :], hyb["decay"][:, h, :]
                    chain.give(V.tensor_tensor(St[:, 0:256], ps[:, h % 2, 0:256], dec, MUL))
                    V.tensor_tensor(St[:, 256:384], ps[:, h % 2, 256:384], dec[:, 0:P], MUL).then_inc(S["ret_s_ready"], 1)
                o = ps[:, 6:8, :].rearrange("p t (h n) -> p t h n", n=64)
                ret = hyb["ret"].rearrange("p t (h n) -> p t h n", n=64)
                sq = hyb["sq"].rearrange("p t (h n) -> p t h n", n=64)
                mean = stat[:, 0:16].rearrange("p (t h) -> p t h", t=2)
                var = stat[:, 16:32].rearrange("p (t h) -> p t h", t=2)

                def each(f):
                    for t in range(2):
                        chain.give(f(t))
                    chain.wait()

                def retention_norm(part):
                    rt = hyb["ret"]
                    if part == 0:
                        dve.wait_ge(S["ret_o_ps"], 8)
                        chain(V.tensor_reduce(mean, o, AX.X, ADD))
                        chain(V.tensor_scalar(mean, mean, 1.0 / 64, None, MUL))
                        each(lambda t: V.tensor_tensor(ret[:, t], o[:, t], mean[:, t].unsqueeze(2).to_broadcast((P, 8, 64)), SUB))
                    elif part == 1:
                        each(lambda t: V.tensor_tensor(sq[:, t], ret[:, t], ret[:, t], MUL))
                        V.tensor_reduce(var, sq, AX.X, ADD).then_inc(S["var_ready"], 1)
                    elif part == 2:
                        invert_std(16)
                        r = rstd[:, 0:16].rearrange("p (t h) -> p t h", t=2)
                        each(lambda t: V.tensor_tensor(ret[:, t], ret[:, t], r[:, t].unsqueeze(2).to_broadcast((P, 8, 64)), MUL))
                    elif part == 3:
                        each(lambda t: V.tensor_tensor(rt[:, t], rt[:, t], hyb["gn"], MUL))
                    elif part == 4:
                        dve.wait_ge(S["silu_rg"], 1)
                        for t in range(2):
                            V.tensor_tensor(rt[:, t], rt[:, t], pr[:, t, 1536:2048], MUL).then_inc(S["ret_ready"], 1)

                def weights(j):
                    n = P * (j % 2 + 1)
                    return hyb["P"][j % 3][:, 0:2 * n].rearrange("p (h n) -> p h n", h=2), n

                def top(j):
                    dve.wait_ge(S["s_ps"], 16 + j + 1)
                    if j >= 3:
                        dve.wait_ge(S["pT_ps"], 16 + j - 2)
                    Pj, n = weights(j)
                    m, mj = T["bias"][:, 256 - n:256].unsqueeze(1).to_broadcast((P, 2, n)), mx[:, 2 * j:2 * j + 2]
                    b = 2 * (j % 2)
                    chain(V.tensor_tensor(Pj, ps[:, b:b + 2, 0:n], m, ADD))
                    chain(V.reduce_max(mj, Pj, AX.X))
                    V.tensor_scalar(mj, mj, -0.125, None, MUL).then_inc(S["max_ready"], 1)

                top(0)
                top(1)
                for j in range(2 * DIL_PAIRS):
                    retention_norm(j)
                    if j < 2 * DIL_PAIRS - 2:
                        top(j + 2)
                    Pj, n = weights(j)
                    rj = rden[:, 2 * j:2 * j + 2]
                    dve.wait_ge(S["exp_ready"], 16 + j + 1)
                    chain(V.reciprocal(rj, den[:, 2 * j:2 * j + 2]))
                    V.tensor_tensor(Pj, Pj, rj.unsqueeze(2).to_broadcast((P, 2, n)), MUL).then_inc(S["p_ready"], 1)

            def stick_breaking():
                causal = T["causal"].unsqueeze(1).to_broadcast((P, 2, P))

                def masked(buf, last):
                    for h in range(2):
                        v = buf[:, h, :].rearrange("p (b n) -> p b n", b=3)[:, 0:3:2, :]
                        ins = V.tensor_tensor(v, v, causal, MUL)
                        if h:
                            last(ins)
                        else:
                            chain.give(ins)

                def z_of(g):
                    return ps[:, 2 * (g % 2):2 * (g % 2) + 2, 0:384]

                def negabs(g):
                    dve.wait_ge(S["z_ps"], g + 1)
                    if g >= 2:
                        dve.wait_ge(S["arg_ready"], g - 1)
                    LS = sbk["LS"][:, g % 2]
                    chain(V.tensor_scalar(LS, z_of(g), 0.0, 0.25, ALU.min, MUL))
                    V.scalar_tensor_tensor(sbk["E"][:, g % 2], z_of(g), -0.125, LS, MUL, ADD
                                           ).then_inc(S["negabs_ready"], 1)

                negabs(0)
                for g in range(8):
                    if g < 7:
                        negabs(g + 1)
                    b = g % 2
                    z, E_, LS, ST, A_ = z_of(g), sbk["E"][:, b], sbk["LS"][:, b], sbk["ST"][:, b], sbk["A"][:, b]
                    dve.wait_ge(S["log_ready"], g + 1)
                    chain(V.scalar_tensor_tensor(LS, LS, 0.5, E_, MUL, SUB))
                    chain(V.scalar_tensor_tensor(ST, z, -0.125, LS, MUL, ADD))
                    masked(ST, lambda ins: ins.then_inc(S["stay_ready"], 1))
                    if g:
                        dve.wait_ge(S["a_exp"], g)
                        masked(sbk["A"][:, 1 - b], lambda ins: ins.then_inc(S["a_ready"], 1))
                    dve.wait_ge(S["later_ps"], g + 1)
                    V.tensor_tensor(A_, LS, ps[:, 6:8, 0:384], ADD).then_inc(S["arg_ready"], 1)
                dve.wait_ge(S["a_exp"], 8)
                masked(sbk["A"][:, 1], lambda ins: ins.then_inc(S["a_ready"], 1))

            dve.wait_ge(S["csil_ready"], 1)
            dve.wait_ge(loads["consts"], 16)
            for v in range(2):
                src = csil[:, :, v:v + 1].to_broadcast((P, DC, 32))
                h = cvec[:, :, 64 * v:64 * v + 32]
                chain(V.tensor_copy(h, src))
                V.tensor_tensor(cvec[:, :, 64 * v + 32:64 * v + 64], src, h, SUB).then_inc(S["cvec_ready"], 1)
            for n in range(AHEAD):
                split_lo(n, 0)
            for ph in phases:
                s = ph.stage
                N = tokens(s)

                def mod_column(ch):
                    dve.wait_ge(S["modcol_ps"], ch + 1)
                    V.tensor_tensor(modcol[:, bass.ds(ch * 8, 8)].rearrange("p (c v) -> p c v", v=2),
                                    ps[:, 5, 0:8].rearrange("p (c v) -> p c v", v=2),
                                    bmod[:, bass.ds(ch * 4, 4)].rearrange("p (c o) -> p c o", o=1).to_broadcast((P, 4, 2)),
                                    ADD).then_inc(S["modcol_ready"], 1)

                if ph.kind == "mod":
                    def visit(kind, x, idx, n0, q, i):
                        split_lo(n0 + AHEAD, q)
                        if x % 4 == 3:
                            mod_column(x // 4 + i)
                    walk(dve, ph, visit)
                    coefficients(-1)
                    V.tensor_copy(mx[:, 0:1], csil[:, 0, 0:1]).then_inc(S["coef_ready"], 1)
                    for t in range(4):
                        split_x(t, True)
                elif ph.kind in ("ffn_in", "u"):
                    pending = []

                    def visit(kind, x, idx, n0, q, i):
                        split_lo(n0 + AHEAD, q)
                        if kind == "M":
                            if x % 4 == 3:
                                pending.append(x // 4 + i)
                            return
                        if kind == "U":
                            dve.wait_ge(S["gate_ready"], tiles_before[s] + idx + 1)
                            dve.wait_ge(unit_used, n0 + 1 + RING * q)
                            h = hidf[:, bass.ds(idx * TOK, N)]
                            V.tensor_tensor(h, h, ps[:, 2 + x % 2, 0:N], MUL).then_inc(S["hid_ready"], 1)
                        if pending:
                            mod_column(pending.pop())
                    walk(dve, ph, visit)
                elif ph.kind in ("v", "proj"):
                    base = groups_before[ph.first]

                    def visit(kind, x, idx, n0, q, i):
                        split_lo(n0 + AHEAD, q)
                        if STAGES[s] == ATTN:
                            attention_queries(idx, base)
                        if STAGES[s] == HYB and isinstance(idx, int):
                            hybrid_positions(idx, base)
                        if ph.kind == "v" and x % 4 == 3:
                            g = x // 4
                            dve.wait_ge(S["proj_ready"], base + g + 1 + q)
                            for t in range(2):
                                V.bn_stats(bnst[:, 2 * t:2 * t + 2, :, :].rearrange("p a b c -> p (a b c)")[:, bass.ds((g + q) * 6, 6)],
                                           v_tok[:, t, bass.ds((idx - 3) * 128, 512)]).then_inc(S["vstat_ready"], 1)
                    walk(dve, ph, visit)
                    if ph.kind == "v":
                        vec = ph.more["vec"]
                        dve.wait_ge(S["vstat_ready"], 12 * (vec + 1))
                        for t in range(2):
                            st_ = bnst[:, 2 * t:2 * t + 2, :, :].rearrange("p a b c -> p (a b c)")[:, 0:36]
                            ins = V.bn_aggr(mv[:, t, :], st_.rearrange("p (a b) -> p a b", b=6))
                            if t:
                                ins.then_inc(S["var_ready"], 1)
                            else:
                                chain.give(ins)
                        invert_std(2)
                        for t in range(2):
                            V.tensor_scalar(v_tok[:, t, :], v_tok[:, t, :], mv[:, t, 0:1], rstd[:, t:t + 1], SUB, MUL
                                            ).then_inc(S["v_normed"], 1)
                    if STAGES[s] == ATTN:
                        dve.wait_ge(S["proj_ready"], base + 3)
                        attention()
                    elif STAGES[s] == HYB:
                        dve.wait_ge(S["proj_ready"], base + 7)
                        hybrid()
                    elif STAGES[s] == SB:
                        dve.wait_ge(S["proj_ready"], base + 6)
                        stick_breaking()
                elif ph.kind == "out":
                    if s < N_MODULATED:
                        gates(s)
                    K = OUT_K[s]
                    src_ap = out_source(s)
                    src = (lambda k: hidf[:, bass.ds(k * TOK, N)]) if src_ap is None else (lambda k: src_ap[:, k, :])
                    for k in range(AHEAD):
                        hs_lo(s, src, k, k, hs_before[s] + k + 1)

                    def visit(kind, x, idx, n0, q, i):
                        split_lo(n0 + AHEAD, q)
                        hs_lo(s, src, idx + AHEAD, x + AHEAD, hs_before[s] + idx + AHEAD + 1)
                    walk(dve, ph, visit)
                elif ph.kind == "tail":
                    k = OUT_K[s] - 1
                    split_lo(ph.first + RING - 1, 0)
                    hs_lo(s, src, k, k, hs_before[s] + k + 1)
                    epilogue(s, ph.first + ph.units)
                if ph.kind in ("u", "v") and not (ph.kind == "v" and ph.more["vec"] == LAT):
                    vec = LAT if ph.kind == "u" else CTX
                    def affine(c):
                        dve.wait_ge(S["mix_scaled"], GT * vec + c + 1)
                        m = mixbuf[:, c % 2, :].rearrange("p (n q) -> p n q", n=2)
                        b = ps[:, 4 + c % 4, 256:384].unsqueeze(1).to_broadcast((P, 2, P))
                        V.tensor_tensor(m, m, b, ADD).then_inc(S["mix_step"], 1)

                    affine(0)
                    for c in range(GT):
                        if c < GT - 1:
                            affine(c + 1)
                        h = hid[:, c, 256 * vec:256 * vec + 256]
                        dve.wait_ge(S["mix_step"], GT * vec + c + 1)
                        if c == 0:
                            dve.wait_ge(S["gate_ready"], tiles_before[s] + GT)
                        V.tensor_tensor(h, h, mixbuf[:, c % 2, :], MUL).then_inc(S["mix_done"], 1)

        @block.tensor
        def _(pe):
            seen = Tally()
            mm = nc.tensor.matmul

            def passes(out, hi, lo, w_hi, w_lo, first, last, stationary_w):
                todo = [(hi, w_hi), (lo, w_hi), (hi, w_lo)] if stationary_w else [(hi, w_hi), (hi, w_lo), (lo, w_hi)]
                for k, (x, w) in enumerate(todo):
                    ins = mm(out, w if stationary_w else x, x if stationary_w else w,
                             start=first and k == 0, stop=last and k == 2)
                return ins

            def feature_unit(n0, bank, N):
                slot = n0 % RING
                for kt in range(DC):
                    w = slice(kt * P, kt * P + P)
                    ins = passes(ps[:, bank, 0:N], xhi[:, kt, 0:N], xlo[:, kt, 0:N], whi[:, slot, w], wlo[:, slot, w],
                                 kt == 0, kt == DC - 1, True)
                ins.then_inc(unit_used, 1)

            def token_unit(n0, quarter, tiles, banks):
                slot = n0 % RING
                for kk in range(2):
                    kt = 2 * quarter + kk
                    for t, bank in zip(tiles, banks):
                        r, w = slice(t * P, t * P + P), slice(512 * kk, 512 * kk + 512)
                        ins = passes(ps[:, bank, :], xhi[:, kt, r], xlo[:, kt, r], whi[:, slot, w], wlo[:, slot, w],
                                     kt == 0, kt == DC - 1, False)
                ins.then_inc(unit_used, 1)

            def mod_unit(n0, quarter):
                slot = n0 % RING
                for kk in range(2):
                    kt = 2 * quarter + kk
                    for w, part in ((whi, 0), (wlo, 1)):
                        ins = mm(ps[:, 4, :], cvec[:, kt, :], w[:, slot, 512 * kk:512 * kk + 512],
                                 start=kt == 0 and part == 0, stop=kt == DC - 1 and part == 1)
                ins.then_inc(unit_used, 1)

            def mod_column(ch):
                pe.wait_ge(S["modrow_ready"], ch + 1)
                if not isinstance(ch, int) or ch > 0:
                    pe.wait_ge(S["modcol_ready"], ch)
                for c in range(4):
                    ins = mm(ps[:, 5, 2 * c:2 * c + 2], modrow[:, c * P:c * P + P], sel, start=True, stop=True)
                ins.then_inc(S["modcol_ps"], 1)

            def out_products(s, n0, x, t, last):
                slot, h = n0 % RING, x % RING
                first = x == 0
                r = slice(t * P, t * P + P)
                hi, lo = hs[:, h, 0, r], hs[:, h, 1, r]
                for half in range(2):
                    w = slice(512 * half, 512 * half + 512)
                    mm(ps[:, 2 * t + half, :], hi, whi[:, slot, w], start=first, stop=False)
                    mm(ps[:, 2 * t + half, :], hi, wlo[:, slot, w], start=False, stop=False)
                for half in range(2):
                    w = slice(512 * half, 512 * half + 512)
                    ins = mm(ps[:, 2 * t + half, :], lo, whi[:, slot, w], start=False, stop=last)
                return ins

            def transposes(src, t):
                for c in range(DC):
                    ins = nc.tensor.transpose(ps[:, 2 * t + c // 4, (c % 4) * P:(c % 4 + 1) * P],
                                              src[:, c * P:(c + 1) * P], ident)
                ins.then_inc(S["xT_ps"], 1)

            def out_tail(s, first):
                k0, n = OUT_K[s] - RING, TILES[s]
                src = [X[:, t, :] for t in range(n)] if s < 5 else normed
                for t in range(n):
                    for j in range(RING):
                        if t == 0:
                            unit_wait(first + j, 0)
                            pe.wait_ge(S["hs_lo"], hs_before[s] + k0 + j + 1)
                        ins = out_products(s, first + j, k0 + j, t, j == RING - 1)
                        if t == n - 1:
                            ins.then_inc(unit_used, 1)
                    if t < n - 1:
                        ins.then_inc(S["y_ready"], 1)
                    if t and s < 11:
                        pe.wait_ge(S["norm_ready"], seen("norm"))
                        transposes(src[t - 1], t - 1)
                if s < 11:
                    pe.wait_ge(S["norm_ready"], seen("norm"))
                    transposes(src[n - 1], n - 1)

            def gates(s):
                for v in range(2 if TILES[s] == 4 else 1):
                    pe.wait_ge(S["diag_ready"], seen("diag"))
                    if v:
                        pe.wait_ge(S["gate_row_ready"], seen.n.get("gate_row", 0) + 1)
                    for h in range(2):
                        ins = mm(ps[:, 6 + h, :], ones, diag[:, 512 * h:512 * h + 512], start=True, stop=True)
                    ins.then_inc(S["gate_ps"], 1)
                seen("gate_row", 2 if TILES[s] == 4 else 1)
                pe.wait_ge(S["gate_row_ready"], seen.n["gate_row"])

            def mix(vec):
                pe.wait_ge(S["v_normed"], 2 * (vec + 1))
                if vec == LAT:
                    pe.wait_ge(S["rs_ready"], 4)
                for c in range(GT):
                    g, bank = c // 3, 4 + c % 4
                    i = GT * vec + c
                    if c >= 4:
                        pe.wait_ge(S["mix_done"], i - 3)
                    for n in range(2):
                        mm(ps[:, bank, n * P:(n + 1) * P], v_tok[:, n, c * P:(c + 1) * P], wsT[:, g * P:(g + 1) * P],
                           start=True, stop=True)
                    r = 32 * (c // 6)
                    mm(ps[:, bank, 256:384], lnb_row[r:r + 2, (c % 6) * P:(c % 6 + 1) * P],
                       sum_row[r:r + 2, (g % 2) * P:(g % 2 + 1) * P], start=True, stop=True).then_inc(S["mix_ps"], 1)

            def attention():
                pe.wait_ge(S["qk_ready"], 1)
                for h in range(8):
                    for t in range(2):
                        ins = nc.tensor.transpose(ps[:, h // 2, (h % 2) * 256 + t * P:(h % 2) * 256 + (t + 1) * P],
                                                  att["q"][:, t, h * P:(h + 1) * P], ident)
                ins.then_inc(S["qkT_ps"], 1)
                pe.wait_ge(S["qk_ready"], 2)
                pe.wait_ge(S["value_ready"], 1)
                for g in range(2):
                    for t in range(4):
                        ins = nc.tensor.transpose(ps[:, 4 + g, t * P:(t + 1) * P], att["k"][:, t, g * P:(g + 1) * P], ident)
                ins.then_inc(S["qkT_ps"], 1)
                pe.wait_ge(S["qkT_ready"], 2)

                def scores(i):
                    h, t = divmod(i, 2)
                    if i >= 4:
                        pe.wait_ge(S["exp_ready"], i - 3)
                    mm(ps[:, SCORE_BANKS[i % 4], :], att["qT"][:, h, t * P:(t + 1) * P], att["kT"][:, h // 4, :],
                       start=True, stop=True).then_inc(S["s_ps"], 1)

                for i in range(3):
                    scores(i)
                for i in range(16):
                    h, t = divmod(i, 2)
                    if i < 13:
                        scores(i + 3)
                    pe.wait_ge(S["p_ready"], i + 1)
                    if i >= 2:
                        pe.wait_ge(S["pT_ready"], i - 1)
                    for k in range(4):
                        ins = nc.tensor.transpose(ps[:, 2 + i % 2, k * P:(k + 1) * P], att["P"][:, i % 4, k * P:(k + 1) * P], ident)
                    ins.then_inc(S["pT_ps"], 1)
                    if t == 1:
                        pe.wait_ge(S["pT_ready"], i + 1)
                        if h >= 2:
                            pe.wait_ge(S["o_ready"], h - 1)
                        v = slice((h // 4) * P, (h // 4 + 1) * P)
                        for k in range(4):
                            ins = mm(ps[:, 4 + h % 2, 0:256], att["v"][:, k, v], att["PT"][:, h % 2, k, :],
                                     start=k == 0, stop=k == 3)
                        ins.then_inc(S["o_ps"], 1)
                pe.wait_ge(S["o_ready"], o_made[ATTN])

            def qk_transposes(pr, columns, ready):
                for k, at in enumerate(columns):
                    if k % 8 == 0:
                        pe.wait_ge(*ready[k // 8])
                    bank = (4 + k // 2) % 8
                    for t in range(2):
                        ins = nc.tensor.transpose(ps[:, bank, (k % 2) * 256 + t * P:(k % 2) * 256 + (t + 1) * P],
                                                  pr[:, t, at:at + P], ident)
                    if k % 8 == 7:
                        ins.then_inc(S["qkT_ps"], 1)

            def key_major(bank, qT, kT, head):
                r = slice(64 * (head % 2), 64 * (head % 2) + 64)
                c = head // 2
                mm(ps[:, bank, 0:256], kT[r, c, 0:P], qT[r, c, 0:256], start=True, stop=True)
                return mm(ps[:, bank, 256:384], kT[r, c, P:256], qT[r, c, P:256], start=True, stop=True)

            def hybrid(base):
                pr = proj_dst(7)
                pe.wait_ge(S["qk_ready"], 4)
                qk_transposes(pr, [P * k for k in range(8)] + [2048 + P * k for k in range(8)],
                              [(S["qk_ready"], 3), (S["proj_ready"], base + 7)])
                pe.wait_ge(S["qkT_ready"], 4)
                rq, rk, dq, dk = (hyb["qkT"][:, 4 * k:4 * k + 4, :] for k in range(4))

                def ret_scores(h):
                    if h >= 2:
                        pe.wait_ge(S["ret_s_ready"], h - 1)
                    key_major(h % 2, rq, rk, h).then_inc(S["ret_s_ps"], 1)

                ret_scores(0)
                for h in range(8):
                    if h < 7:
                        ret_scores(h + 1)
                    pe.wait_ge(S["ret_s_ready"], h + 1)
                    St = hyb["St"][:, h % 2, :]
                    c = slice(64 * h, 64 * h + 64)
                    v = slice(1024 + 64 * h, 1024 + 64 * h + 64)
                    mm(ps[:, 6, c], St[:, 0:P], pr[:, 0, v], start=True, stop=True)
                    mm(ps[:, 7, c], St[:, P:256], pr[:, 0, v], start=True, stop=False)
                    mm(ps[:, 7, c], St[:, 256:384], pr[:, 1, v], start=False, stop=True).then_inc(S["ret_o_ps"], 1)

                def scores(j):
                    g, t = divmod(j, 2)
                    n = P * (t + 1)
                    if j >= 2:
                        pe.wait_ge(S["max_ready"], 16 + j - 1)
                    for h in range(2):
                        r = slice(64 * h, 64 * h + 64)
                        ins = mm(ps[:, 2 * (j % 2) + h, 0:n], dq[r, g, t * P:(t + 1) * P], dk[r, g, 0:n],
                                 start=True, stop=True)
                    ins.then_inc(S["s_ps"], 1)

                scores(0)
                scores(1)
                for j in range(2 * DIL_PAIRS):
                    g, t = divmod(j, 2)
                    if j < 2 * DIL_PAIRS - 2:
                        scores(j + 2)
                    if j == 2 * DIL_PAIRS - 1:
                        pe.wait_ge(S["ret_ready"], 2)
                        pe.wait_ge(S["max_ready"], 16 + j)
                        for k in range(4):
                            for tile in range(2):
                                at = (k % 2) * 256 + tile * P
                                ins = nc.tensor.transpose(ps[:, k // 2, at:at + P], hyb["ret"][:, tile, k * P:(k + 1) * P], ident)
                        ins.then_inc(S["retT_ps"], 1)
                    pe.wait_ge(S["p_ready"], 16 + j + 1)
                    if j >= 2:
                        pe.wait_ge(S["pT_ready"], 16 + j - 1)
                    for k in range(2 * (t + 1)):
                        ins = nc.tensor.transpose(ps[:, 4 + j % 2, k * P:(k + 1) * P], hyb["P"][j % 3][:, k * P:(k + 1) * P], ident)
                    ins.then_inc(S["pT_ps"], 1)
                    if t == 1:
                        pe.wait_ge(S["pT_ready"], 16 + j + 1)
                        if g >= 2:
                            pe.wait_ge(S["o_ready"], o_made[ATTN] + g - 1)
                        for h in range(2):
                            r = slice(64 * h, 64 * h + 64)
                            v = slice(3072 + 64 * (2 * g + h), 3072 + 64 * (2 * g + h) + 64)
                            mm(ps[r, 6 + g % 2, 0:256], pr[:, 0, v], hyb["PT"][:, g % 2, 2 * h, :], start=True, stop=False)
                            ins = mm(ps[r, 6 + g % 2, P:256], pr[:, 1, v], hyb["PT"][:, g % 2, 2 * h + 1, P:256],
                                     start=False, stop=True)
                        ins.then_inc(S["o_ps"], 1)
                pe.wait_ge(S["o_ready"], o_made[HYB])

            def stick_breaking(base):
                pr = proj_dst(10)
                qk_transposes(pr, [P * k for k in range(16)], [(S["proj_ready"], base + 4), (S["proj_ready"], base + 6)])
                pe.wait_ge(S["qkT_ready"], 6)
                qT, kT = sbk["qkT"][:, 0:8, :], sbk["qkT"][:, 8:16, :]
                tri = T["tri"]

                def scores(g):
                    if g >= 2:
                        pe.wait_ge(S["stay_ready"], g - 1)
                    for h in range(2):
                        ins = key_major(2 * (g % 2) + h, qT, kT, 2 * g + h)
                    ins.then_inc(S["z_ps"], 1)

                def output(g):
                    A_ = sbk["A"][:, g % 2]
                    pe.wait_ge(S["a_ready"], g + 1)
                    if g >= 2:
                        pe.wait_ge(S["o_ready"], o_made[HYB] + g - 1)
                    for h in range(2):
                        r = slice(64 * h, 64 * h + 64)
                        v = slice(2048 + 64 * (2 * g + h), 2048 + 64 * (2 * g + h) + 64)
                        mm(ps[r, 4 + g % 2, 0:256], pr[:, 0, v], A_[:, h, 0:256], start=True, stop=False)
                        ins = mm(ps[r, 4 + g % 2, P:256], pr[:, 1, v], A_[:, h, 256:384], start=False, stop=True)
                    ins.then_inc(S["o_ps"], 1)

                scores(0)
                scores(1)
                for g in range(8):
                    pe.wait_ge(S["stay_ready"], g + 1)
                    ST = sbk["ST"][:, g % 2]
                    if g:
                        pe.wait_ge(S["arg_ready"], g)
                    for h in range(2):
                        mm(ps[:, 6 + h, 0:256], tri, ST[:, h, 0:256], start=True, stop=False)
                        mm(ps[:, 6 + h, P:256], ones, ST[:, h, 256:384], start=False, stop=True)
                        ins = mm(ps[:, 6 + h, 256:384], tri, ST[:, h, 256:384], start=True, stop=True)
                    ins.then_inc(S["later_ps"], 1)
                    if g < 6:
                        scores(g + 2)
                    if g:
                        output(g - 1)
                output(7)
                pe.wait_ge(S["o_ready"], o_made[SB])

            def unit_wait(n0, q):
                pe.wait_ge(lo_ready, n0 + 1 + RING * q)

            pe.wait_ge(S["cvec_ready"], 2)
            pe.wait_ge(loads["consts"], 16)
            for ph in phases:
                s = ph.stage
                N = tokens(s)

                def before_chunk(ch, x):
                    if not isinstance(ch, int) or ch > 0:
                        pe.wait_ge(S["modrow_ready"], ch)

                if ph.kind == "mod":
                    def visit(kind, x, idx, n0, q, i):
                        ch = x // 4 + i
                        unit_wait(n0, q)
                        if x % 4 == 0:
                            before_chunk(ch, x)
                        mod_unit(n0, x % 4)
                        if x % 4 == 3:
                            mod_column(ch)
                    walk(pe, ph, visit)
                    pe.wait_ge(loads["x"], 32)
                    pe.wait_ge(S["coef_ready"], 1)
                    for t in range(4):
                        transposes(X[:, t, :], t)
                elif ph.kind in ("ffn_in", "u"):
                    pending = []
                    base = tiles_before[s]
                    pe.wait_ge(S["x_ready"], tiles_ready(s))

                    def visit(kind, x, idx, n0, q, i):
                        unit_wait(n0, q)
                        if kind == "M":
                            ch = x // 4 + i
                            if x % 4 == 0:
                                before_chunk(ch, x)
                            mod_unit(n0, x % 4)
                            if x % 4 == 3:
                                pending.append(ch)
                            return
                        if kind in "GF":
                            if not isinstance(q, int) or base + idx > 1:
                                pe.wait_ge(S["gate_ready"], base + idx - 1)
                            feature_unit(n0, x % 2, N)
                        else:
                            hb = hid_before[s]
                            if not isinstance(q, int) or hb + idx > 1:
                                pe.wait_ge(S["hid_ready"], hb + idx - 1)
                            feature_unit(n0, 2 + x % 2, N)
                        if pending:
                            mod_column(pending.pop())
                    walk(pe, ph, visit)
                    if s in mods_by:
                        pe.wait_ge(S["modcol_ready"], mods_by[s])
                    if ph.kind == "u":
                        mix(LAT)
                elif ph.kind in ("v", "proj"):
                    base = groups_before[ph.first]
                    pe.wait_ge(S["x_ready"], tiles_ready(s))
                    if ph.kind == "v" and ph.more["vec"] == LAT:
                        pe.wait_ge(loads["gmlp"], 16 * 9)
                        for i in range(4):
                            ins = mm(ps[32 * i:32 * i + 1, 7, 0:256], ones[:, 0:1], wsT[:, 256 * i:256 * i + 256],
                                     start=True, stop=True)
                        ins.then_inc(S["rs_ps"], 1)

                    def visit(kind, x, idx, n0, q, i):
                        g = x // 4
                        unit_wait(n0, q)
                        if STAGES[s] == ATTN:
                            tiles, banks = [([0, 1], [0, 1]), ([0, 1], [2, 3]), (range(4), range(4, 8))][g]
                        else:
                            t0 = 2 * ph.more.get("vec", 0)
                            tiles, banks = [t0, t0 + 1], [2 * (g % 2), 2 * (g % 2) + 1]
                            if x % 4 == 0 and (not isinstance(q, int) or base + g > 1):
                                pe.wait_ge(S["proj_ready"], base + g - 1 + q)
                        token_unit(n0, x % 4, tiles, banks)
                    walk(pe, ph, visit)
                    if ph.kind == "v" and ph.more["vec"] == CTX:
                        mix(CTX)
                    if STAGES[s] == ATTN:
                        attention()
                    elif STAGES[s] == HYB:
                        hybrid(base)
                    elif STAGES[s] == SB:
                        stick_breaking(base)
                elif ph.kind == "out":
                    if STAGES[s] == FFN:
                        pe.wait_ge(S["hid_ready"], hid_before[s] + FT)
                    elif STAGES[s] == GMLP:
                        pe.wait_ge(S["mix_done"], 2 * GT)
                    if s < N_MODULATED:
                        gates(s)

                    def visit(kind, x, idx, n0, q, i):
                        unit_wait(n0, q)
                        pe.wait_ge(S["hs_lo"], hs_before[s] + idx + 1)
                        for t in range(TILES[s]):
                            ins = out_products(s, n0, x, t, False)
                        ins.then_inc(unit_used, 1)
                    walk(pe, ph, visit)
                elif ph.kind == "tail":
                    out_tail(s, ph.first)


def constants():
    import numpy as np

    f4 = np.float32
    consts = np.zeros((P, 264), f4)
    consts[:, 0:P] = np.eye(P)
    consts[:, P:2 * P] = 1.0
    consts[[0, 32], 2 * P] = 1.0
    consts[[64, 96], 2 * P + 1] = 1.0
    consts[:, 260], consts[:, 261] = RMS_EPS, LN_EPS
    pos = np.arange(256)

    def rope(angle):
        both = np.stack([np.cos(angle), np.sin(angle)]).astype(f4)
        return both.reshape(2, 2, P, -1).transpose(2, 0, 1, 3).reshape(P, -1)

    quarter = 32
    freqs = (f4(10000.0) ** (-np.arange(quarter, dtype=f4) / f4(quarter))).astype(f4)
    grid = np.concatenate([(pos // 64).astype(f4)[:, None] * freqs, (pos % 64).astype(f4)[:, None] * freqs], 1)

    def plain(half, theta):
        inv = (f4(1.0) / (f4(theta) ** (np.arange(half, dtype=f4) / f4(half)))).astype(f4)
        return pos.astype(f4)[:, None] * inv[None, :]

    i, j = np.arange(P)[:, None], np.arange(256)[None, :]
    dist = i + P - j
    count = ((dist >= 0) & (dist <= 128)).astype(f4)
    count += (dist >= 0) & (dist % 4 == 0)
    count += (dist >= 0) & (dist % 16 == 0)
    bias = np.where(count > 0, 8.0 * np.log(np.maximum(count, 1.0)), -1e30).astype(f4)
    key, query = np.arange(P)[:, None], np.arange(P)[None, :]
    causal = (key < query).astype(f4)
    tri = (key > query).astype(f4)
    tables = np.concatenate([rope(plain(32, 10000.0)), rope(plain(8, 500000.0)), bias, causal, tri], 1)
    lag = np.arange(256)[None, :] - np.arange(P)[:, None]
    log_g = np.log(1.0 - 2.0 ** (-5.0 - np.arange(8)))
    decay = np.where(lag >= 0, np.exp(np.maximum(lag, 0)[None] * log_g[:, None, None]), 0.0) * 0.125
    return dict(consts=consts, att_rope=rope(grid), tables=tables.astype(f4),
                decay=np.ascontiguousarray(decay.transpose(1, 0, 2)).astype(f4))


def kernel(**inputs):
    import numpy as np
    import concourse.bacc as bacc
    from concourse.bass_utils import run_bass_kernel_spmd

    g = {k: np.asarray(v) for k, v in inputs.items()}

    def feature_units(w, n):
        return w.reshape(DC, P, n, P).transpose(2, 1, 0, 3).reshape(n, P, UNIT)

    def token_units(w):
        n = w.shape[1] // 512
        return w.reshape(4, 2, P, n, 512).transpose(3, 0, 2, 1, 4).reshape(4 * n, P, UNIT)

    def out_units(w):
        return w.reshape(-1, P, UNIT)

    def column(v):
        return v.reshape(-1, P).T

    ffns = [(g["ffn_w_in"][l, i], g["ffn_w_out"][l, i]) for l in range(2) for i in range(2)]
    ffns += [(g[f"ffn{i}_w_in_2"][l], g[f"ffn{i}_w_out_2"][l]) for l in range(2) for i in (1, 2)]
    arrays = constants()
    for i, (w_in, w_out) in enumerate(ffns):
        arrays[f"ffn_gate{i}"] = feature_units(w_in[:, :FF], FT)
        arrays[f"ffn_up{i}"] = feature_units(w_in[:, FF:], FT)
        arrays[f"ffn_out{i}"] = out_units(w_out)
    arrays.update(
        w_mod=np.concatenate([token_units(w) for w in g["w_mod"]]),
        gmlp_u=feature_units(g["gmlp_w_in"][0][:, :3 * D], GT),
        gmlp_v=token_units(g["gmlp_w_in"][0][:, 3 * D:]),
        gmlp_out=out_units(g["gmlp_w_out"][0]),
        attn_in=token_units(g["attn_w_qkv"][0]), attn_out=out_units(g["attn_w_o"][0]),
        hyb_in=token_units(g["hyb_w_in_2"][0]), hyb_out=out_units(g["hyb_w_out_2"][0]),
        sb_in=token_units(g["sb_w_in_2"][0]), sb_out=out_units(g["sb_w_out_2"][0]),
        x=g["x"][0].reshape(2, P, D).transpose(1, 0, 2), ctx=g["ctx"][0].reshape(2, P, D).transpose(1, 0, 2),
        wsT=g["gmlp_w_s"][0].transpose(2, 0, 1).reshape(P, GROUPS * P),
        gmlp_ln_b=g["gmlp_ln_b"].reshape(4, 768), gmlp_b_s=g["gmlp_b_s"].reshape(4, 256),
        q_norm=g["attn_q_norm"].reshape(1, P), k_norm=g["attn_k_norm"].reshape(1, P),
        ln_g=g["ln_g"].reshape(6, D), ln_b=g["ln_b"].reshape(6, D),
        ret_gn=g["ret_gn_2"].reshape(1, 512),
        norm_rows=np.stack([g[n][l] for l in range(2) for n in ("ffn1_norm_2", "mix_norm_2", "ffn2_norm_2")]
                           + [g["final_norm_2"]]),
        cols=np.concatenate([
            np.stack([column(g["c"]), column(g["c_ctx"])], -1).reshape(P, 2 * DC),
            column(g["b_mod"]), column(g["ln_g"]), column(g["ln_b"]), column(g["gmlp_ln_g"])], 1),
    )
    nc = bacc.Bacc("TRN2", target_bir_lowering=False, num_devices=1)
    feed, aps = {}, {}
    for name, v in arrays.items():
        feed["in_" + name] = np.ascontiguousarray(v)
        aps[name] = nc.dram_tensor("in_" + name, v.shape, mybir.dt.from_np(v.dtype), kind="ExternalInput").ap()
    for part in ("gate", "up", "out"):
        aps["ffn_" + part] = [aps[f"ffn_{part}{i}"] for i in range(len(ffns))]
    result = nc.dram_tensor("out_dram", (2, P, D), mybir.dt.float32, kind="ExternalOutput").ap()
    aps["out"] = result.rearrange("t p n -> p t n")
    fused_blocks(nc, aps)
    r = run_bass_kernel_spmd(nc, [feed], core_ids=[0])
    return r.results[0]["out_dram"].reshape(1, 256, D)
```

```python
import concourse.bass as bass
from concourse import mybir
from contextlib import ExitStack

D = 1024
P = 128
DC = D // P
TOK = 512
FF = 2816
FT = FF // P
GT = 3 * D // P
GROUPS = 8
ALPHA = 4.0 ** 0.25
LN_EPS = 1e-5
RMS_EPS = 1e-6
RING = 4
AHEAD = 3
UNIT = 1024
LAT, CTX = 0, 1

FFN, GMLP, ATTN, HYB, SB = "ffn", "gmlp", "attn", "hyb", "sb"
STAGES = [FFN, GMLP, FFN, FFN, ATTN, FFN, FFN, HYB, FFN, FFN, SB, FFN]
N_MODULATED = 6
TILES = [4, 4, 4, 4] + [2] * 8
OUT_K = [{FFN: FT, GMLP: GT}.get(s, DC) for s in STAGES]
DIL_PAIRS = 4
EARLY = (GMLP, ATTN)
LAST_TILE_UNIT = 2
GATES = [2 if tiles == 4 else 1 for tiles in TILES]
GATE_BANKS = (6, 4)
V_PARTS = (slice(0, 4 * P), slice(4 * P, 12 * P), slice(12 * P, GT * P))
SCORE_BANKS = (0, 1, 6, 7)
PROJ_GROUPS = {ATTN: 3, HYB: 7, SB: 6}


class Phase:

    def __init__(self, kind, stage, first, rounds, **more):
        self.kind, self.stage, self.first, self.rounds = kind, stage, first, rounds
        self.units = sum(trips * len(body) for trips, body in rounds)
        self.more = more


def tiles_ready(s):
    return 4 + sum(TILES[:s])


def plan():
    phases, at = [], 0

    def add(kind, stage, rounds, **more):
        nonlocal at
        phases.append(Phase(kind, stage, at, rounds, **more))
        at += phases[-1].units

    def chunk(a, b):
        return [("M", 4 * a + q, 4 * b) for q in range(4)]

    def shifted(body, by):
        return [(k, a + by * b, b) for k, a, b in body]

    def proj(groups, first_peeled):
        body = [("B", u, 8) for u in range(8)]
        rounds = [(1, body), (groups // 2 - 1, shifted(body, 1))] if first_peeled else [(groups // 2, body)]
        if groups % 2:
            rounds.append((1, [("B", 4 * (groups - 1) + q, 0) for q in range(4)]))
        return rounds

    def out(k):
        rounds = [(1, [("O", j, 0) for j in range(4)])]
        turns = max(0, (k - 8) // 4)
        if turns:
            rounds.append((turns, [("O", 4 + j, 4) for j in range(4)]))
        middle = [("O", j, 0) for j in range(4 + 4 * turns, k - RING)]
        return rounds + ([(1, middle)] if middle else [])

    add("mod", -1, [(1, chunk(0, 0)), (3, chunk(1, 1))])
    chunks = 4
    for s, kind in enumerate(STAGES):
        if kind == FFN:
            mods = {0: 10, 2: 10, 3: 6}.get(s, 0)
            m = chunk(chunks, 1)
            mixed = m[:2] + [("G", 0, 2), ("U", 0, 2)] + m[2:] + [("G", 1, 2), ("U", 1, 2)]
            rounds = []
            if mods and s == 0:
                rounds = [(1, mixed), (mods - 1, shifted(mixed, 1))]
            elif mods:
                rounds = [(mods, mixed)]
            rest = FT // 2 - mods - 1
            plain = [("G", 2 * mods, 2), ("U", 2 * mods, 2), ("G", 2 * mods + 1, 2), ("U", 2 * mods + 1, 2)]
            if rest:
                rounds.append((rest, plain))
            rounds.append((1, shifted(plain, rest)))
            add("ffn_in", s, rounds)
            chunks += mods
        elif kind == GMLP:
            add("v", s, proj(GT // 4, True), vec=LAT)
            m = chunk(chunks, 1)
            body = m[:2] + [("F", 0, 4), ("F", 1, 4)] + m[2:] + [("F", 2, 4), ("F", 3, 4)]
            add("u", s, [(GT // 4, body)])
            chunks += GT // 4
            add("v", s, proj(GT // 4, False), vec=CTX)
        else:
            groups = PROJ_GROUPS[kind]
            if kind == ATTN:
                add("proj", s, [(1, [("B", u, 0) for u in range(4 * groups)])])
            elif kind == HYB:
                body = [("B", u, 8) for u in range(8)]
                last = [("B", u, 0) for u in range(16, 4 * groups)]
                add("proj", s, [(2, body), (1, last)])
            else:
                add("proj", s, proj(groups, False))
        add("out", s, out(OUT_K[s]))
        add("tail", s, [(1, [("O", j, 0) for j in range(OUT_K[s] - RING, OUT_K[s])])])
    return phases, at


def fused_blocks(nc, a):
    f32, f32r = mybir.dt.float32, mybir.dt.float32r
    ALU, ACT, AX = mybir.AluOpType, mybir.ActivationFunctionType, mybir.AxisListType
    MUL, ADD, SUB = ALU.mult, ALU.add, ALU.subtract
    phases, n_units = plan()

    with ExitStack() as ctx:
        def sb(name, shape, dt=f32):
            return ctx.enter_context(nc.sbuf_tensor(name, shape, dt))

        def sem(name):
            return ctx.enter_context(nc.semaphore(name))

        w32 = sb("w32", [P, RING, UNIT])
        whi = sb("whi", [P, RING, UNIT], f32r)
        wlo = sb("wlo", [P, RING, UNIT], f32r)
        xhi = sb("xhi", [P, DC, TOK], f32r)
        xlo = sb("xlo", [P, DC, TOK], f32r)
        hid = sb("hid", [P, GT, TOK])
        hs = sb("hs", [P, RING, 2, TOK], f32r)
        X = sb("X", [P, 4, D])
        arena = sb("arena", [P, 6144])
        side = sb("side", [P, 2048])
        cvec = sb("cvec", [P, DC, P], f32r)
        modrow = sb("modrow", [P, 512])
        modcol = sb("modcol", [P, 2 * 9 * DC * 2])
        cols = sb("cols", [P, a["cols"].shape[1]])
        consts = sb("consts", [P, a["consts"].shape[1]])
        coef = sb("coef", [P, 4, DC, 2])
        csil = sb("csil", [P, DC, 2])
        bnst = sb("bnst", [P, 4, 6, 6])
        mv = sb("mv", [P, 4, 2])
        std = sb("std", [P, 64])
        rstd = sb("rstd", [P, 64])
        stat = sb("stat", [P, 64])
        mx = sb("mx", [P, 16])
        den = sb("den", [P, 16])
        rden = sb("rden", [P, 16])
        ps = ctx.enter_context(nc.psum_tensor("ps", [P, 8, 512], f32))

        hidf = hid[:, :, :].rearrange("p c n -> p (c n)")
        Xf = X[:, :, :].rearrange("p t n -> p (t n)")
        ident, ones, sel = consts[:, 0:P], consts[:, P:2 * P], consts[:, 2 * P:2 * P + 2]

        def col(name, per):
            at = {"c": 0, "b_mod": 16, "ln_g": 160, "ln_b": 208, "gmlp_g": 256}[name]
            return cols[:, at:at + per]

        c_col = col("c", 16).rearrange("p (c v) -> p c v", v=2)
        bmod = col("b_mod", 144)
        lng = col("ln_g", 48).rearrange("p (s c) -> p s c", c=DC)
        lnb = col("ln_b", 48).rearrange("p (s c) -> p s c", c=DC)
        gmg = col("gmlp_g", GT)
        gate_row = arena[:, 0:2 * D].rearrange("p (v n) -> p v n", v=2)
        g_row, b_row = arena[:, 2 * D:3 * D], arena[:, 3 * D:4 * D]
        diag = arena[:, 4 * D:5 * D]
        full = arena[:, 4 * D:6 * D].rearrange("p (b n) -> p b n", b=2)
        next_gain = arena[:, 4 * D:5 * D]
        normed = [arena[:, D:2 * D], arena[:, 0:D]]
        v_tok = arena[:, :].rearrange("p (t n) -> p t n", t=2)
        wsT = side[:, 0:GROUPS * P]
        lnb_row, sum_row = side[:, 1024:1792], side[:, 1792:2048]

        mixbuf = modrow[:, :].rearrange("p (b n) -> p b n", b=2)

        def modv(layer, v):
            at = (layer * 9 + v) * DC * 2
            return modcol[:, at:at + DC * 2].rearrange("p (c v) -> p c v", v=2)

        landed = [sem(f"unit_landed{i}") for i in range(RING)]
        hi_ready, lo_ready, unit_used = sem("hi_ready"), sem("lo_ready"), sem("unit_used")
        names = """gate_ready hid_ready proj_ready vstat_ready modrow_ready modcol_ps modcol_ready
            hs_hi hs_lo y_ready diag_ready gate_ps gate_row_ready dve_step act_step pool_step
            var_ready std_ready norm_ready xT_half xT_ps affine_ready full_ready x_ready xres_ready coef_ready
            mix_ps mix_scaled mix_step mix_done v_normed rs_ps rs_ready value_ready qk_ready qkT_ps qkT_ready
            s_ps max_ready exp_ready p_ready pT_ps pT_ready o_ps o_ready
            ret_s_ps ret_s_ready ret_o_ps ret_ready silu_rg retT_ps
            z_ps negabs_ready log_ready stay_ready later_ps arg_ready a_exp a_ready ss_ready
            csil_ready cvec_ready out_ready""".split()
        S = {n: sem(n) for n in names}
        loads = {n: sem("loaded_" + n) for n in ("x", "consts", "cols", "gmlp", "rows", "attn", "hyb", "decay", "gain")}
        stored = sem("stored")

        class Tally:

            def __init__(self):
                self.n = {}

            def __call__(self, name, k=1):
                self.n[name] = self.n.get(name, 0) + k
                return self.n[name]

        class Chain:

            def __init__(self, eng, ended):
                self.eng, self.ended, self.n = eng, ended, 0

            def give(self, ins):
                self.n += 1
                ins.then_inc(self.ended, 1)

            def wait(self):
                self.eng.wait_ge(self.ended, self.n)

            def __call__(self, ins):
                self.give(ins)
                self.wait()

        def walk(eng, phase, visit):
            n0 = phase.first
            for trips, body in phase.rounds:
                def once(i):
                    for off, (kind, x, b) in enumerate(body):
                        visit(kind, x, x + b * i, n0 + off, i * (len(body) // RING), i)
                if trips == 1:
                    once(0)
                else:
                    assert len(body) % RING == 0
                    with eng.Fori(0, trips) as i:
                        once(i)
                n0 += trips * len(body)

        tiles_before, hs_before, groups_before = {}, {}, {}
        n_tiles = n_hs = n_groups = 0
        for p_ in phases:
            if p_.kind in ("ffn_in", "u"):
                tiles_before[p_.stage] = n_tiles
                n_tiles += FT if p_.kind == "ffn_in" else GT
            if p_.kind == "out":
                hs_before[p_.stage] = n_hs
                n_hs += OUT_K[p_.stage]
            if p_.kind in ("v", "proj"):
                groups_before[p_.first] = n_groups
                n_groups += GT // 4 if p_.kind == "v" else PROJ_GROUPS[STAGES[p_.stage]]
        mods_by, n_mods = {}, 0
        for p_ in phases:
            here = sum(trips * sum(k == "M" for k, _, _ in body) for trips, body in p_.rounds) // 4
            n_mods += here
            if here:
                mods_by[p_.stage] = n_mods
        hid_before, n_hid = {}, 0
        for s, kind in enumerate(STAGES):
            hid_before[s] = n_hid
            if kind == FFN:
                n_hid += FT

        o_before = {ATTN: 0, HYB: 8, SB: 8 + DIL_PAIRS}
        o_made = {ATTN: 8, HYB: 9 + DIL_PAIRS, SB: 17 + DIL_PAIRS}

        def with_gate(ph, idx):
            return ph.kind == "ffn_in" and ph.stage < N_MODULATED and isinstance(idx, int) and idx >= FT - 2

        def tokens(s):
            return TILES[s] * P

        def proj_dst(s):
            w = {HYB: 3584, SB: 3072}[STAGES[s]]
            return hidf[:, 0:2 * w].rearrange("p (t n) -> p t n", t=2)

        att = dict(
            q=Xf[:, 2048:4096].rearrange("p (t n) -> p t n", t=2),
            k=hidf[:, 0:1024].rearrange("p (t n) -> p t n", t=4),
            v=hidf[:, 1024:2048].rearrange("p (t n) -> p t n", t=4),
            qT=hidf[:, 2048:4096].rearrange("p (h n) -> p h n", h=8),
            kT=hidf[:, 4096:5120].rearrange("p (h n) -> p h n", h=2),
            P=hidf[:, 10240:12288].rearrange("p (b n) -> p b n", b=4),
            PT=hidf[:, 6144:8192].rearrange("p (b k n) -> p b k n", b=2, k=4),
            oT=hidf[:, 8192:10240].rearrange("p (c n) -> p c n", c=8),
            tmp=hidf[:, 10240:12288],
        )
        HW_ = 3584
        hyb = dict(
            qkT=hidf[:, 7168:11264].rearrange("p (c n) -> p c n", c=16),
            P=[hidf[:, 11264:11776], hidf[:, 11776:12288], arena[:, 4864:5376]],
            oT=arena[:, 0:2048].rearrange("p (c n) -> p c n", c=8),
            tmp=arena[:, 2048:4096],
            PT=arena[:, 2048:4096].rearrange("p (b k n) -> p b k n", b=2, k=4),
            St=arena[:, 4096:4864].rearrange("p (b n) -> p b n", b=2),
            gn=arena[:, 5376:5888],
            decay=Xf[:, 2048:4096].rearrange("p (h n) -> p h n", h=8),
            ret=hidf[:, 0:HW_ * 2].rearrange("p (t n) -> p t n", t=2)[:, :, 0:512],
            sq=hidf[:, 0:HW_ * 2].rearrange("p (t n) -> p t n", t=2)[:, :, 512:1024],
        )
        sbk = dict(
            qkT=hidf[:, 6144:10240].rearrange("p (c n) -> p c n", c=16),
            oT=hidf[:, 10240:12288].rearrange("p (c n) -> p c n", c=8),
            E=arena[:, 0:1536].rearrange("p (b h n) -> p b h n", b=2, h=2),
            LS=[part.rearrange("p (h n) -> p h n", h=2)
                for part in (arena[:, 1536:2304], arena[:, 2304:3072], hidf[:, 0:768])],
            ST=arena[:, 3072:4608].rearrange("p (b h n) -> p b h n", b=2, h=2),
            A=arena[:, 4608:6144].rearrange("p (b h n) -> p b h n", b=2, h=2),
        )
        T = dict(att_rope=side[:, 0:256].rearrange("p (k t n) -> p k t n", k=2, t=2),
                 qk_gain=side[:, 256:512].rearrange("p (k n) -> p k n", k=2),
                 ret_rope=side[:, 512:640].rearrange("p (k t n) -> p k t n", k=2, t=2),
                 dil_rope=side[:, 640:672].rearrange("p (k t n) -> p k t n", k=2, t=2),
                 bias=side[:, 672:928], causal=side[:, 928:1056], tri=side[:, 1056:1184])

        def out_source(s):
            return {ATTN: att["oT"], HYB: hyb["oT"], SB: sbk["oT"]}.get(STAGES[s])

        block = ctx.enter_context(nc.Block())

        @block.sync
        def _(sp):
            def load(kind, x, idx, n0, q, i):
                src = sources[kind]
                if n0 >= RING or not isinstance(q, int):
                    sp.wait_ge(lo_ready, n0 - RING + 1 + RING * q)
                sp.dma_start(w32[:, n0 % RING, :],
                             src[bass.ds(idx, 1), :, :].rearrange("o p n -> p (o n)")
                             ).then_inc(landed[n0 % RING], 16)

            sp.dma_start(cols[:, :], a["cols"]).then_inc(loads["cols"], 16)
            sp.dma_start(consts[:, :], a["consts"]).then_inc(loads["consts"], 16)
            ffn = 0
            for ph in phases:
                s = ph.stage
                sources = {"M": a["w_mod"]}
                if ph.kind == "ffn_in":
                    sources["G"], sources["U"] = a["ffn_gate"][ffn], a["ffn_up"][ffn]
                elif ph.kind == "u":
                    sources["F"] = a["gmlp_u"]
                elif ph.kind == "v":
                    sources["B"] = a["gmlp_v"]
                elif ph.kind == "proj":
                    sources["B"] = a[STAGES[s] + "_in"]
                elif ph.kind in ("out", "tail"):
                    sources["O"] = a["ffn_out"][ffn] if STAGES[s] == FFN else a[STAGES[s] + "_out"]
                    ffn += ph.kind == "tail" and STAGES[s] == FFN
                walk(sp, ph, load)

        @block.gpsimd
        def _(pool):
            chain = Chain(pool, S["pool_step"])
            pool.wait_ge(S["modrow_ready"], 1)
            pool.dma_start(X[:, 0:2, :], a["x"]).then_inc(loads["x"], 16)
            pool.dma_start(X[:, 2:4, :], a["ctx"]).then_inc(loads["x"], 16)
            pool.dma_start(wsT, a["wsT"]).then_inc(loads["gmlp"], 16)
            chain(nc.gpsimd.memset(side[:, 1024:2048], 1.0))
            for i in range(4):
                pool.dma_start(lnb_row[32 * i:32 * i + 1, :], a["gmlp_ln_b"][i:i + 1, :]).then_inc(loads["gmlp"], 16)
                pool.dma_start(sum_row[32 * i + 1:32 * i + 2, :], a["gmlp_b_s"][i:i + 1, :]).then_inc(loads["gmlp"], 16)
            done = Tally()
            for s in range(N_MODULATED):
                pool.wait_ge(S["gate_row_ready"], done("gate_row", 2 if TILES[s] == 4 else 1))
                if s == 1:
                    pool.wait_ge(S["mix_done"], 2 * GT)
                    pool.dma_start(side[:, 0:256], a["att_rope"]).then_inc(loads["attn"], 16)
                    for k, g in enumerate(("q_norm", "k_norm")):
                        pool.dma_start(T["qk_gain"][:, k, :], a[g].to_broadcast((P, P))).then_inc(loads["attn"], 16)
                    pool.dma_start(side[:, 512:1184], a["tables"]).then_inc(loads["hyb"], 16)
                pool.dma_start(g_row, a["ln_g"][s:s + 1, :].to_broadcast((P, D))).then_inc(loads["rows"], 16)
                pool.dma_start(b_row, a["ln_b"][s:s + 1, :].to_broadcast((P, D))).then_inc(loads["rows"], 16)
                if s == 5:
                    continue
                pool.wait_ge(loads["rows"], 32 * (s + 1))
                for t in range(4 if s < 3 else 2):
                    pool.wait_ge(S["xT_ps"], tiles_ready(s) + t + 1)
                    chain(nc.gpsimd.tensor_tensor(X[:, t, :], X[:, t, :], g_row, MUL))
                    nc.gpsimd.tensor_tensor(X[:, t, :], X[:, t, :], b_row, ADD).then_inc(S["xres_ready"], 1)
                pool.wait_ge(S["xres_ready"], 4 * min(s + 1, 3) + 2 * max(0, s - 2))
            for s in range(5, len(STAGES)):
                if s > 5:
                    pool.wait_ge(S["norm_ready"], tiles_ready(s) - 4)
                if STAGES[s] in o_made:
                    pool.wait_ge(S["o_ready"], o_made[STAGES[s]])
                gain = a["norm_rows"][s - 5:s - 4, :]
                pool.dma_start(next_gain, gain.to_broadcast((P, D))).then_inc(loads["gain"], 16)
                if s == 5:
                    pool.wait_ge(S["norm_ready"], tiles_ready(6) - 4)
                    pool.dma_start(hyb["decay"], a["decay"]).then_inc(loads["decay"], 16)
                if s == 6:
                    pool.wait_ge(S["x_ready"], tiles_ready(7))
                    pool.dma_start(hyb["gn"], a["ret_gn"].to_broadcast((P, 512))).then_inc(loads["decay"], 16)
            for t in range(2):
                pool.wait_ge(S["out_ready"], t + 1)
                pool.dma_start(a["out"][:, t, :], X[:, t, :]).then_inc(stored, 16)
            pool.wait_ge(stored, 32)

        @block.scalar
        def _(act):
            seen = Tally()
            ident_f = ACT.Identity

            def split_hi(n0, q):
                if isinstance(q, int) and n0 >= n_units:
                    return
                act.wait_ge(landed[n0 % RING], 16 * (n0 // RING + 1) + 16 * q)
                if n0 >= RING or not isinstance(q, int):
                    act.wait_ge(unit_used, n0 - RING + 1 + RING * q)
                nc.scalar.copy(whi[:, n0 % RING, :], w32[:, n0 % RING, :]).then_inc(hi_ready, 1)

            def hs_hi(s, src, k, x):
                n = tokens(s)
                nc.scalar.copy(hs[:, x % RING, 0, 0:n], src(k)).then_inc(S["hs_hi"], 1)

            def transposed(t, modulated, shared):
                n = seen("tile")
                bank = ps[:, 2 * t:2 * t + 2, :].rearrange("p b (c n) -> p (b c) n", n=P)
                high = xhi[:, :, t * P:(t + 1) * P]
                f = full[:, n % 2, :].rearrange("p (c n) -> p c n", n=P)
                if shared:
                    act.wait_ge(S["xT_half"], seen("half"))
                else:
                    act.wait_ge(S["xT_ps"], n)
                if modulated:
                    if n > 2:
                        act.wait_ge(S["x_ready"], n - 2)
                    for c in range(DC // 2 if shared else DC):
                        ins = nc.scalar.activation(f[:, c, :], bank[:, c, :], ident_f,
                                                   scale=coef[:, 0, c, t // 2:t // 2 + 1], bias=coef[:, 1, c, t // 2:t // 2 + 1])
                    ins.then_inc(S["act_step"], 1)
                    act.wait_ge(S["act_step"], seen("act_step"))
                src = f if modulated else bank
                if not shared:
                    nc.scalar.copy(high, src).then_inc(S["full_ready"], 1)
                    return
                nc.scalar.copy(high[:, 0:4, :], src[:, 0:4, :]).then_inc(S["full_ready"], 1)
                if modulated:
                    act.wait_ge(S["affine_ready"], seen("affine"))
                else:
                    act.wait_ge(S["xT_ps"], n)
                nc.scalar.copy(high[:, 4:8, :], src[:, 4:8, :]).then_inc(S["full_ready"], 1)

            def sqrt(dst, src, scale, eps):
                act.wait_ge(S["var_ready"], seen("var_ready"))
                nc.scalar.activation(dst, src, ACT.Sqrt, bias=eps, scale=scale).then_inc(S["std_ready"], 1)

            def gate(s, v):
                if v < GATES[s]:
                    act.wait_ge(S["gate_ps"], seen("gate_ps"))
                    b = GATE_BANKS[v]
                    nc.scalar.activation(gate_row[:, v, :].rearrange("p (h n) -> p h n", h=2), ps[:, b:b + 2, :],
                                         ACT.Copy, scale=0.5 if STAGES[s] == FFN else 1.0
                                         ).then_inc(S["gate_row_ready"], 1)

            def half_squares(t):
                act.wait_ge(S["ss_ready"], seen("ss_ready"))
                nc.scalar.activation(normed[t][:, 0:512], X[:, t, 0:512], ACT.Square,
                                     accum_out=stat[:, 4:5]).then_inc(S["act_step"], 1)
                act.wait_ge(S["act_step"], seen("act_step"))
                nc.scalar.activation(stat[:, 5:6], stat[:, 4:5], ident_f, bias=consts[:, 260:261],
                                     scale=1.0 / D).then_inc(S["act_step"], 1)
                seen("act_step")

            def root_mean_square(t, last):
                at, bias = (512, stat[:, 5:6]) if last else (0, consts[:, 260:261])
                act.wait_ge(S["ss_ready"], seen("ss_ready"))
                nc.scalar.activation(normed[t][:, at:D], X[:, t, at:D], ACT.Square,
                                     accum_out=stat[:, t:t + 1]).then_inc(S["act_step"], 1)
                act.wait_ge(S["act_step"], seen("act_step"))
                nc.scalar.activation(std[:, 8 + t:9 + t], stat[:, t:t + 1], ACT.Sqrt, bias=bias,
                                     scale=1.0 / D).then_inc(S["std_ready"], 1)

            def epilogue(s, first):
                n = TILES[s]
                early = s < 11 and STAGES[s + 1] in EARLY
                for t in range(n):
                    last = t == n - 1
                    if last and early:
                        for k in range(AHEAD):
                            split_hi(first + k, 0)
                    if last and s >= N_MODULATED:
                        half_squares(t)
                    if 0 < t and s < 11:
                        transposed(t - 1, s < 5, False)
                    if s < N_MODULATED:
                        sqrt(std[:, t:t + 1], mv[:, t, 1:2], 1.0, consts[:, 261:262])
                    if last and s == N_MODULATED - 1:
                        half_squares(t)
                    if s >= N_MODULATED - 1:
                        root_mean_square(t, last)
                if not early:
                    for k in range(2):
                        split_hi(first + k, 0)
                    if s < 11:
                        transposed(n - 1, s < 5, True)
                    for k in range(2, AHEAD):
                        split_hi(first + k, 0)
                table = {GMLP: ACT.Gelu}.get(STAGES[min(s + 1, 11)], ACT.Silu)
                nc.scalar.activation(std[:, 63:64], consts[:, 260:261], table).then_inc(S["act_step"], 1)
                seen("act_step")

            def mix(vec):
                for c in range(GT):
                    i = GT * vec + c
                    act.wait_ge(S["mix_ps"], i + 1)
                    if i >= 2:
                        act.wait_ge(S["mix_done"], i - 1)
                    nc.scalar.activation(mixbuf[:, c % 2, :], ps[:, 4 + c % 4, 0:256], ACT.Copy,
                                         scale=gmg[:, c:c + 1]).then_inc(S["mix_scaled"], 1)

            def attention():
                for part, src in ((att["qT"].rearrange("p (b h) n -> p b (h n)", b=4), ps[:, 0:4, :]),
                                  (att["kT"], ps[:, 4:6, :])):
                    act.wait_ge(S["qkT_ps"], seen("qkT_ps"))
                    nc.scalar.copy(part, src).then_inc(S["qkT_ready"], 1)

                def exp(i):
                    act.wait_ge(S["max_ready"], i + 1)
                    if i >= 4:
                        act.wait_ge(S["pT_ps"], i - 3)
                    nc.scalar.activation(att["P"][:, i % 4, :], ps[:, SCORE_BANKS[i % 4], :], ACT.Exp, bias=mx[:, i:i + 1],
                                         scale=P ** -0.5, accum_out=den[:, i:i + 1]).then_inc(S["exp_ready"], 1)

                exp(0)
                exp(1)
                for i in range(16):
                    h, t = divmod(i, 2)
                    if i < 14:
                        exp(i + 2)
                    act.wait_ge(S["pT_ps"], i + 1)
                    if t == 0 and h >= 2:
                        act.wait_ge(S["o_ps"], h - 1)
                    nc.scalar.copy(att["PT"][:, h % 2, :, t * P:(t + 1) * P],
                                   ps[:, 2 + i % 2, :].rearrange("p (k n) -> p k n", k=4)).then_inc(S["pT_ready"], 1)
                    if t == 1:
                        act.wait_ge(S["o_ps"], h + 1)
                        nc.scalar.copy(att["oT"][:, h, :], ps[:, 4 + h % 2, 0:256]).then_inc(S["o_ready"], 1)

            def qk_transposed(dst):
                for half, bank in enumerate((4, 0)):
                    act.wait_ge(S["qkT_ps"], seen("qkT_ps"))
                    nc.scalar.copy(dst[:, 8 * half:8 * half + 8, :].rearrange("p (b h) n -> p b (h n)", b=4),
                                   ps[:, bank:bank + 4, :]).then_inc(S["qkT_ready"], 1)

            def hybrid():
                qk_transposed(hyb["qkT"])

                def exp(j):
                    g, t = divmod(j, 2)
                    act.wait_ge(S["max_ready"], 16 + j + 1)
                    n = P * (t + 1)
                    for h in range(2):
                        part, at = hyb["P"][j % 3][:, n * h:n * h + n], 2 * j + h
                        ins = nc.scalar.activation(part, part, ACT.Exp, bias=mx[:, at:at + 1], scale=0.125,
                                                   accum_out=den[:, at:at + 1])
                    ins.then_inc(S["exp_ready"], 1)

                exp(0)
                exp(1)
                for j in range(2 * DIL_PAIRS):
                    g, t = divmod(j, 2)
                    if j == 1:
                        sqrt(std[:, 0:16], stat[:, 16:32], 1.0 / 64, consts[:, 261:262])
                    if j < 2 * DIL_PAIRS - 2:
                        exp(j + 2)
                    act.wait_ge(S["pT_ps"], 16 + j + 1)
                    if t == 0 and g >= 2:
                        act.wait_ge(S["o_ps"], o_before[HYB] + g - 1)
                    dst = hyb["PT"][:, g % 2, :, P:256] if t else hyb["PT"][:, g % 2, 0:4:2, 0:P]
                    nc.scalar.copy(dst, ps[:, 4 + j % 2, 0:256 * (t + 1)].rearrange("p (k n) -> p k n", n=P)
                                   ).then_inc(S["pT_ready"], 1)
                    if t == 1:
                        if g == DIL_PAIRS - 1:
                            act.wait_ge(S["retT_ps"], 1)
                            nc.scalar.copy(hyb["oT"][:, 0:4, :].rearrange("p (b h) n -> p b (h n)", b=2), ps[:, 0:2, :]
                                           ).then_inc(S["o_ready"], 1)
                        act.wait_ge(S["o_ps"], o_before[HYB] + g + 1)
                        nc.scalar.copy(hyb["oT"][:, 4 + g, :], ps[:, 6 + g % 2, 0:256]
                                       ).then_inc(S["o_ready"], 1)

            def stick_breaking():
                qk_transposed(sbk["qkT"])

                def logs(g):
                    act.wait_ge(S["negabs_ready"], g + 1)
                    E_ = sbk["E"][:, g % 2]
                    nc.scalar.activation(E_, E_, ACT.Exp).then_inc(S["act_step"], 1)
                    act.wait_ge(S["act_step"], seen("act_step"))
                    nc.scalar.activation(E_, E_, ACT.Ln, bias=1.0).then_inc(S["log_ready"], 1)

                def output(g):
                    act.wait_ge(S["o_ps"], o_before[SB] + g + 1)
                    nc.scalar.copy(sbk["oT"][:, g, :], ps[:, 4 + g % 2, 0:256]).then_inc(S["o_ready"], 1)

                logs(0)
                logs(1)
                for g in range(8):
                    if g < 6:
                        logs(g + 2)
                    act.wait_ge(S["arg_ready"], g + 1)
                    A_ = sbk["A"][:, g % 2]
                    nc.scalar.activation(A_, A_, ACT.Exp).then_inc(S["a_exp"], 1)
                    if g:
                        output(g - 1)
                output(7)

            act.wait_ge(loads["cols"], 16)
            nc.scalar.activation(csil[:, :, :], c_col, ACT.Silu).then_inc(S["csil_ready"], 1)
            act.wait_ge(loads["consts"], 16)
            for n in range(AHEAD):
                split_hi(n, 0)
            for ph in phases:
                s = ph.stage
                N = tokens(s)

                def mod_row(ch, n0, q):
                    act.wait_ge(unit_used, n0 + 1 + RING * q)
                    if not isinstance(ch, int) or ch > 0:
                        act.wait_ge(S["modcol_ps"], ch)
                    nc.scalar.copy(modrow[:, :], ps[:, 4, :]).then_inc(S["modrow_ready"], 1)

                if ph.kind == "mod":
                    def visit(kind, x, idx, n0, q, i):
                        split_hi(n0 + AHEAD, q)
                        if x % 4 == 3:
                            mod_row(x // 4 + i, n0, q)
                    walk(act, ph, visit)
                    for t in range(4):
                        transposed(t, True, True)
                elif ph.kind in ("ffn_in", "u"):
                    func = ACT.Silu if ph.kind == "ffn_in" else ACT.Gelu

                    def visit(kind, x, idx, n0, q, i):
                        split_hi(n0 + AHEAD, q)
                        if kind in "GF":
                            act.wait_ge(unit_used, n0 + 1 + RING * q)
                            nc.scalar.activation(hidf[:, bass.ds(idx * TOK, N)], ps[:, x % 2, 0:N],
                                                 func).then_inc(S["gate_ready"], 1)
                        elif kind == "M" and x % 4 == 3:
                            mod_row(x // 4 + i, n0, q)
                        if with_gate(ph, idx):
                            if (kind, idx) == ("G", FT - 1):
                                gate(s, 0)
                            if (kind, idx) == ("U", FT - 1):
                                gate(s, 1)
                    walk(act, ph, visit)
                    if ph.kind == "u":
                        mix(LAT)
                elif ph.kind in ("v", "proj"):
                    kind_ = STAGES[s]
                    base = groups_before[ph.first]

                    def visit(kind, x, idx, n0, q, i):
                        split_hi(n0 + AHEAD, q)
                        if ph.more.get("vec", LAT) == LAT and kind_ in EARLY and isinstance(idx, int):
                            if idx == LAST_TILE_UNIT:
                                transposed(TILES[s - 1] - 1, True, True)
                            if idx == 3:
                                act.wait_ge(S["x_ready"], tiles_ready(s))
                                act.wait_ge(S["xres_ready"], 4 * min(s, 3))
                        if kind_ == ATTN and idx == 9:
                            sqrt(std[:, 0:16], stat[:, 0:16], 1.0 / P, consts[:, 260:261])
                        if kind_ == HYB and isinstance(idx, int) and idx == 22:
                            act.wait_ge(S["proj_ready"], base + 4)
                            rg = proj_dst(s)[:, :, 1536:2048]
                            nc.scalar.activation(rg, rg, ACT.Silu).then_inc(S["silu_rg"], 1)
                        if x % 4 != 3:
                            return
                        g = x // 4
                        act.wait_ge(unit_used, n0 + 1 + RING * q)
                        if kind_ == ATTN:
                            if g < 2:
                                dst, src = att["q"][:, :, 512 * g:512 * g + 512], ps[:, 2 * g:2 * g + 2, :]
                            else:
                                dst, src = att["k"], ps[:, 4:8, 0:256]
                        else:
                            b = 2 * (g % 2)
                            to = v_tok if kind_ == GMLP else proj_dst(s)
                            dst, src = to[:, :, bass.ds((idx - 3) * 128, 512)], ps[:, b:b + 2, :]
                        nc.scalar.activation(dst, src, ACT.Gelu if kind_ == GMLP else ACT.Copy
                                             ).then_inc(S["proj_ready"], 1)
                    walk(act, ph, visit)
                    if ph.kind == "v" and ph.more["vec"] == LAT:
                        act.wait_ge(S["rs_ps"], 1)
                        for i in range(4):
                            nc.scalar.copy(sum_row[32 * i:32 * i + 1, :], ps[32 * i:32 * i + 1, 7, 0:256]
                                           ).then_inc(S["rs_ready"], 1)
                    if ph.kind == "v":
                        sqrt(std[:, 0:2], mv[:, 0:2, 1], 1.0, consts[:, 261:262])
                        if ph.more["vec"] == CTX:
                            mix(CTX)
                    if kind_ == ATTN:
                        nc.scalar.copy(att["v"], ps[:, 4:8, 256:512]).then_inc(S["value_ready"], 1)
                        sqrt(std[:, 16:24], stat[:, 16:24], 1.0 / P, consts[:, 260:261])
                        attention()
                    if kind_ == HYB:
                        hybrid()
                    if kind_ == SB:
                        stick_breaking()
                elif ph.kind == "out":
                    if s < N_MODULATED and STAGES[s] != FFN:
                        for v in range(2):
                            gate(s, v)
                    K = OUT_K[s]
                    src_ap = out_source(s)
                    if STAGES[s] == FFN:
                        act.wait_ge(S["hid_ready"], hid_before[s] + FT)
                        src = lambda k: hidf[:, bass.ds(k * TOK, N)]
                    elif STAGES[s] == GMLP:
                        act.wait_ge(S["mix_done"], 2 * GT)
                        src = lambda k: hidf[:, bass.ds(k * TOK, N)]
                    else:
                        act.wait_ge(S["o_ready"], o_made[STAGES[s]])
                        src = lambda k: src_ap[:, k, :]
                    for k in range(AHEAD):
                        hs_hi(s, src, k, k)

                    def visit(kind, x, idx, n0, q, i):
                        split_hi(n0 + AHEAD, q)
                        hs_hi(s, src, idx + AHEAD, x + AHEAD)
                    walk(act, ph, visit)
                elif ph.kind == "tail":
                    k = OUT_K[s] - 1
                    split_hi(ph.first + RING - 1, 0)
                    hs_hi(s, src, k, k)
                    nc.scalar.activation(std[:, 62:63], consts[:, 260:261], ACT.Sqrt).then_inc(S["act_step"], 1)
                    act.wait_ge(S["act_step"], seen("act_step"))
                    epilogue(s, ph.first + ph.units)

        @block.vector
        def _(dve):
            seen = Tally()
            chain = Chain(dve, S["dve_step"])
            V = nc.vector

            def split_lo(n0, q):
                if isinstance(q, int) and n0 >= n_units:
                    return
                dve.wait_ge(hi_ready, n0 + 1 + RING * q)
                V.tensor_tensor(wlo[:, n0 % RING, :], w32[:, n0 % RING, :], whi[:, n0 % RING, :], SUB
                                ).then_inc(lo_ready, 1)

            def hs_lo(s, src, k, x, count):
                n = tokens(s)
                dve.wait_ge(S["hs_hi"], count)
                V.tensor_tensor(hs[:, x % RING, 1, 0:n], src(k), hs[:, x % RING, 0, 0:n], SUB).then_inc(S["hs_lo"], 1)

            def split_x(t, modulated, shared):
                n = seen("tile")
                bank = ps[:, 2 * t:2 * t + 2, :].rearrange("p b (c n) -> p (b c) n", n=P)
                f = full[:, n % 2, :].rearrange("p (c n) -> p c n", n=P) if modulated else bank
                if shared and modulated:
                    dve.wait_ge(S["xT_ps"], n)
                    if n > 2:
                        dve.wait_ge(S["x_ready"], n - 2)
                    for c in range(4, DC):
                        ins = V.tensor_scalar(f[:, c, :], bank[:, c, :], coef[:, 0, c, t // 2:t // 2 + 1],
                                              coef[:, 1, c, t // 2:t // 2 + 1], MUL, ADD)
                    ins.then_inc(S["affine_ready"], 1)
                r = slice(t * P, (t + 1) * P)
                for c in ((slice(0, 4), slice(4, 8)) if shared else (slice(0, 8),)):
                    dve.wait_ge(S["full_ready"], seen("full"))
                    ins = V.tensor_tensor(xlo[:, c, r], f[:, c, :], xhi[:, c, r], SUB)
                ins.then_inc(S["x_ready"], 1)

            def invert_std(n, at=0):
                dve.wait_ge(S["std_ready"], seen("std_ready"))
                chain(V.reciprocal(rstd[:, at:at + n], std[:, at:at + n]))

            def coefficients(s):
                layer, i = divmod(s + 1, 3)
                shift, scale = modv(layer, 3 * i), modv(layer, 3 * i + 1)
                dve.wait_ge(S["modcol_ready"], layer * 18 + 2 * (3 * i + 1) + 2)
                A_, B_ = coef[:, 0, :, :], coef[:, 1, :, :]
                if s < 0:
                    V.tensor_scalar(A_, scale, 1.0, None, ADD)
                    chain(V.tensor_copy(B_, shift))
                    return
                one = coef[:, 2, :, :]
                g = lng[:, s, :].unsqueeze(2).to_broadcast((P, DC, 2))
                b = lnb[:, s, :].unsqueeze(2).to_broadcast((P, DC, 2))
                chain(V.tensor_scalar(one, scale, 1.0, None, ADD))
                chain(V.tensor_tensor(A_, one, g, MUL))
                chain(V.tensor_tensor(B_, one, b, MUL))
                chain(V.tensor_tensor(B_, B_, shift, ADD))

            def gate(s, v):
                layer, i = divmod(s, 3)
                gate = modv(layer, 3 * i + 2)
                if v < GATES[s]:
                    if v:
                        dve.wait_ge(S["gate_ps"], seen.n["gate_ps"])
                    else:
                        dve.wait_ge(S["modcol_ready"], layer * 18 + 2 * (3 * i + 2) + 2)
                    seen("gate_ps")
                    V.tensor_tensor(diag.rearrange("p (c n) -> p c n", c=DC),
                                    ident.unsqueeze(1).to_broadcast((P, DC, P)),
                                    gate[:, :, v:v + 1].to_broadcast((P, DC, P)), MUL).then_inc(S["diag_ready"], 1)

            last_unit = {ph.stage: ph.first + ph.units for ph in phases if ph.kind == "tail"}

            def y_parts(s, t):
                n = TILES[s]
                dve.wait_ge(S["y_ready"], seen("y_ready"))
                if t < n - 1:
                    yield ps[:, 2 * t:2 * t + 2, :], slice(0, D)
                    return
                yield ps[:, 2 * t:2 * t + 1, :], slice(0, 512)
                dve.wait_ge(unit_used, last_unit[s])
                yield ps[:, 2 * t + 1:2 * t + 2, :], slice(512, D)

            def residual_norm(s, t):
                for y, w in y_parts(s, t):
                    Xt = X[:, t, w].rearrange("p (h n) -> p h n", n=512)
                    chain(V.tensor_tensor(y, y, gate_row[:, t // 2, w].rearrange("p (h n) -> p h n", n=512), MUL))
                    chain(V.scalar_tensor_tensor(Xt, Xt, ALPHA, y, MUL, ADD))
                    for h in range(w.start // 512, w.stop // 512):
                        chain.give(V.bn_stats(bnst[:, t, h, :], X[:, t, 512 * h:512 * h + 512]))
                chain.wait()
                V.bn_aggr(mv[:, t, :], bnst[:, t, 0:2, :]).then_inc(S["var_ready"], 1)
                invert_std(1, t)
                if s < 5:
                    V.tensor_scalar(X[:, t, :], X[:, t, :], mv[:, t, 0:1], rstd[:, t:t + 1], SUB, MUL
                                    ).then_inc(S["norm_ready"], 1)
                    return
                dve.wait_ge(loads["rows"], 32 * 6)
                for w in ((slice(0, 512), slice(512, D)) if t == TILES[s] - 1 else (slice(0, D),)):
                    chain(V.tensor_scalar(X[:, t, w], X[:, t, w], mv[:, t, 0:1], rstd[:, t:t + 1], SUB, MUL))
                    chain(V.tensor_tensor(X[:, t, w], X[:, t, w], g_row[:, w], MUL))
                    V.tensor_tensor(X[:, t, w], X[:, t, w], b_row[:, w], ADD).then_inc(S["ss_ready"], 1)

            def epilogue(s, first):
                n = TILES[s]
                if s < N_MODULATED:
                    if s < 5:
                        coefficients(s)
                    dve.wait_ge(S["gate_row_ready"], seen("gate_row", 2 if n == 4 else 1))
                    if s > 0:
                        dve.wait_ge(S["xres_ready"], 4 * min(s, 3) + 2 * max(0, s - 3))
                early = s < 11 and STAGES[s + 1] in EARLY

                def residual(parts, count):
                    for _ in range(count):
                        t, y, w = next(parts)
                        Xt = X[:, t, w].rearrange("p (h n) -> p h n", n=512)
                        V.scalar_tensor_tensor(Xt, y, 0.5 if STAGES[s] == FFN else 1.0, Xt, MUL, ADD
                                               ).then_inc(S["ss_ready"], 1)

                def rms_apply(t, count):
                    dve.wait_ge(S["ss_ready"], seen("ss", count))
                    invert_std(1, 8 + t)
                    if t == 0:
                        dve.wait_ge(loads["gain"], 16 * (s - 4))
                    dst = normed[t] if s < 11 else X[:, t, :]
                    V.scalar_tensor_tensor(dst, X[:, t, :], rstd[:, 8 + t:9 + t], next_gain, MUL, MUL
                                           ).then_inc(S["norm_ready" if s < 11 else "out_ready"], 1)

                if s < N_MODULATED:
                    for t in range(n):
                        if t == n - 1 and early:
                            for k in range(AHEAD):
                                split_lo(first + k, 0)
                        residual_norm(s, t)
                        if t and s == 5:
                            split_x(t - 1, False, False)
                        if s == 5:
                            rms_apply(t, t + 1)
                        if t and s < 5:
                            split_x(t - 1, True, False)
                else:
                    parts = ((t, y, w) for t in range(n) for y, w in y_parts(s, t))
                    residual(parts, 2)
                    rms_apply(0, 2)
                    residual(parts, 1)
                    if s < 11:
                        split_x(0, False, False)
                    rms_apply(1, 1)
                if not early:
                    split_lo(first, 0)
                    if s < 11:
                        split_x(n - 1, s < 5, True)
                    for k in range(1, AHEAD):
                        split_lo(first + k, 0)

            def rope(x1, x2, cos, sin, tmp, heads, half):
                c = cos.unsqueeze(1).to_broadcast((P, heads, half))
                s_ = sin.unsqueeze(1).to_broadcast((P, heads, half))
                w = heads * half
                t4 = [tmp[:, k * w:(k + 1) * w].rearrange("p (h n) -> p h n", h=heads) for k in range(4)]
                for dst, x, table in zip(t4, (x1, x2, x2, x1), (c, s_, c, s_)):
                    chain.give(V.tensor_tensor(dst, x, table, MUL))
                chain.wait()
                chain.give(V.tensor_tensor(x1, t4[0], t4[1], SUB))
                ins = V.tensor_tensor(x2, t4[2], t4[3], ADD)
                chain(ins)

            def head_squares(v, at):
                sq = att["tmp"][:, 0:1024].rearrange("p (h n) -> p h n", n=P)
                chain(V.tensor_tensor(sq, v, v, MUL))
                return V.tensor_reduce(stat[:, at:at + 8], sq, AX.X, ADD)

            def head_norm(v, at, gain):
                chain(V.tensor_tensor(v, v, rstd[:, at:at + 8].unsqueeze(2).to_broadcast((P, 8, P)), MUL))
                chain(V.tensor_tensor(v, v, gain.unsqueeze(1).to_broadcast((P, 8, P)), MUL))

            def attention_rope(v, heads, t):
                rope(v[:, :, 0:64], v[:, :, 64:128], T["att_rope"][:, 0, t, :], T["att_rope"][:, 1, t, :],
                     att["tmp"], heads, 64)

            def qk_given():
                V.tensor_copy(mx[:, 0:1], rstd[:, 0:1]).then_inc(S["qk_ready"], 1)
                dve.wait_ge(S["qk_ready"], seen("qk"))

            def attention_queries(unit, base):
                q = [att["q"][:, t, :].rearrange("p (h n) -> p h n", n=P) for t in range(2)]
                if unit == 8:
                    dve.wait_ge(loads["attn"], 48)
                    dve.wait_ge(S["proj_ready"], base + 2)
                    chain(head_squares(q[0], 0))
                    head_squares(q[1], 8).then_inc(S["var_ready"], 1)
                elif unit == 9:
                    invert_std(16)
                    for t in range(2):
                        head_norm(q[t], 8 * t, T["qk_gain"][:, 0, :])
                elif unit >= 10:
                    attention_rope(q[unit - 10], 8, unit - 10)
                if unit == 11:
                    qk_given()

            def attention():
                k = att["k"].rearrange("p t (h n) -> p (t h) n", n=P)
                head_squares(k, 16).then_inc(S["var_ready"], 1)
                invert_std(8, 16)
                head_norm(k, 16, T["qk_gain"][:, 1, :])
                for t in range(2):
                    attention_rope(k[:, 2 * t:2 * t + 2, :], 2, t)
                qk_given()

                def top(i):
                    dve.wait_ge(S["s_ps"], i + 1)
                    chain(V.reduce_max(mx[:, i:i + 1], ps[:, SCORE_BANKS[i % 4], :], AX.X))
                    V.tensor_scalar(mx[:, i:i + 1], mx[:, i:i + 1], -(P ** -0.5), None, MUL).then_inc(S["max_ready"], 1)

                top(0)
                top(1)
                for i in range(16):
                    if i < 14:
                        top(i + 2)
                    dve.wait_ge(S["exp_ready"], i + 1)
                    chain(V.reciprocal(rden[:, i:i + 1], den[:, i:i + 1]))
                    Pi = att["P"][:, i % 4, :]
                    V.tensor_scalar(Pi, Pi, rden[:, i:i + 1], None, MUL).then_inc(S["p_ready"], 1)

            def hybrid_positions(unit, base):
                pr = proj_dst(7)
                for units, groups, at, table, half in (((17, 20), 2, 0, T["ret_rope"], 32), ((25, 26), 6, 2048, T["dil_rope"], 8)):
                    if unit in units:
                        t = units.index(unit)
                        dve.wait_ge(loads["hyb"], 16)
                        dve.wait_ge(S["proj_ready"], base + groups)
                        v = pr[:, t, at:at + 1024].rearrange("p (h n) -> p h n", n=64)
                        rope(v[:, :, 0:half], v[:, :, half:2 * half], table[:, 0, t, :], table[:, 1, t, :], hyb["tmp"], 16, half)
                        if t:
                            qk_given()

            def hybrid():
                pr = proj_dst(7)
                dve.wait_ge(loads["decay"], 32)
                for h in range(8):
                    dve.wait_ge(S["ret_s_ps"], h + 1)
                    if h >= 2:
                        dve.wait_ge(S["ret_o_ps"], h - 1)
                    St, dec = hyb["St"][:, h % 2, :], hyb["decay"][:, h, :]
                    chain.give(V.tensor_tensor(St[:, 0:256], ps[:, h % 2, 0:256], dec, MUL))
                    V.tensor_tensor(St[:, 256:384], ps[:, h % 2, 256:384], dec[:, 0:P], MUL).then_inc(S["ret_s_ready"], 1)
                o = ps[:, 6:8, :].rearrange("p t (h n) -> p t h n", n=64)
                ret = hyb["ret"].rearrange("p t (h n) -> p t h n", n=64)
                sq = hyb["sq"].rearrange("p t (h n) -> p t h n", n=64)
                mean = stat[:, 0:16].rearrange("p (t h) -> p t h", t=2)
                var = stat[:, 16:32].rearrange("p (t h) -> p t h", t=2)

                def each(f):
                    for t in range(2):
                        chain.give(f(t))
                    chain.wait()

                def retention_norm(part):
                    rt = hyb["ret"]
                    if part == 0:
                        dve.wait_ge(S["ret_o_ps"], 8)
                        chain(V.tensor_reduce(mean, o, AX.X, ADD))
                        chain(V.tensor_scalar(mean, mean, 1.0 / 64, None, MUL))
                        each(lambda t: V.tensor_tensor(ret[:, t], o[:, t], mean[:, t].unsqueeze(2).to_broadcast((P, 8, 64)), SUB))
                    elif part == 1:
                        each(lambda t: V.tensor_tensor(sq[:, t], ret[:, t], ret[:, t], MUL))
                        V.tensor_reduce(var, sq, AX.X, ADD).then_inc(S["var_ready"], 1)
                    elif part == 2:
                        invert_std(16)
                        r = rstd[:, 0:16].rearrange("p (t h) -> p t h", t=2)
                        each(lambda t: V.tensor_tensor(ret[:, t], ret[:, t], r[:, t].unsqueeze(2).to_broadcast((P, 8, 64)), MUL))
                    elif part == 3:
                        each(lambda t: V.tensor_tensor(rt[:, t], rt[:, t], hyb["gn"], MUL))
                    elif part == 4:
                        dve.wait_ge(S["silu_rg"], 1)
                        for t in range(2):
                            V.tensor_tensor(rt[:, t], rt[:, t], pr[:, t, 1536:2048], MUL).then_inc(S["ret_ready"], 1)

                def weights(j):
                    n = P * (j % 2 + 1)
                    return hyb["P"][j % 3][:, 0:2 * n].rearrange("p (h n) -> p h n", h=2), n

                def top(j):
                    dve.wait_ge(S["s_ps"], 16 + j + 1)
                    if j >= 3:
                        dve.wait_ge(S["pT_ps"], 16 + j - 2)
                    Pj, n = weights(j)
                    m, mj = T["bias"][:, 256 - n:256].unsqueeze(1).to_broadcast((P, 2, n)), mx[:, 2 * j:2 * j + 2]
                    b = 2 * (j % 2)
                    chain(V.tensor_tensor(Pj, ps[:, b:b + 2, 0:n], m, ADD))
                    chain(V.reduce_max(mj, Pj, AX.X))
                    V.tensor_scalar(mj, mj, -0.125, None, MUL).then_inc(S["max_ready"], 1)

                top(0)
                top(1)
                for j in range(2 * DIL_PAIRS):
                    retention_norm(j)
                    if j < 2 * DIL_PAIRS - 2:
                        top(j + 2)
                    Pj, n = weights(j)
                    rj = rden[:, 2 * j:2 * j + 2]
                    dve.wait_ge(S["exp_ready"], 16 + j + 1)
                    chain(V.reciprocal(rj, den[:, 2 * j:2 * j + 2]))
                    V.tensor_tensor(Pj, Pj, rj.unsqueeze(2).to_broadcast((P, 2, n)), MUL).then_inc(S["p_ready"], 1)

            def stick_breaking():
                causal = T["causal"].unsqueeze(1).to_broadcast((P, 2, P))

                def masked(buf, last):
                    for h in range(2):
                        v = buf[:, h, :].rearrange("p (b n) -> p b n", b=3)[:, 0:3:2, :]
                        ins = V.tensor_tensor(v, v, causal, MUL)
                        if h:
                            last(ins)
                        else:
                            chain.give(ins)

                def z_of(g):
                    return ps[:, 2 * (g % 2):2 * (g % 2) + 2, 0:384]

                def negabs(g):
                    dve.wait_ge(S["z_ps"], g + 1)
                    if g >= 3:
                        dve.wait_ge(S["arg_ready"], g - 2)
                    LS = sbk["LS"][g % 3]
                    chain(V.tensor_scalar(LS, z_of(g), 0.0, 0.25, ALU.min, MUL))
                    V.scalar_tensor_tensor(sbk["E"][:, g % 2], z_of(g), -0.125, LS, MUL, ADD
                                           ).then_inc(S["negabs_ready"], 1)

                def stay(g):
                    E_, LS, ST = sbk["E"][:, g % 2], sbk["LS"][g % 3], sbk["ST"][:, g % 2]
                    dve.wait_ge(S["log_ready"], g + 1)
                    chain(V.scalar_tensor_tensor(LS, LS, 0.5, E_, MUL, SUB))
                    chain(V.scalar_tensor_tensor(ST, z_of(g), -0.125, LS, MUL, ADD))
                    masked(ST, lambda ins: ins.then_inc(S["stay_ready"], 1))

                def weights(g):
                    dve.wait_ge(S["a_exp"], g + 1)
                    masked(sbk["A"][:, g % 2], lambda ins: ins.then_inc(S["a_ready"], 1))

                negabs(0)
                negabs(1)
                stay(0)
                for g in range(8):
                    if g < 6:
                        negabs(g + 2)
                    if g < 7:
                        stay(g + 1)
                    dve.wait_ge(S["later_ps"], g + 1)
                    V.tensor_tensor(sbk["A"][:, g % 2], sbk["LS"][g % 3], ps[:, 6:8, 0:384], ADD
                                    ).then_inc(S["arg_ready"], 1)
                    if g:
                        weights(g - 1)
                weights(7)

            dve.wait_ge(S["csil_ready"], 1)
            dve.wait_ge(loads["consts"], 16)
            for v in range(2):
                src = csil[:, :, v:v + 1].to_broadcast((P, DC, 32))
                h = cvec[:, :, 64 * v:64 * v + 32]
                chain(V.tensor_copy(h, src))
                V.tensor_tensor(cvec[:, :, 64 * v + 32:64 * v + 64], src, h, SUB).then_inc(S["cvec_ready"], 1)
            for n in range(AHEAD):
                split_lo(n, 0)
            for ph in phases:
                s = ph.stage
                N = tokens(s)

                def mod_column(ch):
                    dve.wait_ge(S["modcol_ps"], ch + 1)
                    V.tensor_tensor(modcol[:, bass.ds(ch * 8, 8)].rearrange("p (c v) -> p c v", v=2),
                                    ps[:, 5, 0:8].rearrange("p (c v) -> p c v", v=2),
                                    bmod[:, bass.ds(ch * 4, 4)].rearrange("p (c o) -> p c o", o=1).to_broadcast((P, 4, 2)),
                                    ADD).then_inc(S["modcol_ready"], 1)

                if ph.kind == "mod":
                    def visit(kind, x, idx, n0, q, i):
                        split_lo(n0 + AHEAD, q)
                        if x % 4 == 3:
                            mod_column(x // 4 + i)
                    walk(dve, ph, visit)
                    coefficients(-1)
                    V.tensor_copy(mx[:, 0:1], csil[:, 0, 0:1]).then_inc(S["coef_ready"], 1)
                    for t in range(4):
                        split_x(t, True, True)
                elif ph.kind in ("ffn_in", "u"):
                    pending = []

                    def visit(kind, x, idx, n0, q, i):
                        split_lo(n0 + AHEAD, q)
                        if kind == "M":
                            if x % 4 == 3:
                                pending.append(x // 4 + i)
                            return
                        if kind == "U":
                            dve.wait_ge(S["gate_ready"], tiles_before[s] + idx + 1)
                            dve.wait_ge(unit_used, n0 + 1 + RING * q)
                            h = hidf[:, bass.ds(idx * TOK, N)]
                            V.tensor_tensor(h, h, ps[:, 2 + x % 2, 0:N], MUL).then_inc(S["hid_ready"], 1)
                        if pending:
                            mod_column(pending.pop())
                        if with_gate(ph, idx):
                            if (kind, idx) == ("G", FT - 2):
                                gate(s, 0)
                            if (kind, idx) == ("U", FT - 2):
                                gate(s, 1)
                    walk(dve, ph, visit)
                elif ph.kind in ("v", "proj"):
                    base = groups_before[ph.first]

                    def visit(kind, x, idx, n0, q, i):
                        split_lo(n0 + AHEAD, q)
                        if ph.more.get("vec", LAT) == LAT and STAGES[s] in EARLY and isinstance(idx, int):
                            if idx == LAST_TILE_UNIT:
                                split_x(TILES[s - 1] - 1, True, True)
                        if STAGES[s] == ATTN:
                            attention_queries(idx, base)
                        if STAGES[s] == HYB and isinstance(idx, int):
                            hybrid_positions(idx, base)
                        if ph.kind == "v" and x % 4 == 3:
                            g = x // 4
                            dve.wait_ge(S["proj_ready"], base + g + 1 + q)
                            for t in range(2):
                                V.bn_stats(bnst[:, 2 * t:2 * t + 2, :, :].rearrange("p a b c -> p (a b c)")[:, bass.ds((g + q) * 6, 6)],
                                           v_tok[:, t, bass.ds((idx - 3) * 128, 512)]).then_inc(S["vstat_ready"], 1)
                    walk(dve, ph, visit)
                    if ph.kind == "v":
                        vec = ph.more["vec"]
                        dve.wait_ge(S["vstat_ready"], 12 * (vec + 1))
                        for t in range(2):
                            st_ = bnst[:, 2 * t:2 * t + 2, :, :].rearrange("p a b c -> p (a b c)")[:, 0:36]
                            ins = V.bn_aggr(mv[:, t, :], st_.rearrange("p (a b) -> p a b", b=6))
                            if t:
                                ins.then_inc(S["var_ready"], 1)
                            else:
                                chain.give(ins)
                        invert_std(2)
                        for w in V_PARTS:
                            for t in range(2):
                                V.tensor_scalar(v_tok[:, t, w], v_tok[:, t, w], mv[:, t, 0:1], rstd[:, t:t + 1], SUB, MUL
                                                ).then_inc(S["v_normed"], 1)
                    if STAGES[s] == ATTN:
                        dve.wait_ge(S["proj_ready"], base + 3)
                        attention()
                    elif STAGES[s] == HYB:
                        dve.wait_ge(S["proj_ready"], base + 7)
                        hybrid()
                    elif STAGES[s] == SB:
                        dve.wait_ge(S["proj_ready"], base + 6)
                        stick_breaking()
                elif ph.kind == "out":
                    if s < N_MODULATED and STAGES[s] != FFN:
                        for v in range(2):
                            gate(s, v)
                    K = OUT_K[s]
                    src_ap = out_source(s)
                    src = (lambda k: hidf[:, bass.ds(k * TOK, N)]) if src_ap is None else (lambda k: src_ap[:, k, :])
                    for k in range(AHEAD):
                        hs_lo(s, src, k, k, hs_before[s] + k + 1)

                    def visit(kind, x, idx, n0, q, i):
                        split_lo(n0 + AHEAD, q)
                        hs_lo(s, src, idx + AHEAD, x + AHEAD, hs_before[s] + idx + AHEAD + 1)
                    walk(dve, ph, visit)
                elif ph.kind == "tail":
                    k = OUT_K[s] - 1
                    split_lo(ph.first + RING - 1, 0)
                    hs_lo(s, src, k, k, hs_before[s] + k + 1)
                    epilogue(s, ph.first + ph.units)
                if ph.kind in ("u", "v") and not (ph.kind == "v" and ph.more["vec"] == LAT):
                    vec = LAT if ph.kind == "u" else CTX
                    def affine(c):
                        dve.wait_ge(S["mix_scaled"], GT * vec + c + 1)
                        m = mixbuf[:, c % 2, :].rearrange("p (n q) -> p n q", n=2)
                        b = ps[:, 4 + c % 4, 256:384].unsqueeze(1).to_broadcast((P, 2, P))
                        V.tensor_tensor(m, m, b, ADD).then_inc(S["mix_step"], 1)

                    affine(0)
                    for c in range(GT):
                        if c < GT - 1:
                            affine(c + 1)
                        h = hid[:, c, 256 * vec:256 * vec + 256]
                        dve.wait_ge(S["mix_step"], GT * vec + c + 1)
                        if c == 0:
                            dve.wait_ge(S["gate_ready"], tiles_before[s] + GT)
                        V.tensor_tensor(h, h, mixbuf[:, c % 2, :], MUL).then_inc(S["mix_done"], 1)

        @block.tensor
        def _(pe):
            seen = Tally()
            mm = nc.tensor.matmul

            def passes(out, hi, lo, w_hi, w_lo, first, last, stationary_w):
                todo = [(hi, w_hi), (lo, w_hi), (hi, w_lo)] if stationary_w else [(hi, w_hi), (hi, w_lo), (lo, w_hi)]
                for k, (x, w) in enumerate(todo):
                    ins = mm(out, w if stationary_w else x, x if stationary_w else w,
                             start=first and k == 0, stop=last and k == 2)
                return ins

            def feature_unit(n0, bank, N):
                slot = n0 % RING
                for kt in range(DC):
                    w = slice(kt * P, kt * P + P)
                    ins = passes(ps[:, bank, 0:N], xhi[:, kt, 0:N], xlo[:, kt, 0:N], whi[:, slot, w], wlo[:, slot, w],
                                 kt == 0, kt == DC - 1, True)
                ins.then_inc(unit_used, 1)

            def token_unit(n0, quarter, tiles, banks):
                slot = n0 % RING
                for kk in range(2):
                    kt = 2 * quarter + kk
                    for t, bank in zip(tiles, banks):
                        r, w = slice(t * P, t * P + P), slice(512 * kk, 512 * kk + 512)
                        ins = passes(ps[:, bank, :], xhi[:, kt, r], xlo[:, kt, r], whi[:, slot, w], wlo[:, slot, w],
                                     kt == 0, kt == DC - 1, False)
                ins.then_inc(unit_used, 1)

            def mod_unit(n0, quarter):
                slot = n0 % RING
                for kk in range(2):
                    kt = 2 * quarter + kk
                    for w, part in ((whi, 0), (wlo, 1)):
                        ins = mm(ps[:, 4, :], cvec[:, kt, :], w[:, slot, 512 * kk:512 * kk + 512],
                                 start=kt == 0 and part == 0, stop=kt == DC - 1 and part == 1)
                ins.then_inc(unit_used, 1)

            def mod_column(ch):
                pe.wait_ge(S["modrow_ready"], ch + 1)
                if not isinstance(ch, int) or ch > 0:
                    pe.wait_ge(S["modcol_ready"], ch)
                for c in range(4):
                    ins = mm(ps[:, 5, 2 * c:2 * c + 2], modrow[:, c * P:c * P + P], sel, start=True, stop=True)
                ins.then_inc(S["modcol_ps"], 1)

            def out_products(s, n0, x, t, last, halves=(0, 1)):
                slot, h = n0 % RING, x % RING
                first = x == 0
                r = slice(t * P, t * P + P)
                hi, lo = hs[:, h, 0, r], hs[:, h, 1, r]
                for half in halves:
                    w = slice(512 * half, 512 * half + 512)
                    mm(ps[:, 2 * t + half, :], hi, whi[:, slot, w], start=first, stop=False)
                    mm(ps[:, 2 * t + half, :], hi, wlo[:, slot, w], start=False, stop=False)
                for half in halves:
                    w = slice(512 * half, 512 * half + 512)
                    ins = mm(ps[:, 2 * t + half, :], lo, whi[:, slot, w], start=False, stop=last)
                return ins

            def transposes(src, t, shared):
                for c in range(DC):
                    ins = nc.tensor.transpose(ps[:, 2 * t + c // 4, (c % 4) * P:(c % 4 + 1) * P],
                                              src[:, c * P:(c + 1) * P], ident)
                    if shared and c == DC // 2 - 1:
                        ins.then_inc(S["xT_half"], 1)
                ins.then_inc(S["xT_ps"], 1)

            def tile_source(s, t):
                return X[:, t, :] if s < 5 else normed[t]

            def last_transposes(s):
                pe.wait_ge(S["norm_ready"], seen("norm"))
                transposes(tile_source(s, TILES[s] - 1), TILES[s] - 1, True)

            def out_tail(s, first):
                k0, n = OUT_K[s] - RING, TILES[s]
                for t in range(n - 1):
                    for j in range(RING):
                        if t == 0:
                            unit_wait(first + j, 0)
                            pe.wait_ge(S["hs_lo"], hs_before[s] + k0 + j + 1)
                        ins = out_products(s, first + j, k0 + j, t, j == RING - 1)
                    ins.then_inc(S["y_ready"], 1)
                    if t and s < 11:
                        pe.wait_ge(S["norm_ready"], seen("norm"))
                        transposes(tile_source(s, t - 1), t - 1, False)
                for half in range(2):
                    for j in range(RING):
                        ins = out_products(s, first + j, k0 + j, n - 1, j == RING - 1, (half,))
                        if half:
                            ins.then_inc(unit_used, 1)
                    if half == 0:
                        ins.then_inc(S["y_ready"], 1)
                if s < 11:
                    pe.wait_ge(S["norm_ready"], seen("norm"))
                    transposes(tile_source(s, n - 2), n - 2, False)
                    if STAGES[s + 1] not in EARLY:
                        last_transposes(s)

            def gate(s, v):
                if v < GATES[s]:
                    pe.wait_ge(S["diag_ready"], seen("diag"))
                    for h in range(2):
                        ins = mm(ps[:, GATE_BANKS[v] + h, :], ones, diag[:, 512 * h:512 * h + 512], start=True, stop=True)
                    ins.then_inc(S["gate_ps"], 1)

            def mix(vec):
                if vec == LAT:
                    pe.wait_ge(S["rs_ready"], 4)
                for c in range(GT):
                    g, bank = c // 3, 4 + c % 4
                    i = GT * vec + c
                    for k, w in enumerate(V_PARTS):
                        if c * P == w.start:
                            pe.wait_ge(S["v_normed"], 2 * len(V_PARTS) * vec + 2 * (k + 1))
                    if c >= 4:
                        pe.wait_ge(S["mix_done"], i - 3)
                    for n in range(2):
                        mm(ps[:, bank, n * P:(n + 1) * P], v_tok[:, n, c * P:(c + 1) * P], wsT[:, g * P:(g + 1) * P],
                           start=True, stop=True)
                    r = 32 * (c // 6)
                    mm(ps[:, bank, 256:384], lnb_row[r:r + 2, (c % 6) * P:(c % 6 + 1) * P],
                       sum_row[r:r + 2, (g % 2) * P:(g % 2 + 1) * P], start=True, stop=True).then_inc(S["mix_ps"], 1)

            def attention():
                pe.wait_ge(S["qk_ready"], 1)
                for h in range(8):
                    for t in range(2):
                        ins = nc.tensor.transpose(ps[:, h // 2, (h % 2) * 256 + t * P:(h % 2) * 256 + (t + 1) * P],
                                                  att["q"][:, t, h * P:(h + 1) * P], ident)
                ins.then_inc(S["qkT_ps"], 1)
                pe.wait_ge(S["qk_ready"], 2)
                pe.wait_ge(S["value_ready"], 1)
                for g in range(2):
                    for t in range(4):
                        ins = nc.tensor.transpose(ps[:, 4 + g, t * P:(t + 1) * P], att["k"][:, t, g * P:(g + 1) * P], ident)
                ins.then_inc(S["qkT_ps"], 1)
                pe.wait_ge(S["qkT_ready"], 2)

                def scores(i):
                    h, t = divmod(i, 2)
                    if i >= 4:
                        pe.wait_ge(S["exp_ready"], i - 3)
                    mm(ps[:, SCORE_BANKS[i % 4], :], att["qT"][:, h, t * P:(t + 1) * P], att["kT"][:, h // 4, :],
                       start=True, stop=True).then_inc(S["s_ps"], 1)

                for i in range(3):
                    scores(i)
                for i in range(16):
                    h, t = divmod(i, 2)
                    if i < 13:
                        scores(i + 3)
                    pe.wait_ge(S["p_ready"], i + 1)
                    if i >= 2:
                        pe.wait_ge(S["pT_ready"], i - 1)
                    for k in range(4):
                        ins = nc.tensor.transpose(ps[:, 2 + i % 2, k * P:(k + 1) * P], att["P"][:, i % 4, k * P:(k + 1) * P], ident)
                    ins.then_inc(S["pT_ps"], 1)
                    if t == 1:
                        pe.wait_ge(S["pT_ready"], i + 1)
                        if h >= 2:
                            pe.wait_ge(S["o_ready"], h - 1)
                        v = slice((h // 4) * P, (h // 4 + 1) * P)
                        for k in range(4):
                            ins = mm(ps[:, 4 + h % 2, 0:256], att["v"][:, k, v], att["PT"][:, h % 2, k, :],
                                     start=k == 0, stop=k == 3)
                        ins.then_inc(S["o_ps"], 1)
                pe.wait_ge(S["o_ready"], o_made[ATTN])

            def qk_transposes(pr, columns, ready):
                for k, at in enumerate(columns):
                    if k % 8 == 0:
                        pe.wait_ge(*ready[k // 8])
                    bank = (4 + k // 2) % 8
                    for t in range(2):
                        ins = nc.tensor.transpose(ps[:, bank, (k % 2) * 256 + t * P:(k % 2) * 256 + (t + 1) * P],
                                                  pr[:, t, at:at + P], ident)
                    if k % 8 == 7:
                        ins.then_inc(S["qkT_ps"], 1)

            def key_major(bank, qT, kT, head):
                r = slice(64 * (head % 2), 64 * (head % 2) + 64)
                c = head // 2
                mm(ps[:, bank, 0:256], kT[r, c, 0:P], qT[r, c, 0:256], start=True, stop=True)
                return mm(ps[:, bank, 256:384], kT[r, c, P:256], qT[r, c, P:256], start=True, stop=True)

            def hybrid(base):
                pr = proj_dst(7)
                pe.wait_ge(S["qk_ready"], 4)
                qk_transposes(pr, [P * k for k in range(8)] + [2048 + P * k for k in range(8)],
                              [(S["qk_ready"], 3), (S["proj_ready"], base + 7)])
                pe.wait_ge(S["qkT_ready"], 4)
                rq, rk, dq, dk = (hyb["qkT"][:, 4 * k:4 * k + 4, :] for k in range(4))

                def ret_scores(h):
                    if h >= 2:
                        pe.wait_ge(S["ret_s_ready"], h - 1)
                    key_major(h % 2, rq, rk, h).then_inc(S["ret_s_ps"], 1)

                ret_scores(0)
                for h in range(8):
                    if h < 7:
                        ret_scores(h + 1)
                    pe.wait_ge(S["ret_s_ready"], h + 1)
                    St = hyb["St"][:, h % 2, :]
                    c = slice(64 * h, 64 * h + 64)
                    v = slice(1024 + 64 * h, 1024 + 64 * h + 64)
                    mm(ps[:, 6, c], St[:, 0:P], pr[:, 0, v], start=True, stop=True)
                    mm(ps[:, 7, c], St[:, P:256], pr[:, 0, v], start=True, stop=False)
                    mm(ps[:, 7, c], St[:, 256:384], pr[:, 1, v], start=False, stop=True).then_inc(S["ret_o_ps"], 1)

                def scores(j):
                    g, t = divmod(j, 2)
                    n = P * (t + 1)
                    if j >= 2:
                        pe.wait_ge(S["max_ready"], 16 + j - 1)
                    for h in range(2):
                        r = slice(64 * h, 64 * h + 64)
                        ins = mm(ps[:, 2 * (j % 2) + h, 0:n], dq[r, g, t * P:(t + 1) * P], dk[r, g, 0:n],
                                 start=True, stop=True)
                    ins.then_inc(S["s_ps"], 1)

                scores(0)
                scores(1)
                for j in range(2 * DIL_PAIRS):
                    g, t = divmod(j, 2)
                    if j < 2 * DIL_PAIRS - 2:
                        scores(j + 2)
                    if j == 2 * DIL_PAIRS - 1:
                        pe.wait_ge(S["ret_ready"], 2)
                        pe.wait_ge(S["max_ready"], 16 + j)
                        for k in range(4):
                            for tile in range(2):
                                at = (k % 2) * 256 + tile * P
                                ins = nc.tensor.transpose(ps[:, k // 2, at:at + P], hyb["ret"][:, tile, k * P:(k + 1) * P], ident)
                        ins.then_inc(S["retT_ps"], 1)
                    pe.wait_ge(S["p_ready"], 16 + j + 1)
                    if j >= 2:
                        pe.wait_ge(S["pT_ready"], 16 + j - 1)
                    for k in range(2 * (t + 1)):
                        ins = nc.tensor.transpose(ps[:, 4 + j % 2, k * P:(k + 1) * P], hyb["P"][j % 3][:, k * P:(k + 1) * P], ident)
                    ins.then_inc(S["pT_ps"], 1)
                    if t == 1:
                        pe.wait_ge(S["pT_ready"], 16 + j + 1)
                        if g >= 2:
                            pe.wait_ge(S["o_ready"], o_made[ATTN] + g - 1)
                        for h in range(2):
                            r = slice(64 * h, 64 * h + 64)
                            v = slice(3072 + 64 * (2 * g + h), 3072 + 64 * (2 * g + h) + 64)
                            mm(ps[r, 6 + g % 2, 0:256], pr[:, 0, v], hyb["PT"][:, g % 2, 2 * h, :], start=True, stop=False)
                            ins = mm(ps[r, 6 + g % 2, P:256], pr[:, 1, v], hyb["PT"][:, g % 2, 2 * h + 1, P:256],
                                     start=False, stop=True)
                        ins.then_inc(S["o_ps"], 1)
                pe.wait_ge(S["o_ready"], o_made[HYB])

            def stick_breaking(base):
                pr = proj_dst(10)
                qk_transposes(pr, [P * k for k in range(16)], [(S["proj_ready"], base + 4), (S["proj_ready"], base + 6)])
                pe.wait_ge(S["qkT_ready"], 6)
                qT, kT = sbk["qkT"][:, 0:8, :], sbk["qkT"][:, 8:16, :]
                tri = T["tri"]

                def scores(g):
                    if g >= 2:
                        pe.wait_ge(S["stay_ready"], g - 1)
                    for h in range(2):
                        ins = key_major(2 * (g % 2) + h, qT, kT, 2 * g + h)
                    ins.then_inc(S["z_ps"], 1)

                def output(g):
                    A_ = sbk["A"][:, g % 2]
                    pe.wait_ge(S["a_ready"], g + 1)
                    if g >= 2:
                        pe.wait_ge(S["o_ready"], o_made[HYB] + g - 1)
                    for h in range(2):
                        r = slice(64 * h, 64 * h + 64)
                        v = slice(2048 + 64 * (2 * g + h), 2048 + 64 * (2 * g + h) + 64)
                        mm(ps[r, 4 + g % 2, 0:256], pr[:, 0, v], A_[:, h, 0:256], start=True, stop=False)
                        ins = mm(ps[r, 4 + g % 2, P:256], pr[:, 1, v], A_[:, h, 256:384], start=False, stop=True)
                    ins.then_inc(S["o_ps"], 1)

                scores(0)
                scores(1)
                for g in range(8):
                    pe.wait_ge(S["stay_ready"], g + 1)
                    if g < 6:
                        scores(g + 2)
                    ST = sbk["ST"][:, g % 2]
                    if g:
                        pe.wait_ge(S["arg_ready"], g)
                    for h in range(2):
                        mm(ps[:, 6 + h, 0:256], tri, ST[:, h, 0:256], start=True, stop=False)
                        mm(ps[:, 6 + h, P:256], ones, ST[:, h, 256:384], start=False, stop=True)
                        ins = mm(ps[:, 6 + h, 256:384], tri, ST[:, h, 256:384], start=True, stop=True)
                    ins.then_inc(S["later_ps"], 1)
                    if g:
                        output(g - 1)
                output(7)
                pe.wait_ge(S["o_ready"], o_made[SB])

            def unit_wait(n0, q):
                pe.wait_ge(lo_ready, n0 + 1 + RING * q)

            pe.wait_ge(S["cvec_ready"], 2)
            pe.wait_ge(loads["consts"], 16)
            for ph in phases:
                s = ph.stage
                N = tokens(s)

                def before_chunk(ch, x):
                    if not isinstance(ch, int) or ch > 0:
                        pe.wait_ge(S["modrow_ready"], ch)

                if ph.kind == "mod":
                    def visit(kind, x, idx, n0, q, i):
                        ch = x // 4 + i
                        unit_wait(n0, q)
                        if x % 4 == 0:
                            before_chunk(ch, x)
                        mod_unit(n0, x % 4)
                        if x % 4 == 3:
                            mod_column(ch)
                    walk(pe, ph, visit)
                    pe.wait_ge(loads["x"], 32)
                    pe.wait_ge(S["coef_ready"], 1)
                    for t in range(4):
                        transposes(X[:, t, :], t, True)
                elif ph.kind in ("ffn_in", "u"):
                    pending = []
                    base = tiles_before[s]
                    pe.wait_ge(S["x_ready"], tiles_ready(s))

                    def visit(kind, x, idx, n0, q, i):
                        unit_wait(n0, q)
                        if kind == "M":
                            ch = x // 4 + i
                            if x % 4 == 0:
                                before_chunk(ch, x)
                            mod_unit(n0, x % 4)
                            if x % 4 == 3:
                                pending.append(ch)
                            return
                        if kind in "GF":
                            if not isinstance(q, int) or base + idx > 1:
                                pe.wait_ge(S["gate_ready"], base + idx - 1)
                            feature_unit(n0, x % 2, N)
                        else:
                            hb = hid_before[s]
                            if not isinstance(q, int) or hb + idx > 1:
                                pe.wait_ge(S["hid_ready"], hb + idx - 1)
                            feature_unit(n0, 2 + x % 2, N)
                        if pending:
                            mod_column(pending.pop())
                        if with_gate(ph, idx):
                            if (kind, idx) == ("U", FT - 2):
                                if s in mods_by:
                                    pe.wait_ge(S["modcol_ready"], mods_by[s])
                                gate(s, 0)
                            if (kind, idx) == ("G", FT - 1):
                                gate(s, 1)
                    walk(pe, ph, visit)
                    if ph.kind == "u":
                        pe.wait_ge(S["modcol_ready"], mods_by[s])
                    if ph.kind == "u":
                        mix(LAT)
                elif ph.kind in ("v", "proj"):
                    base = groups_before[ph.first]
                    early = STAGES[s] in EARLY and ph.more.get("vec", LAT) == LAT
                    pe.wait_ge(S["x_ready"], tiles_ready(s) - (2 if early else 0))

                    def visit(kind, x, idx, n0, q, i):
                        g = x // 4
                        unit_wait(n0, q)
                        if STAGES[s] == ATTN:
                            tiles, banks = [([0, 1], [0, 1]), ([0, 1], [2, 3]), (range(4), range(4, 8))][g]
                        else:
                            t0 = 2 * ph.more.get("vec", 0)
                            tiles, banks = [t0, t0 + 1], [2 * (g % 2), 2 * (g % 2) + 1]
                            if x % 4 == 0 and (not isinstance(q, int) or base + g > 1):
                                pe.wait_ge(S["proj_ready"], base + g - 1 + q)
                        if STAGES[s] == ATTN and idx == 8:
                            pe.wait_ge(S["x_ready"], tiles_ready(s))
                        token_unit(n0, x % 4, tiles, banks)
                        if early and isinstance(idx, int) and idx == LAST_TILE_UNIT:
                            last_transposes(s - 1)
                    walk(pe, ph, visit)
                    if ph.kind == "v" and ph.more["vec"] == LAT:
                        pe.wait_ge(S["x_ready"], tiles_ready(s))
                        pe.wait_ge(loads["gmlp"], 16 * 9)
                        for i in range(4):
                            ins = mm(ps[32 * i:32 * i + 1, 7, 0:256], ones[:, 0:1], wsT[:, 256 * i:256 * i + 256],
                                     start=True, stop=True)
                        ins.then_inc(S["rs_ps"], 1)
                    if ph.kind == "v" and ph.more["vec"] == CTX:
                        mix(CTX)
                    if STAGES[s] == ATTN:
                        attention()
                    elif STAGES[s] == HYB:
                        hybrid(base)
                    elif STAGES[s] == SB:
                        stick_breaking(base)
                elif ph.kind == "out":
                    if STAGES[s] == FFN:
                        pe.wait_ge(S["hid_ready"], hid_before[s] + FT)
                    elif STAGES[s] == GMLP:
                        pe.wait_ge(S["mix_done"], 2 * GT)
                    if s < N_MODULATED:
                        if STAGES[s] != FFN:
                            for v in range(2):
                                gate(s, v)
                        pe.wait_ge(S["gate_row_ready"], seen("gate_row", GATES[s]))

                    def visit(kind, x, idx, n0, q, i):
                        unit_wait(n0, q)
                        pe.wait_ge(S["hs_lo"], hs_before[s] + idx + 1)
                        for t in range(TILES[s]):
                            ins = out_products(s, n0, x, t, False)
                        ins.then_inc(unit_used, 1)
                    walk(pe, ph, visit)
                elif ph.kind == "tail":
                    out_tail(s, ph.first)


def constants():
    import numpy as np

    f4 = np.float32
    consts = np.zeros((P, 264), f4)
    consts[:, 0:P] = np.eye(P)
    consts[:, P:2 * P] = 1.0
    consts[[0, 32], 2 * P] = 1.0
    consts[[64, 96], 2 * P + 1] = 1.0
    consts[:, 260], consts[:, 261] = RMS_EPS, LN_EPS
    pos = np.arange(256)

    def rope(angle):
        both = np.stack([np.cos(angle), np.sin(angle)]).astype(f4)
        return both.reshape(2, 2, P, -1).transpose(2, 0, 1, 3).reshape(P, -1)

    quarter = 32
    freqs = (f4(10000.0) ** (-np.arange(quarter, dtype=f4) / f4(quarter))).astype(f4)
    grid = np.concatenate([(pos // 64).astype(f4)[:, None] * freqs, (pos % 64).astype(f4)[:, None] * freqs], 1)

    def plain(half, theta):
        inv = (f4(1.0) / (f4(theta) ** (np.arange(half, dtype=f4) / f4(half)))).astype(f4)
        return pos.astype(f4)[:, None] * inv[None, :]

    i, j = np.arange(P)[:, None], np.arange(256)[None, :]
    dist = i + P - j
    count = ((dist >= 0) & (dist <= 128)).astype(f4)
    count += (dist >= 0) & (dist % 4 == 0)
    count += (dist >= 0) & (dist % 16 == 0)
    bias = np.where(count > 0, 8.0 * np.log(np.maximum(count, 1.0)), -1e30).astype(f4)
    key, query = np.arange(P)[:, None], np.arange(P)[None, :]
    causal = (key < query).astype(f4)
    tri = (key > query).astype(f4)
    tables = np.concatenate([rope(plain(32, 10000.0)), rope(plain(8, 500000.0)), bias, causal, tri], 1)
    lag = np.arange(256)[None, :] - np.arange(P)[:, None]
    log_g = np.log(1.0 - 2.0 ** (-5.0 - np.arange(8)))
    decay = np.where(lag >= 0, np.exp(np.maximum(lag, 0)[None] * log_g[:, None, None]), 0.0) * 0.125
    return dict(consts=consts, att_rope=rope(grid), tables=tables.astype(f4),
                decay=np.ascontiguousarray(decay.transpose(1, 0, 2)).astype(f4))


def kernel(**inputs):
    import numpy as np
    import concourse.bacc as bacc
    from concourse.bass_utils import run_bass_kernel_spmd

    g = {k: np.asarray(v) for k, v in inputs.items()}

    def feature_units(w, n):
        return w.reshape(DC, P, n, P).transpose(2, 1, 0, 3).reshape(n, P, UNIT)

    def token_units(w):
        n = w.shape[1] // 512
        return w.reshape(4, 2, P, n, 512).transpose(3, 0, 2, 1, 4).reshape(4 * n, P, UNIT)

    def out_units(w):
        return w.reshape(-1, P, UNIT)

    def column(v):
        return v.reshape(-1, P).T

    ffns = [(g["ffn_w_in"][l, i], g["ffn_w_out"][l, i]) for l in range(2) for i in range(2)]
    ffns += [(g[f"ffn{i}_w_in_2"][l], g[f"ffn{i}_w_out_2"][l]) for l in range(2) for i in (1, 2)]
    arrays = constants()
    for i, (w_in, w_out) in enumerate(ffns):
        arrays[f"ffn_gate{i}"] = feature_units(w_in[:, :FF], FT)
        arrays[f"ffn_up{i}"] = feature_units(w_in[:, FF:], FT)
        arrays[f"ffn_out{i}"] = out_units(w_out)
    arrays.update(
        w_mod=np.concatenate([token_units(w) for w in g["w_mod"]]),
        gmlp_u=feature_units(g["gmlp_w_in"][0][:, :3 * D], GT),
        gmlp_v=token_units(g["gmlp_w_in"][0][:, 3 * D:]),
        gmlp_out=out_units(g["gmlp_w_out"][0]),
        attn_in=token_units(g["attn_w_qkv"][0]), attn_out=out_units(g["attn_w_o"][0]),
        hyb_in=token_units(g["hyb_w_in_2"][0]), hyb_out=out_units(g["hyb_w_out_2"][0]),
        sb_in=token_units(g["sb_w_in_2"][0]), sb_out=out_units(g["sb_w_out_2"][0]),
        x=g["x"][0].reshape(2, P, D).transpose(1, 0, 2), ctx=g["ctx"][0].reshape(2, P, D).transpose(1, 0, 2),
        wsT=g["gmlp_w_s"][0].transpose(2, 0, 1).reshape(P, GROUPS * P),
        gmlp_ln_b=g["gmlp_ln_b"].reshape(4, 768), gmlp_b_s=g["gmlp_b_s"].reshape(4, 256),
        q_norm=g["attn_q_norm"].reshape(1, P), k_norm=g["attn_k_norm"].reshape(1, P),
        ln_g=g["ln_g"].reshape(6, D), ln_b=g["ln_b"].reshape(6, D),
        ret_gn=g["ret_gn_2"].reshape(1, 512),
        norm_rows=np.stack([g[n][l] for l in range(2) for n in ("ffn1_norm_2", "mix_norm_2", "ffn2_norm_2")]
                           + [g["final_norm_2"]]),
        cols=np.concatenate([
            np.stack([column(g["c"]), column(g["c_ctx"])], -1).reshape(P, 2 * DC),
            column(g["b_mod"]), column(g["ln_g"]), column(g["ln_b"]), column(g["gmlp_ln_g"])], 1),
    )
    nc = bacc.Bacc("TRN2", target_bir_lowering=False, num_devices=1)
    feed, aps = {}, {}
    for name, v in arrays.items():
        feed["in_" + name] = np.ascontiguousarray(v)
        aps[name] = nc.dram_tensor("in_" + name, v.shape, mybir.dt.from_np(v.dtype), kind="ExternalInput").ap()
    for part in ("gate", "up", "out"):
        aps["ffn_" + part] = [aps[f"ffn_{part}{i}"] for i in range(len(ffns))]
    result = nc.dram_tensor("out_dram", (2, P, D), mybir.dt.float32, kind="ExternalOutput").ap()
    aps["out"] = result.rearrange("t p n -> p t n")
    fused_blocks(nc, aps)
    r = run_bass_kernel_spmd(nc, [feed], core_ids=[0])
    return r.results[0]["out_dram"].reshape(1, 256, D)
```
